# Optimizing a Trainium2 kernel written in Bass

```python
import math
import jax, jax.numpy as jnp
from jax import lax
import numpy as np

D_MODEL = 1024
BATCH = 1
SEQ = 1024
DEPTH = 1

ROPE_THETA = 500000.0
NORM_EPS = 1e-6
NEG_INF = -1e30
BLK = 128

A_HEADS = 8
HEAD_DIM = 64
A_ROT_DIM = HEAD_DIM // 4
DIL_PATTERNS = ((128, 1), (512, 4), (2048, 16))
A_WIDTH = A_HEADS * HEAD_DIM

B_HEADS = 8
MLA_Q_RANK = 256
MLA_KV_RANK = 128
MLA_NOPE = 64
MLA_ROPE = 32
MLA_V = 64
B_WIDTH = B_HEADS * MLA_V

MIX_WIDTH = A_WIDTH + B_WIDTH
IN_SPLITS = (A_WIDTH, A_WIDTH, A_WIDTH, MLA_Q_RANK, MLA_KV_RANK, MLA_ROPE)
IN_WIDTH = sum(IN_SPLITS)

PEER_HEADS = 8
PEER_NKEYS = 128
PEER_EXPERTS = PEER_NKEYS * PEER_NKEYS
PEER_QDIM = 256
PEER_TOPK = 16
PEER_CHUNK = 128

kernel_name = "hybrid_dilated_mla_peer_layer"

def rmsnorm(x, g):
    xf = x.astype(jnp.float32)
    y = xf * lax.rsqrt(jnp.mean(xf * xf, axis=-1, keepdims=True) + NORM_EPS)
    return (y * g.astype(jnp.float32)).astype(x.dtype)

def rope(x, pos, rot_dim):
    half = rot_dim // 2
    inv = ROPE_THETA ** (-jnp.arange(half, dtype=jnp.float32) / half)
    ang = pos.astype(jnp.float32)[..., None] * inv
    cos = jnp.cos(ang)[:, :, None, :]
    sin = jnp.sin(ang)[:, :, None, :]
    xr = x[..., :rot_dim].astype(jnp.float32)
    x1, x2 = xr[..., :half], xr[..., half:]
    rot = jnp.concatenate([x1 * cos - x2 * sin, x2 * cos + x1 * sin], axis=-1).astype(x.dtype)
    return jnp.concatenate([rot, x[..., rot_dim:]], axis=-1)

def dilated_window_attention(q, k, v, window, dilation):
    b, s, h, e = q.shape
    span = window // dilation
    L = s // dilation
    nb = -(-L // BLK)
    Lp = nb * BLK

    def to_sub(t):
        t = t.reshape(b, L, dilation, h, e).transpose(0, 2, 1, 3, 4)
        return jnp.pad(t, ((0, 0), (0, 0), (0, Lp - L), (0, 0), (0, 0)))

    def band(t):
        t = jnp.pad(t, ((0, 0), (0, 0), (BLK, 0), (0, 0), (0, 0))).reshape(b, dilation, nb + 1, BLK, h, e)
        return jnp.concatenate([t[:, :, :-1], t[:, :, 1:]], axis=3)

    qb = to_sub(q).reshape(b, dilation, nb, BLK, h, e)
    kb = band(to_sub(k))
    vb = band(to_sub(v))
    scores = jnp.einsum('bdnqhe,bdnkhe->bdnhqk', qb, kb).astype(jnp.float32) * (e ** -0.5)
    qi = jnp.arange(BLK)[:, None]
    kj = jnp.arange(2 * BLK)[None, :]
    dist = qi + BLK - kj
    kpos = (jnp.arange(nb)[:, None, None] - 1) * BLK + kj[None]
    valid = (dist >= 0)[None] & (dist <= span)[None] & (kpos >= 0)
    scores = jnp.where(valid[None, None, :, None], scores, NEG_INF)
    m = jnp.max(scores, axis=-1, keepdims=True)
    p = jnp.exp(scores - m)
    den = jnp.sum(p, axis=-1)
    o = jnp.einsum('bdnhqk,bdnkhe->bdnqhe', p, vb.astype(jnp.float32))
    o = o / den.transpose(0, 1, 2, 4, 3)[..., None]
    lse = (m[..., 0] + jnp.log(den)).transpose(0, 1, 2, 4, 3)
    o = o.reshape(b, dilation, Lp, h, e)[:, :, :L].transpose(0, 2, 1, 3, 4).reshape(b, s, h, e)
    lse = lse.reshape(b, dilation, Lp, h)[:, :, :L].transpose(0, 2, 1, 3).reshape(b, s, h)
    return o, lse

def causal_attention_blocked(q, k, v):
    b, s, h, e = q.shape
    ev = v.shape[-1]
    nb = s // BLK
    scale = e ** -0.5
    qb = q.reshape(b, nb, BLK, h, e).transpose(1, 0, 2, 3, 4)
    kpos = jnp.arange(s)
    vf = v.astype(jnp.float32)

    def one_block(args):
        qblk, i = args
        sc = jnp.einsum('bqhe,bkhe->bhqk', qblk, k).astype(jnp.float32) * scale
        qpos = i * BLK + jnp.arange(BLK)
        sc = jnp.where(kpos[None, :] <= qpos[:, None], sc, NEG_INF)
        p = jax.nn.softmax(sc, axis=-1)
        return jnp.einsum('bhqk,bkhe->bqhe', p, vf)

    o = lax.map(one_block, (qb, jnp.arange(nb)))
    return o.transpose(1, 0, 2, 3, 4).reshape(b, s, h, ev)

def peer(hn, w_pq, sub_keys, u_emb, v_emb):
    b, s, d = hn.shape
    t = hn.reshape(b * s, d)
    q = (t @ w_pq).reshape(-1, PEER_HEADS, 2, PEER_QDIM // 2).astype(jnp.float32)
    sc = jnp.einsum('thpc,hpnc->thpn', q, sub_keys.astype(jnp.float32))
    vals, idx = lax.top_k(sc, PEER_TOPK)
    cand = vals[:, :, 0, :, None] + vals[:, :, 1, None, :]
    best, flat = lax.top_k(cand.reshape(cand.shape[0], PEER_HEADS, PEER_TOPK * PEER_TOPK), PEER_TOPK)
    i1 = jnp.take_along_axis(idx[:, :, 0], flat // PEER_TOPK, axis=-1)
    i2 = jnp.take_along_axis(idx[:, :, 1], flat % PEER_TOPK, axis=-1)
    expert = i1 * PEER_NKEYS + i2
    gate = jax.nn.softmax(best, axis=-1)
    nc = t.shape[0] // PEER_CHUNK

    def one_chunk(args):
        tc, ec, gc = args
        u_sel = u_emb[ec]
        act = jax.nn.gelu(jnp.einsum('td,thkd->thk', tc, u_sel).astype(jnp.float32), approximate=False)
        return jnp.einsum('thk,thkd->td', (act * gc).astype(tc.dtype), v_emb[ec])

    out = lax.map(one_chunk, (t.reshape(nc, PEER_CHUNK, d),
                              expert.reshape(nc, PEER_CHUNK, PEER_HEADS, PEER_TOPK),
                              gate.reshape(nc, PEER_CHUNK, PEER_HEADS, PEER_TOPK)))
    return out.reshape(b, s, d)

def setup_inputs(seed: int = 0) -> dict:
    key = jax.random.key(seed)
    ks = jax.random.split(key, 17)
    nrm = lambda k, shape, scale: jax.random.normal(k, shape, jnp.float32) * scale
    gain = lambda k, shape: 1.0 + 0.02 * jax.random.normal(k, shape, jnp.float32)
    x = jax.random.normal(ks[0], (BATCH, SEQ, D_MODEL), jnp.float32)
    offset = jax.random.randint(ks[1], (BATCH, 1), 0, 1024, dtype=jnp.int32)
    positions = (jnp.arange(SEQ, dtype=jnp.int32)[None, :] + offset).astype(jnp.int32)
    return {
        "x": x,
        "positions": positions,
        "g_mix": gain(ks[2], (DEPTH, D_MODEL)),
        "w_in": nrm(ks[3], (DEPTH, D_MODEL, IN_WIDTH), D_MODEL ** -0.5),
        "g_cq": gain(ks[4], (DEPTH, MLA_Q_RANK)),
        "w_uq": nrm(ks[5], (DEPTH, MLA_Q_RANK, B_HEADS * (MLA_NOPE + MLA_ROPE)), MLA_Q_RANK ** -0.5),
        "g_ckv": gain(ks[6], (DEPTH, MLA_KV_RANK)),
        "w_ukv": nrm(ks[7], (DEPTH, MLA_KV_RANK, B_HEADS * (MLA_NOPE + MLA_V)), MLA_KV_RANK ** -0.5),
        "w_out": nrm(ks[8], (DEPTH, MIX_WIDTH, D_MODEL), MIX_WIDTH ** -0.5),
        "g_ffn": gain(ks[9], (DEPTH, D_MODEL)),
        "w_pq": nrm(ks[10], (DEPTH, D_MODEL, PEER_HEADS * PEER_QDIM), D_MODEL ** -0.5),
        "sub_keys": nrm(ks[11], (DEPTH, PEER_HEADS, 2, PEER_NKEYS, PEER_QDIM // 2), (PEER_QDIM // 2) ** -0.5),
        "u_emb": nrm(ks[12], (DEPTH, PEER_EXPERTS, D_MODEL), D_MODEL ** -0.5),
        "v_emb": nrm(ks[13], (DEPTH, PEER_EXPERTS, D_MODEL), PEER_HEADS ** -0.5),
        "g_final": gain(ks[14], (D_MODEL,)),
    }

def reference(x, positions, g_mix, w_in, g_cq, w_uq, g_ckv, w_ukv, w_out, g_ffn,
              w_pq, sub_keys, u_emb, v_emb, g_final):
    b, s, _ = x.shape
    offs = np.cumsum(IN_SPLITS)[:-1].tolist()
    h = x
    for l in range(DEPTH):
        hn = rmsnorm(h, g_mix[l])
        proj = hn @ w_in[l]
        qa, ka, va, cq, ckv, kr = jnp.split(proj, offs, axis=-1)

        qa = rope(qa.reshape(b, s, A_HEADS, HEAD_DIM), positions, A_ROT_DIM)
        ka = rope(ka.reshape(b, s, A_HEADS, HEAD_DIM), positions, A_ROT_DIM)
        va = va.reshape(b, s, A_HEADS, HEAD_DIM)
        outs, lses = [], []
        for window, dilation in DIL_PATTERNS:
            o_i, lse_i = dilated_window_attention(qa, ka, va, window, dilation)
            outs.append(o_i)
            lses.append(lse_i)
        wts = jax.nn.softmax(jnp.stack(lses, axis=0), axis=0)
        o_a = jnp.einsum('pbsh,pbshe->bshe', wts, jnp.stack(outs, axis=0)).astype(h.dtype)

        qm = (rmsnorm(cq, g_cq[l]) @ w_uq[l]).reshape(b, s, B_HEADS, MLA_NOPE + MLA_ROPE)
        q_m = jnp.concatenate([qm[..., :MLA_NOPE], rope(qm[..., MLA_NOPE:], positions, MLA_ROPE)], axis=-1)
        kv = (rmsnorm(ckv, g_ckv[l]) @ w_ukv[l]).reshape(b, s, B_HEADS, MLA_NOPE + MLA_V)
        k_rope = rope(kr[:, :, None, :], positions, MLA_ROPE)
        k_m = jnp.concatenate([kv[..., :MLA_NOPE],
                               jnp.broadcast_to(k_rope, (b, s, B_HEADS, MLA_ROPE))], axis=-1)
        o_m = causal_attention_blocked(q_m, k_m, kv[..., MLA_NOPE:]).astype(h.dtype)

        mixed = jnp.concatenate([o_a.reshape(b, s, A_WIDTH), o_m.reshape(b, s, B_WIDTH)], axis=-1)
        h = h + mixed @ w_out[l]

        h = h + peer(rmsnorm(h, g_ffn[l]), w_pq[l], sub_keys[l], u_emb[l], v_emb[l])
    return rmsnorm(h, g_final)


_drawn_inputs = setup_inputs


def setup_inputs(seed=0):
    import zlib

    import numpy as np

    out = dict(_drawn_inputs(seed))
    spreads = {}
    factors = {'g_mix': 4.135, 'g_cq': 7.603, 'g_ckv': 4.954, 'g_final': 8.261, 'g_ffn': 8.0}
    for name, (base, spread) in spreads.items():
        noise = np.random.default_rng([zlib.crc32(name.encode()), seed]).standard_normal(out[name].shape)
        drawn = base * np.exp(spread * noise) if base else spread * noise
        out[name] = __import__('jax').numpy.asarray(drawn.astype(out[name].dtype))
    for name, factor in factors.items():
        out[name] = (out[name] * factor).astype(out[name].dtype)
    return out
```

```python
from contextlib import ExitStack, contextmanager

import concourse.bass as bass
from concourse import mybir

P = 128
SEQ = 1024
D = 1024
NT = SEQ // P
KD = D // P
BANK = 512

HA, EA, ROT_A = 8, 64, 16
HM, NOPE, ROPE, VM = 8, 64, 32, 64
EM = NOPE + ROPE
QR, KR = 256, 128
WA = HA * EA
IN_W = 3 * WA + QR + KR + ROPE
UQ_W = HM * EM
UKV_W = HM * (NOPE + VM)
C_AT = 3 * WA
KV_AT = C_AT + QR
KR_AT = KV_AT + KR
MQ, MK, MV = 0, HM * EM, 2 * HM * EM
SM_W = 2 * HM * EM + HM * VM
NF = ROPE // 2
EPS = 1e-6

PH, NKEY, PQ, TOPK = 8, 128, 256, 16
HALFQ = PQ // 2
RUN = [TOPK // (a + 1) for a in range(TOPK)]
RUN_AT = [sum(RUN[:a]) for a in range(TOPK)]
NC_ = sum(RUN)
NEXP = NKEY * NKEY

TWO_PI_HI = 6.28125
TWO_PI_LO = 1.9353071795864769e-3
ROUND = 12582912.0
BIG = 1e30
ONE = 1
LOWEST = -3.0e38

f32 = mybir.dt.float32
f32r = mybir.dt.float32r
i32 = mybir.dt.int32
u32 = mybir.dt.uint32
ALU = mybir.AluOpType
ACT = mybir.ActivationFunctionType
AX = mybir.AxisListType.X


class Own:

    def __init__(self, eng, sem):
        self.eng, self.sem, self.n = eng, sem, 0

    def mark(self, ins):
        ins.then_inc(self.sem, 1)
        self.n += 1
        return self.n

    def link(self, ins):
        self.mark(ins)
        self.eng.wait_ge(self.sem, self.n)

    def sync(self):
        self.eng.wait_ge(self.sem, self.n)

    def restart(self):
        if self.n:
            self.eng.wait_ge(self.sem, self.n)
            self.eng.sem_clear(self.sem)
        self.n = 0


def open_counts(nc, sems):
    with nc.Block() as block:
        @block.sync
        def _(sp):
            for s in sems:
                sp.sem_inc(s, ONE)


class Core:

    def __init__(self, nc, ctx, ins, out):
        self.nc, self.i, self.out = nc, ins, out
        self.sb = lambda name, shape, dt=f32, c=ctx: c.enter_context(nc.sbuf_tensor(name, shape, dt))
        self.ps = ctx.enter_context(nc.psum_tensor("psum", [P, 8, BANK], f32))
        self.res = self.sb("res", [P, NT, D])
        self.ident = self.sb("ident", [P, P])
        self.g_ffn = self.sb("g_ffn_col", [P, KD])
        dram = lambda name, shape: nc.dram_tensor(name, shape, f32, kind="Internal").ap()
        self.scr_a = dram("scr_a", [SEQ, C_AT])
        self.scr_m = dram("scr_m", [SEQ, SM_W])
        self.scr_hi = dram("scr_hi", [P, KD, SEQ])
        self.scr_lo = dram("scr_lo", [P, KD, SEQ])
        self.scr_g = dram("scr_g", [NKEY, NKEY, SEQ])

    def scope(self, ctx):
        sb = lambda name, shape, dt=f32: ctx.enter_context(self.nc.sbuf_tensor(name, shape, dt))
        sem = lambda name: ctx.enter_context(self.nc.semaphore(name))
        return sb, sem


def column(v, n):
    return v.rearrange("(k p) -> p k", p=P)


def project_in(core):
    nc, ps, res = core.nc, core.ps, core.res
    I = core.i
    with ExitStack() as ctx:
        sb, sem = core.scope(ctx)
        w_in = sb("w_in", [P, KD, IN_W])
        w_uq = sb("w_uq", [P, 2, UQ_W])
        w_ukv = sb("w_ukv", [P, UKV_W])
        g_mix = sb("g_mix", [P, KD])
        g_c = sb("g_c", [P, 3])
        pos_i = sb("pos_i", [P, NT], i32)
        pos = sb("pos", [P, NT])
        freq = sb("freq", [P, NF])
        ang = sb("ang", [P, NT, NF])
        turn = sb("turn", [P, NT, NF])
        trig = sb("trig", [P, 2, NT, NF])
        ss = sb("ss", [P, NT])
        rstd = sb("rstd", [P, NT])
        junk = sb("junk", [P, D])
        xn = sb("xn", [P, 2, D])
        hT = sb("hT", [P, 2, KD, P])
        st_a = sb("st_a", [P, 2, IN_W])
        st_m = sb("st_m", [P, 2, SM_W])
        ssc = sb("ssc", [P, 2, 2])
        rstc = sb("rstc", [P, 2, 2])
        cn = sb("cn", [P, 2, QR + KR])
        cT = sb("cT", [P, 2, 3, P])
        rt = sb("rt", [P, 4, 2 * HA, NF])

        x_in = [sem(f"x_in{n}") for n in range(NT // 2)]
        w_in_in = [sem(f"w_in_in{n}") for n in range(4)]
        small_in, wc_in = sem("small_in"), sem("wc_in")
        act_own, dve_own = sem("act_own"), sem("dve_own")
        ss_ready, ms_ready, rms_ready = sem("ss_ready"), sem("ms_ready"), sem("rms_ready")
        ang_ready, trig_ready = sem("ang_ready"), sem("trig_ready")
        xn_ready, xT_done, hT_ready = sem("xn_ready"), sem("xT_done"), sem("hT_ready")
        chunk_done, chunk_out = sem("chunk_done"), sem("chunk_out")
        css_ready, cms_ready, crms_ready = sem("css_ready"), sem("cms_ready"), sem("crms_ready")
        cn_ready, cnT_done, cT_ready = sem("cn_ready"), sem("cnT_done"), sem("cT_ready")
        a_roped, m_roped = sem("a_roped"), sem("m_roped")
        a_sent = [sem(f"a_sent{k}") for k in range(2)]
        m_sent = [sem(f"m_sent{k}") for k in range(2)]
        SLOTS = 4
        PER = 16

        def width(c):
            return min(BANK, IN_W - c * BANK)

        x_v = I["x"].rearrange("b (i p) d -> p (b i) d", p=P)
        w_v = I["w_in"].rearrange("l (k p) n -> p (l k) n", p=P)
        open_counts(nc, (a_roped, *a_sent, cT_ready, chunk_done, chunk_out, cms_ready, cnT_done, cn_ready, crms_ready,
                         css_ready, hT_ready, m_roped, *m_sent, xT_done, xn_ready))
        block = ctx.enter_context(nc.Block())

        @block.sync
        def _(sp):
            for n in range(NT // 2):
                sp.dma_start(res[:, 2 * n:2 * n + 2, :], x_v[:, 2 * n:2 * n + 2, :]).then_inc(x_in[n], 16)
                if n == 0:
                    for c in range(2):
                        sp.dma_start(w_in[:, :, c * BANK:c * BANK + width(c)],
                                     w_v[:, :, c * BANK:c * BANK + width(c)]).then_inc(w_in_in[c], 16)
            for c in range(2, 4):
                sp.dma_start(w_in[:, :, c * BANK:c * BANK + width(c)],
                             w_v[:, :, c * BANK:c * BANK + width(c)]).then_inc(w_in_in[c], 16)
            sp.dma_start(w_uq[:, :, :], I["w_uq"].rearrange("l (k p) n -> p (l k) n", p=P)).then_inc(wc_in, 16)
            sp.dma_start(w_ukv[:, :], I["w_ukv"].rearrange("l p n -> p (l n)")).then_inc(wc_in, 16)
            with sp.Fori(0, NT // 2) as it:
                for k in range(2):
                    sp.wait_ge(a_roped, ONE + it * 2 + k + 1)
                    sp.dma_start(core.scr_a.rearrange("(i p) n -> i p n", p=P)[it * 2 + k],
                                 st_a[:, k, 0:C_AT]).then_inc(a_sent[k], 16)
                for k in range(2):
                    sp.wait_ge(m_roped, ONE + it * 2 + k + 1)
                    sp.dma_start(core.scr_m.rearrange("(i p) n -> i p n", p=P)[it * 2 + k],
                                 st_m[:, k, :]).then_inc(m_sent[k], 16)
            for k in range(2):
                sp.wait_ge(a_sent[k], ONE + 16 * NT // 2)
                sp.wait_ge(m_sent[k], ONE + 16 * NT // 2)

        @block.scalar
        def _(act):
            own = Own(act, act_own)
            with nc.allow_non_contiguous_dma(reason="gains and positions as columns"):
                act.dma_start(pos_i[:, :], I["positions"].rearrange("b (i p) -> p (b i)", p=P)).then_inc(small_in, 16)
                act.dma_start(g_mix[:, :], column(I["g_mix"][0], KD)).then_inc(small_in, 16)
                act.dma_start(core.g_ffn[:, :], column(I["g_ffn"][0], KD)).then_inc(small_in, 16)
                act.dma_start(g_c[:, 0:2], column(I["g_cq"][0], 2)).then_inc(small_in, 16)
                act.dma_start(g_c[:, 2:3], column(I["g_ckv"][0], 1)).then_inc(small_in, 16)
            act.dma_start(freq[:, :], I["c_freq"]).then_inc(small_in, 16)
            act.dma_start(core.ident[:, :], I["c_ident"]).then_inc(small_in, 16)
            for i in range(NT):
                act.wait_ge(x_in[i // 2], 16)
                if i:
                    own.sync()
                own.mark(nc.scalar.activation(junk[:, :], res[:, i, :], ACT.Square, accum_out=ss[:, i:i + 1]))
            own.sync()
            act.sem_inc(ss_ready, 1)
            act.wait_ge(ms_ready, 1)
            nc.scalar.activation(rstd[:, :], ss[:, :], ACT.Sqrt).then_inc(rms_ready, 1)
            act.wait_ge(ang_ready, 1)
            nc.scalar.activation(trig[:, :, :, :], trig[:, :, :, :], ACT.Sin).then_inc(trig_ready, 1)
            own.restart()
            with act.Fori(0, NT // 2) as it:
                for k in range(2):
                    act.wait_ge(a_sent[k], ONE + it * 16)
                    for c in range(4):
                        act.wait_ge(chunk_done, ONE + it * PER + k * 4 + c + 1)
                        own.mark(nc.scalar.activation(st_a[:, k, c * BANK:c * BANK + width(c)],
                                                      ps[:, 2 + c, 0:width(c)], ACT.Copy))
                        own.sync()
                        act.sem_inc(chunk_out, 1)
                    own.mark(nc.scalar.activation(junk[:, 0:QR], st_a[:, k, C_AT:KV_AT], ACT.Square,
                                                  accum_out=ssc[:, k, 0:1]))
                    own.mark(nc.scalar.activation(junk[:, QR:QR + KR], st_a[:, k, KV_AT:KR_AT], ACT.Square,
                                                  accum_out=ssc[:, k, 1:2]))
                    own.sync()
                    act.sem_inc(css_ready, 1)
                for k in range(2):
                    act.wait_ge(cms_ready, ONE + it * 2 + k + 1)
                    nc.scalar.activation(rstc[:, k, :], ssc[:, k, :], ACT.Sqrt).then_inc(crms_ready, 1)
                for k in range(2):
                    act.wait_ge(m_sent[k], ONE + it * 16)
                    mk = st_m[:, k, MK:MV].rearrange("p (h e) -> p h e", h=HM)
                    mv = st_m[:, k, MV:SM_W].rearrange("p (h e) -> p h e", h=HM)
                    for c in range(4):
                        act.wait_ge(chunk_done, ONE + it * PER + 8 + k * 4 + c + 1)
                        if c < 2:
                            n = min(BANK, UQ_W - c * BANK)
                            own.mark(nc.scalar.activation(st_m[:, k, c * BANK:c * BANK + n], ps[:, 2 + c, 0:n],
                                                          ACT.Copy))
                        else:
                            hs = slice((c - 2) * 4, (c - 2) * 4 + 4)
                            kv = ps[:, 2 + c, :].rearrange("p (h e) -> p h e", h=4)
                            own.mark(nc.scalar.activation(mk[:, hs, 0:NOPE], kv[:, :, 0:NOPE], ACT.Copy))
                            own.mark(nc.scalar.activation(mv[:, hs, :], kv[:, :, NOPE:], ACT.Copy))
                        own.sync()
                        act.sem_inc(chunk_out, 1)
                own.restart()

        @block.vector
        def _(dve):
            own = Own(dve, dve_own)
            dve.wait_ge(small_in, 16 * 7)
            own.link(nc.vector.tensor_copy(pos[:, :], pos_i[:, :]))
            own.link(nc.vector.tensor_tensor(
                ang[:, :, :], pos[:, :].rearrange("p (i o) -> p i o", o=1).to_broadcast([P, NT, NF]),
                freq[:, :].rearrange("p (o f) -> p o f", o=1).to_broadcast([P, NT, NF]), ALU.mult))
            for s, quarter in ((0, 0.25), (1, 0.0)):
                r = trig[:, s, :, :]
                own.link(nc.vector.tensor_scalar(turn[:, :, :], ang[:, :, :], 0.15915494309189535, quarter,
                                                 ALU.mult, ALU.add))
                own.link(nc.vector.tensor_scalar_add(turn[:, :, :], turn[:, :, :], ROUND))
                own.link(nc.vector.tensor_scalar_add(turn[:, :, :], turn[:, :, :], -ROUND))
                own.link(nc.vector.scalar_tensor_tensor(out=r, in0=turn[:, :, :], scalar=-TWO_PI_HI,
                                                        in1=ang[:, :, :], op0=ALU.mult, op1=ALU.add))
                own.link(nc.vector.scalar_tensor_tensor(out=r, in0=turn[:, :, :], scalar=-TWO_PI_LO,
                                                        in1=r, op0=ALU.mult, op1=ALU.add))
                own.link(nc.vector.tensor_scalar(r, r, 2 * 3.14159265358979 * quarter, 3.1415925,
                                                 ALU.add, ALU.min))
                own.link(nc.vector.tensor_scalar(r, r, -3.1415925, None, ALU.max))
            dve.sem_inc(ang_ready, 1)
            dve.wait_ge(ss_ready, 1)
            own.link(nc.vector.tensor_scalar(ss[:, :], ss[:, :], 1.0 / D, EPS, ALU.mult, ALU.add))
            dve.sem_inc(ms_ready, 1)
            dve.wait_ge(rms_ready, 1)
            own.link(nc.vector.reciprocal(rstd[:, :], rstd[:, :]))
            dve.sem_inc(chunk_out, SLOTS)
            dve.wait_ge(trig_ready, 1)
            own.restart()

            def rotate(k, i, x1, x2, heads, step, o1=None, o2=None, copies=1):
                n = NF // step
                c, s = (trig[:, z, bass.ts(i, 1), :].rearrange("p o f -> p (o f)")[:, 0:NF:step]
                        .rearrange("p (o f) -> p o f", o=1).to_broadcast([P, heads, n]) for z in range(2))
                t = [rt[:, z, 0:heads, 0:n] for z in range(4)]
                own.mark(nc.vector.tensor_tensor(t[0], x1, c, ALU.mult))
                own.mark(nc.vector.tensor_tensor(t[1], x2, s, ALU.mult))
                own.mark(nc.vector.tensor_tensor(t[2], x2, c, ALU.mult))
                own.mark(nc.vector.tensor_tensor(t[3], x1, s, ALU.mult))
                own.sync()
                if copies > 1:
                    t = [u.to_broadcast([P, copies, n]) for u in t]
                own.mark(nc.vector.tensor_tensor(x1 if o1 is None else o1, t[0], t[1], ALU.subtract))
                own.mark(nc.vector.tensor_tensor(x2 if o2 is None else o2, t[2], t[3], ALU.add))
                own.sync()

            with dve.Fori(0, NT // 2) as it:
                for k in range(2):
                    dve.wait_ge(xT_done, ONE + it * 2)
                    nc.vector.tensor_scalar(xn[:, k, :], res[:, bass.ts(it * 2 + k, 1), :].rearrange("p o d -> p (o d)"),
                                            rstd[:, bass.ts(it * 2 + k, 1)], None, ALU.mult).then_inc(xn_ready, 1)
                for k in range(2):
                    dve.wait_ge(xT_done, ONE + it * 2 + k + 1)
                    nc.vector.tensor_tensor(
                        hT[:, k, :, :], ps[:, 0:2, :].rearrange("p b (j t) -> p (b j) t", t=P),
                        g_mix[:, :].rearrange("p (j o) -> p j o", o=1).to_broadcast([P, KD, P]),
                        ALU.mult).then_inc(hT_ready, 1)
                for k in range(2):
                    dve.wait_ge(css_ready, ONE + it * 2 + k + 1)
                    own.mark(nc.vector.tensor_scalar(ssc[:, k, 0:1], ssc[:, k, 0:1], 1.0 / QR, EPS, ALU.mult, ALU.add))
                    own.mark(nc.vector.tensor_scalar(ssc[:, k, 1:2], ssc[:, k, 1:2], 1.0 / KR, EPS, ALU.mult, ALU.add))
                    own.sync()
                    dve.sem_inc(cms_ready, 1)
                    qk = st_a[:, k, 0:2 * WA].rearrange("p (h e) -> p h e", e=EA)
                    rotate(k, it * 2 + k, qk[:, :, 0:ROT_A // 2], qk[:, :, ROT_A // 2:ROT_A], 2 * HA, 2)
                    dve.sem_inc(a_roped, 1)
                for k in range(2):
                    dve.wait_ge(crms_ready, ONE + it * 2 + k + 1)
                    own.link(nc.vector.reciprocal(rstc[:, k, :], rstc[:, k, :]))
                    own.mark(nc.vector.tensor_scalar(cn[:, k, 0:QR], st_a[:, k, C_AT:KV_AT], rstc[:, k, 0:1], None, ALU.mult))
                    own.mark(nc.vector.tensor_scalar(cn[:, k, QR:], st_a[:, k, KV_AT:KR_AT], rstc[:, k, 1:2], None, ALU.mult))
                    own.sync()
                    dve.sem_inc(cn_ready, 1)
                for k in range(2):
                    dve.wait_ge(cnT_done, ONE + it * 2 + k + 1)
                    nc.vector.tensor_tensor(
                        cT[:, k, :, :], ps[:, 6 + k, 0:3 * P].rearrange("p (j t) -> p j t", t=P),
                        g_c[:, :].rearrange("p (j o) -> p j o", o=1).to_broadcast([P, 3, P]),
                        ALU.mult).then_inc(cT_ready, 1)
                for k in range(2):
                    dve.wait_ge(chunk_out, ONE + SLOTS + it * PER + 8 + k * 4 + 4)
                    q = st_m[:, k, MQ:MK].rearrange("p (h e) -> p h e", h=HM)
                    rotate(k, it * 2 + k, q[:, :, NOPE:NOPE + NF], q[:, :, NOPE + NF:], HM, 1)
                    kk = st_m[:, k, MK:MV].rearrange("p (h e) -> p h e", h=HM)
                    kr = st_a[:, k, KR_AT:IN_W].rearrange("p (o e) -> p o e", o=1)
                    rotate(k, it * 2 + k, kr[:, :, 0:NF], kr[:, :, NF:], 1, 1,
                           kk[:, :, NOPE:NOPE + NF], kk[:, :, NOPE + NF:], HM)
                    dve.sem_inc(m_roped, 1)
                own.restart()

        @block.tensor
        def _(pe):
            pe.wait_ge(small_in, 16 * 7)
            with pe.Fori(0, NT // 2) as it:
                for k in range(2):
                    pe.wait_ge(xn_ready, ONE + it * 2 + k + 1)
                    pe.wait_ge(hT_ready, ONE + it * 2 + k)
                    for j in range(KD):
                        last = nc.tensor.transpose(ps[:, j // 4, (j % 4) * P:(j % 4 + 1) * P],
                                                   xn[:, k, j * P:(j + 1) * P], core.ident[:, :])
                    last.then_inc(xT_done, 1)
                for k in range(2):
                    pe.wait_ge(hT_ready, ONE + it * 2 + k + 1)
                    for c in range(4):
                        pe.wait_ge(w_in_in[c], 16)
                        pe.wait_ge(chunk_out, ONE + it * PER + k * 4 + c + 1)
                        for j in range(KD):
                            last = nc.tensor.matmul(ps[:, 2 + c, 0:width(c)], hT[:, k, j, :],
                                                    w_in[:, j, c * BANK:c * BANK + width(c)],
                                                    start=j == 0, stop=j == KD - 1)
                        last.then_inc(chunk_done, 1)
                for k in range(2):
                    pe.wait_ge(cn_ready, ONE + it * 2 + k + 1)
                    for j in range(3):
                        last = nc.tensor.transpose(ps[:, 6 + k, j * P:(j + 1) * P], cn[:, k, j * P:(j + 1) * P],
                                                   core.ident[:, :])
                    last.then_inc(cnT_done, 1)
                pe.wait_ge(wc_in, 32)
                for k in range(2):
                    pe.wait_ge(cT_ready, ONE + it * 2 + k + 1)
                    for c in range(4):
                        pe.wait_ge(chunk_out, ONE + it * PER + 8 + k * 4 + c + 1)
                        if c < 2:
                            n = min(BANK, UQ_W - c * BANK)
                            for j in range(2):
                                last = nc.tensor.matmul(ps[:, 2 + c, 0:n], cT[:, k, j, :],
                                                        w_uq[:, j, c * BANK:c * BANK + n], start=j == 0, stop=j == 1)
                        else:
                            last = nc.tensor.matmul(ps[:, 2 + c, :], cT[:, k, 2, :],
                                                    w_ukv[:, (c - 2) * BANK:(c - 1) * BANK], start=True, stop=True)
                        last.then_inc(chunk_done, 1)


def attend(core, mix, mask, group, heads, dim, scr, q_at, k_at, v_at, mix_at):
    nc, ps = core.nc, core.ps
    ev = EA
    N = NT * 2
    with ExitStack() as ctx:
        sb, sem = core.scope(ctx)
        g = lambda s: f"{s}_{group}"
        qn, kn = sb(g("qn"), [P, 2, NT, dim]), sb(g("kn"), [P, 2, NT, dim])
        vn = sb(g("vn"), [P, 2, NT, ev])
        qT, kT = sb(g("qT"), [dim, 2, SEQ]), sb(g("kT"), [dim, 2, SEQ])
        sm = sb(g("sm"), [P, 2, SEQ])
        pr = sb(g("pr"), [P, 2, SEQ])
        pT = sb(g("pT"), [P, 2, NT, P])
        least = sb(g("least"), [P, N])
        den = sb(g("den"), [P, N])
        rden = sb(g("rden"), [P, N])
        qkv_in = [sem(g(f"qkv_in{k}")) for k in range(2)]
        qkv_used = [sem(g(f"qkv_used{k}")) for k in range(2)]
        score_done, masked_ready, prob_ready = sem(g("score_done")), sem(g("masked_ready")), sem(g("prob_ready"))
        turned = sem(g("turned"))
        out_act, out_dve = sem(g("out_act")), sem(g("out_dve"))
        pv_done, o_out = sem(g("pv_done")), sem(g("o_out"))
        dve_own, dve_held, pe_held = sem(g("dve_own")), sem(g("dve_held")), sem(g("pe_held"))
        scale = float(dim) ** -0.5

        fills, of_unit = [], {}
        order = []
        def fill(what):
            fills.append(what)
            return len(fills) - 1
        head_fills = {}

        def head_turn(k):
            head_fills[k] = [fill(("qk", k, z, half)) for z in range(2) for half in range(2)]
            order.append(("head", k))

        def score(u):
            if u < N:
                if u % NT == 0:
                    head_turn(u // NT)
                order.append(("score", u))

        score(0)
        score(1)
        for u in range(N):
            i = u % NT
            of_unit[u] = [fill(("p", u, b0, min(4, i + 1 - b0))) for b0 in range(0, i + 1, 4)]
            order.append(("turn", u))
            score(u + 2)
            order.append(("pv", u))
        NFILL = len(fills)
        assert NFILL % 2 == 0

        def outs_before(n):
            return (n + 1) // 2, n // 2

        open_counts(nc, (masked_ready, o_out, out_act, out_dve, prob_ready, pv_done, *qkv_in, *qkv_used, score_done,
                         turned))
        block = ctx.enter_context(nc.Block())

        @block.sync
        def _(sp):
            tiles = scr.rearrange("(i p) n -> p i n", p=P)
            with sp.Fori(0, heads // 2) as it:
                for k in range(2):
                    sp.wait_ge(qkv_used[k], ONE + it)
                    for dst, at, w in ((qn, q_at, dim), (kn, k_at, dim), (vn, v_at, ev)):
                        sp.dma_start(dst[:, k, :, :], tiles[:, :, bass.ds(it * (2 * w) + (at + k * w), w)]
                                     ).then_inc(qkv_in[k], 16)

        @block.tensor
        def _(pe):
            def wait_bank(it, n):
                a, d = outs_before(n)
                if n % 2 == 0:
                    pe.wait_ge(out_act, ONE + it * (NFILL // 2) + a)
                else:
                    pe.wait_ge(out_dve, ONE + it * (NFILL // 2) + d)

            def wait_copied(it, n):
                a, d = outs_before(n + 1)
                if n % 2 == 0:
                    pe.wait_ge(out_act, ONE + it * (NFILL // 2) + a)
                else:
                    pe.wait_ge(out_dve, ONE + it * (NFILL // 2) + d)

            with pe.Fori(0, heads // 2) as it:
                for kind, x in order:
                    if kind == "head":
                        pe.wait_ge(qkv_in[x], ONE + it * 48 + 48)
                        for n in head_fills[x]:
                            _, _, z, half = fills[n]
                            wait_bank(it, n)
                            pe.sem_inc(pe_held, 1)
                            src = (qn, kn)[z]
                            for j in range(4):
                                last = nc.tensor.transpose(ps[0:dim, 4 + n % 2, j * P:(j + 1) * P],
                                                           src[:, x, half * 4 + j, :], core.ident[:, :])
                            last.then_inc(turned, 1)
                        for n in head_fills[x][-2:]:
                            wait_copied(it, n)
                    elif kind == "score":
                        k, i, b = x // NT, x % NT, x % 2
                        nk = (i + 1) * P
                        pe.wait_ge(masked_ready, ONE + (it * N + x - 1 if x else it * N))
                        for c in range(0, nk, BANK):
                            w = min(BANK, nk - c)
                            last = nc.tensor.matmul(ps[:, 2 * b + c // BANK, 0:w], qT[:, k, i * P:(i + 1) * P],
                                                    kT[:, k, c:c + w], start=True, stop=True)
                        last.then_inc(score_done, 1)
                    elif kind == "turn":
                        k, b = x // NT, x % 2
                        pe.wait_ge(prob_ready, ONE + it * N + x + 1)
                        for n in of_unit[x]:
                            _, _, b0, nb = fills[n]
                            wait_bank(it, n)
                            for j in range(nb):
                                last = nc.tensor.transpose(ps[:, 4 + n % 2, j * P:(j + 1) * P],
                                                           pr[:, b, (b0 + j) * P:(b0 + j + 1) * P], core.ident[:, :])
                            last.then_inc(turned, 1)
                    else:
                        k, i, b = x // NT, x % NT, x % 2
                        for n in of_unit[x]:
                            wait_copied(it, n)
                        pe.wait_ge(o_out, ONE + (it * N + x - 1 if x else it * N))
                        for j in range(i + 1):
                            last = nc.tensor.matmul(ps[:, 6 + b, 0:ev], pT[:, b, j, :], vn[:, k, j, :],
                                                    start=j == 0, stop=j == i)
                        last.then_inc(pv_done, 1)
                        if i == NT - 1:
                            pe.wait_ge(pv_done, ONE + it * N + x + 1)
                            pe.sem_inc(qkv_used[k], 1)

        def copy_fill(eng, it, n):
            what, x, z, c = fills[n]
            eng.wait_ge(turned, ONE + it * NFILL + n + 1)
            done = (out_act, out_dve)[n % 2]
            if what == "qk":
                dst = (qT, kT)[z][:, x, c * BANK:(c + 1) * BANK]
                src = ps[0:dim, 4 + n % 2, :]
                s = -scale if z == 0 else 1.0
                if n % 2 == 0:
                    nc.scalar.activation(dst, src, ACT.Copy, scale=s).then_inc(done, 1)
                else:
                    nc.vector.tensor_scalar_mul(dst, src, s).then_inc(done, 1)
            else:
                eng.wait_ge(pv_done, ONE + (it * N + x - 1 if x else it * N))
                dst = pT[:, x % 2, z:z + c, :]
                src = ps[:, 4 + n % 2, 0:c * P].rearrange("p (j t) -> p j t", t=P)
                if n % 2 == 0:
                    nc.scalar.activation(dst, src, ACT.Copy).then_inc(done, 1)
                else:
                    nc.vector.tensor_copy(dst, src).then_inc(done, 1)

        @block.scalar
        def _(act):
            def exp(it, u):
                i, b = u % NT, u % 2
                nk = (i + 1) * P
                act.wait_ge(masked_ready, ONE + it * N + u + 1)
                if u >= 2:
                    act.wait_ge(turned, ONE + it * NFILL + of_unit[u - 2][-1] + 1)
                else:
                    act.wait_ge(turned, ONE + it * NFILL)
                nc.scalar.activation(pr[:, b, 0:nk], sm[:, b, 0:nk], ACT.Exp, scale=-1.0, bias=least[:, u:u + 1],
                                     accum_out=den[:, u:u + 1]).then_inc(prob_ready, 1)

            with act.Fori(0, heads // 2) as it:
                for kind, x in order:
                    if kind == "head":
                        for n in head_fills[x]:
                            if n % 2 == 0:
                                copy_fill(act, it, n)
                    elif kind == "score":
                        exp(it, x)
                    elif kind == "turn":
                        for n in of_unit[x]:
                            if n % 2 == 0:
                                copy_fill(act, it, n)

        @block.vector
        def _(dve):
            own = Own(dve, dve_own)
            with dve.Fori(0, heads // 2) as it:
                for kind, x in order:
                    if kind == "head":
                        for n in head_fills[x]:
                            if n % 2 == 1:
                                copy_fill(dve, it, n)
                    elif kind == "score":
                        i, b = x % NT, x % 2
                        nk = (i + 1) * P
                        dve.wait_ge(prob_ready, ONE + (it * N + x - 1 if x else it * N))
                        dve.wait_ge(score_done, ONE + it * N + x + 1)
                        dve.sem_inc(dve_held, 1)
                        nc.vector.tensor_tensor_reduce(
                            out=sm[:, b, 0:nk], in0=ps[:, 2 * b:2 * b + 2, :].rearrange("p b n -> p (b n)")[:, 0:nk],
                            in1=mask[:, (NT - 1 - i) * P:], scale=1.0, scalar=3.0e38, op0=ALU.add, op1=ALU.min,
                            accum_out=least[:, x:x + 1]).then_inc(masked_ready, 1)
                    elif kind == "turn":
                        for n in of_unit[x]:
                            if n % 2 == 1:
                                copy_fill(dve, it, n)
                    else:
                        k, i, b = x // NT, x % NT, x % 2
                        own.link(nc.vector.reciprocal(rden[:, x:x + 1], den[:, x:x + 1]))
                        dve.wait_ge(pv_done, ONE + it * N + x + 1)
                        nc.vector.tensor_scalar(mix[:, i, bass.ds(it * (2 * ev) + (mix_at + k * ev), ev)],
                                                ps[:, 6 + b, 0:ev], rden[:, x:x + 1], None, ALU.mult).then_inc(o_out, 1)
                own.restart()


def project_out(core, mix, w_out, w_out_in):
    nc, ps, res = core.nc, core.ps, core.res
    with ExitStack() as ctx:
        sb, sem = core.scope(ctx)
        st = sb("mix_st", [P, 2, D])
        mT = sb("mixT", [P, 2, KD, P])
        hn = sb("hn", [P, 2, D])
        full = sb("hnT", [P, 2, KD, P])
        hi = sb("hnT_hi", [P, 2, KD, P], f32r)
        lo = sb("hnT_lo", [P, 2, KD, P], f32r)
        junk = sb("junk_o", [P, D])
        ss = sb("ss_o", [P, 2])
        rstd = sb("rstd_o", [P, 2])
        staged, mT_done, mT_ready = sem("staged"), sem("mT_done"), sem("mT_ready")
        y_done, h_ready, hss_ready, hms_ready, hrms_ready = (sem(x) for x in (
            "y_done", "h_ready", "hss_ready", "hms_ready", "hrms_ready"))
        hn_ready, hnT_done, full_ready, hi_ready, lo_ready = (sem(x) for x in (
            "hn_ready", "hnT_done", "full_ready", "hi_ready", "lo_ready"))
        hi_sent = [sem(f"hi_sent{k}") for k in range(2)]
        lo_sent = [sem(f"lo_sent{k}") for k in range(2)]
        own_a, own_v = sem("act_own_o"), sem("dve_own_o")
        open_counts(nc, (full_ready, h_ready, hi_ready, *hi_sent, hms_ready, hnT_done, hn_ready, hrms_ready, hss_ready,
                         lo_ready, *lo_sent, mT_done, mT_ready, staged, y_done))
        block = ctx.enter_context(nc.Block())

        def split_banks(k):
            return ps[:, 2 + 2 * k:4 + 2 * k, :]

        @block.sync
        def _(sp):
            with sp.Fori(0, NT // 2) as it:
                for k in range(2):
                    at = bass.ts(it * 2 + k, P)
                    sp.wait_ge(hi_ready, ONE + it * 2 + k + 1)
                    sp.dma_start(core.scr_hi[:, :, at], hi[:, k, :, :].bitcast(f32)).then_inc(hi_sent[k], 16)
                    sp.wait_ge(lo_ready, ONE + it * 2 + k + 1)
                    sp.dma_start(core.scr_lo[:, :, at], lo[:, k, :, :].bitcast(f32)).then_inc(lo_sent[k], 16)
            for k in range(2):
                sp.wait_ge(hi_sent[k], ONE + 16 * NT // 2)
                sp.wait_ge(lo_sent[k], ONE + 16 * NT // 2)

        @block.tensor
        def _(pe):
            pe.wait_ge(w_out_in, 16)
            with pe.Fori(0, NT // 2) as it:
                for k in range(2):
                    pe.wait_ge(staged, ONE + it * 2 + k + 1)
                    pe.wait_ge(mT_ready, ONE + it * 2 + k)
                    for j in range(KD):
                        last = nc.tensor.transpose(ps[:, j // 4, (j % 4) * P:(j % 4 + 1) * P],
                                                   st[:, k, j * P:(j + 1) * P], core.ident[:, :])
                    last.then_inc(mT_done, 1)
                for k in range(2):
                    pe.wait_ge(mT_ready, ONE + it * 2 + k + 1)
                    pe.wait_ge(h_ready, ONE + it * 2)
                    for c in range(2):
                        for j in range(KD):
                            last = nc.tensor.matmul(split_banks(k)[:, c, :], mT[:, k, j, :],
                                                    w_out[:, j, c * BANK:(c + 1) * BANK], start=j == 0, stop=j == KD - 1)
                    last.then_inc(y_done, 1)
                for k in range(2):
                    pe.wait_ge(hn_ready, ONE + it * 2 + k + 1)
                    pe.wait_ge(full_ready, ONE + it * 2 + k)
                    for j in range(KD):
                        last = nc.tensor.transpose(ps[:, 6 + j // 4, (j % 4) * P:(j % 4 + 1) * P],
                                                   hn[:, k, j * P:(j + 1) * P], core.ident[:, :])
                    last.then_inc(hnT_done, 1)

        @block.scalar
        def _(act):
            own = Own(act, own_a)
            with act.Fori(0, NT // 2) as it:
                for k in range(2):
                    act.wait_ge(mT_done, ONE + it * 2)
                    nc.scalar.activation(st[:, k, :], mix[:, bass.ts(it * 2 + k, 1), :].rearrange("p o d -> p (o d)"),
                                         ACT.Copy).then_inc(staged, 1)
                for k in range(2):
                    act.wait_ge(h_ready, ONE + it * 2 + k + 1)
                    own.sync()
                    own.mark(nc.scalar.activation(junk[:, :], res[:, bass.ts(it * 2 + k, 1), :].rearrange("p o d -> p (o d)"),
                                                  ACT.Square, accum_out=ss[:, k:k + 1]))
                    own.sync()
                    act.sem_inc(hss_ready, 1)
                for k in range(2):
                    act.wait_ge(hms_ready, ONE + it * 2 + k + 1)
                    nc.scalar.activation(rstd[:, k:k + 1], ss[:, k:k + 1], ACT.Sqrt).then_inc(hrms_ready, 1)
                for k in range(2):
                    act.wait_ge(hi_sent[k], ONE + it * 16)
                    act.wait_ge(full_ready, ONE + it * 2 + k + 1)
                    nc.scalar.activation(hi[:, k, :, :], full[:, k, :, :], ACT.Copy).then_inc(hi_ready, 1)
                own.restart()

        @block.vector
        def _(dve):
            own = Own(dve, own_v)
            with dve.Fori(0, NT // 2) as it:
                for k in range(2):
                    dve.wait_ge(mT_done, ONE + it * 2 + k + 1)
                    nc.vector.tensor_copy(mT[:, k, :, :], ps[:, 0:2, :].rearrange("p b (j t) -> p (b j) t", t=P)
                                          ).then_inc(mT_ready, 1)
                for k in range(2):
                    dve.wait_ge(y_done, ONE + it * 2 + k + 1)
                    h = res[:, bass.ts(it * 2 + k, 1), :].rearrange("p o d -> p (o d)")
                    nc.vector.tensor_tensor(h, split_banks(k).rearrange("p b n -> p (b n)"), h, ALU.add
                                            ).then_inc(h_ready, 1)
                for k in range(2):
                    dve.wait_ge(hss_ready, ONE + it * 2 + k + 1)
                    own.link(nc.vector.tensor_scalar(ss[:, k:k + 1], ss[:, k:k + 1], 1.0 / D, EPS, ALU.mult, ALU.add))
                    dve.sem_inc(hms_ready, 1)
                for k in range(2):
                    dve.wait_ge(hrms_ready, ONE + it * 2 + k + 1)
                    own.link(nc.vector.reciprocal(rstd[:, k:k + 1], rstd[:, k:k + 1]))
                    dve.wait_ge(hnT_done, ONE + it * 2)
                    nc.vector.tensor_scalar(hn[:, k, :], res[:, bass.ts(it * 2 + k, 1), :].rearrange("p o d -> p (o d)"),
                                            rstd[:, k:k + 1], None, ALU.mult).then_inc(hn_ready, 1)
                for k in range(2):
                    dve.wait_ge(hnT_done, ONE + it * 2 + k + 1)
                    nc.vector.tensor_tensor(
                        full[:, k, :, :], ps[:, 6:8, :].rearrange("p b (j t) -> p (b j) t", t=P),
                        core.g_ffn[:, :].rearrange("p (j o) -> p j o", o=1).to_broadcast([P, KD, P]),
                        ALU.mult).then_inc(full_ready, 1)
                for k in range(2):
                    dve.wait_ge(hi_ready, ONE + it * 2 + k + 1)
                    dve.wait_ge(lo_sent[k], ONE + it * 16)
                    nc.vector.tensor_tensor(lo[:, k, :, :], full[:, k, :, :], hi[:, k, :, :].bitcast(f32), ALU.subtract
                                            ).then_inc(lo_ready, 1)
                own.restart()


def rank_keys(core, hn_hi, hn_lo, hn_in, vals, idxf):
    nc, ps = core.nc, core.ps
    with ExitStack() as ctx:
        sb, sem = core.scope(ctx)
        w_raw = sb("w_raw", [P, 2, KD, PQ])
        w_hi = sb("w_hi", [P, KD, PQ], f32r)
        w_lo = sb("w_lo", [P, KD, PQ], f32r)
        keys = sb("keys", [P, 2, 2, HALFQ])
        keysT = sb("keysT", [P, 2, NKEY])
        qT = sb("peer_qT", [P, 2, SEQ])
        sc = sb("sc", [P, 2, NT, NKEY])
        sc2 = sb("sc2", [P, 2, NT, NKEY])
        v_st = sb("v_st", [P, 2, NT, TOPK])
        i_st = sb("i_st", [P, 2, NT, TOPK], u32)
        w_pq_in = [sem(f"w_pq_in{b}") for b in range(2)]
        keys_in = [sem(f"keys_in{b}") for b in range(2)]
        hi_made, lo_made, kT_done, kT_ready = sem("wpq_hi_made"), sem("wpq_lo_made"), sem("kT_done"), sem("kT_ready")
        q_done, q_out, sc_done, sc_out, ranked = (sem(x) for x in ("q_done", "q_out", "sc_done", "sc_out", "ranked"))
        own_v, held = sem("dve_own_r"), sem("dve_held_r")
        open_counts(nc, (hi_made, kT_done, kT_ready, *keys_in, lo_made, q_done, q_out, ranked, sc_done, sc_out, *w_pq_in))
        block = ctx.enter_context(nc.Block())
        NH2 = PH // 2

        @block.sync
        def _(sp):
            w_v = core.i["w_pq"].rearrange("l (k p) n -> p (l k) n", p=P)
            k_v = core.i["sub_keys"].rearrange("l h z n c -> n (l h) z c")
            with sp.Fori(0, NH2) as it:
                for b in range(2):
                    sp.wait_ge(hi_made, ONE + it * 2)
                    sp.wait_ge(lo_made, ONE + it * 2)
                    sp.dma_start(w_raw[:, b, :, :], w_v[:, :, bass.ds(it * (2 * PQ) + b * PQ, PQ)]).then_inc(w_pq_in[b], 16)
                    sp.wait_ge(kT_done, ONE + it * 2)
                    sp.dma_start(keys[:, b, :, :], k_v[:, bass.ts(it * 2 + b, 1), :, :].rearrange("n o z c -> n (o z) c")
                                 ).then_inc(keys_in[b], 16)

        @block.tensor
        def _(pe):
            pe.wait_ge(hn_in, 32)
            with pe.Fori(0, NH2) as it:
                for b in range(2):
                    pe.wait_ge(keys_in[b], ONE + it * 16 + 16)
                    pe.wait_ge(kT_ready, ONE + it * 2 + b)
                    for z in range(2):
                        last = nc.tensor.transpose(ps[:, 2, z * NKEY:(z + 1) * NKEY], keys[:, b, z, :], core.ident[:, :])
                    last.then_inc(kT_done, 1)
                    pe.wait_ge(hi_made, ONE + it * 2 + b + 1)
                    pe.wait_ge(lo_made, ONE + it * 2 + b + 1)
                    for z in range(2):
                        cs = slice(z * HALFQ, (z + 1) * HALFQ)
                        for half in range(2):
                            pe.wait_ge(q_out, ONE + (it * 8 + b * 4 + z * 2 + half - 1 if b or z or half else it * 8))
                            ts = slice(half * BANK, (half + 1) * BANK)
                            terms = [(w, x, j) for w, x in ((w_hi, hn_hi), (w_hi, hn_lo), (w_lo, hn_hi)) for j in range(KD)]
                            for n, (w, x, j) in enumerate(terms):
                                last = nc.tensor.matmul(ps[:, half, :], w[:, j, cs], x[:, j, ts],
                                                        start=n == 0, stop=n == len(terms) - 1)
                            last.then_inc(q_done, 1)
                    pe.wait_ge(kT_ready, ONE + it * 2 + b + 1)
                    for z in range(2):
                        pe.wait_ge(q_out, ONE + it * 8 + b * 4 + z * 2 + 2)
                        pe.wait_ge(sc_out, ONE + (it * 4 + b * 2 + z - 1 if b or z else it * 4))
                        for i in range(NT):
                            last = nc.tensor.matmul(ps[:, 4 + 2 * z + i // 4, (i % 4) * P:(i % 4 + 1) * P],
                                                    qT[:, z, i * P:(i + 1) * P], keysT[:, z, :], start=True, stop=True)
                        last.then_inc(sc_done, 1)

        @block.scalar
        def _(act):
            with act.Fori(0, NH2) as it:
                for b in range(2):
                    act.wait_ge(w_pq_in[b], ONE + it * 16 + 16)
                    act.wait_ge(q_done, ONE + it * 8 + b * 4)
                    nc.scalar.activation(w_hi[:, :, :], w_raw[:, b, :, :], ACT.Copy).then_inc(hi_made, 1)
                    act.wait_ge(kT_done, ONE + it * 2 + b + 1)
                    act.wait_ge(sc_done, ONE + it * 4 + b * 2)
                    nc.scalar.activation(keysT[:, :, :], ps[:, 2, 0:2 * NKEY].rearrange("p (z n) -> p z n", z=2),
                                         ACT.Copy).then_inc(kT_ready, 1)
                    for z in range(2):
                        for half in range(2):
                            act.wait_ge(q_done, ONE + it * 8 + b * 4 + z * 2 + half + 1)
                            nc.scalar.activation(qT[:, z, half * BANK:(half + 1) * BANK], ps[:, half, :],
                                                 ACT.Copy).then_inc(q_out, 1)
                    for z in range(2):
                        act.wait_ge(sc_done, ONE + it * 4 + b * 2 + z + 1)
                        act.wait_ge(ranked, ONE + (it * 4 + b * 2 + z - 1 if b or z else it * 4))
                        nc.scalar.activation(sc[:, z, :, :], ps[:, 4 + 2 * z:6 + 2 * z, :].rearrange(
                            "p b (i n) -> p (b i) n", n=NKEY), ACT.Copy).then_inc(sc_out, 1)

        @block.vector
        def _(dve):
            own = Own(dve, own_v)
            with dve.Fori(0, NH2) as it:
                for b in range(2):
                    dve.wait_ge(hi_made, ONE + it * 2 + b + 1)
                    nc.vector.tensor_tensor(w_lo[:, :, :], w_raw[:, b, :, :], w_hi[:, :, :].bitcast(f32), ALU.subtract
                                            ).then_inc(lo_made, 1)
                    for z in range(2):
                        dve.wait_ge(sc_out, ONE + it * 4 + b * 2 + z + 1)
                        dve.sem_inc(held, 1)
                        for i in range(NT):
                            own.mark(nc.vector.max(v_st[:, z, i, 0:8], sc[:, z, i, :]))
                        own.sync()
                        for i in range(NT):
                            own.mark(nc.vector.max_index(i_st[:, z, i, 0:8], v_st[:, z, i, 0:8], sc[:, z, i, :]))
                            own.mark(nc.vector.match_replace(sc2[:, z, i, :], v_st[:, z, i, 0:8], sc[:, z, i, :], LOWEST))
                        own.sync()
                        for i in range(NT):
                            own.mark(nc.vector.max(v_st[:, z, i, 8:16], sc2[:, z, i, :]))
                        own.sync()
                        dve.sem_inc(ranked, 1)
                        for i in range(NT):
                            own.mark(nc.vector.max_index(i_st[:, z, i, 8:16], v_st[:, z, i, 8:16], sc2[:, z, i, :]))
                        own.sync()
                    h = bass.ts(it * 2 + b, 1)
                    own.mark(nc.vector.tensor_copy(vals[:, h, :, :, :].rearrange("p o z i k -> p (o z i k)"),
                                                   v_st[:, :, :, :].rearrange("p z i k -> p (z i k)")))
                    own.mark(nc.vector.tensor_copy(idxf[:, h, :, :, :].rearrange("p o z i k -> p (o z i k)"),
                                                   i_st[:, :, :, :].rearrange("p z i k -> p (z i k)")))
                    own.restart()


def pick_experts(core, vals, idxf, slotT):
    nc, ps = core.nc, core.ps
    NS = PH * TOPK
    with ExitStack() as ctx:
        sb, sem = core.scope(ctx)
        pair = sb("pair", [P, PH, NC_])
        pair2 = sb("pair2", [P, PH, NC_])
        number = sb("number", [P, PH, NC_])
        best = sb("best", [P, PH, TOPK])
        at_u = sb("at_u", [P, PH, TOPK], u32)
        at = sb("at", [P, PH, TOPK])
        hit = sb("hit", [P, PH, TOPK, NC_])
        expert = sb("expert", [P, NS])
        expert_i = sb("expert_i", [P, NS], i32)
        key_i = sb("key_i", [P, 2, NS], i32)
        slot = sb("slot", [P, 3, NS])
        ex = sb("ex", [P, PH, TOPK])
        den = sb("den_p", [P, PH])
        iota = sb("iota_p", [P, NC_])
        iota_in, scaled, number_ready, number_used = (sem(x) for x in ("iota_in", "scaled", "number_ready", "number_used"))
        hit_ready, hit_numbered = sem("hit_ready"), sem("hit_numbered")
        centred, ex_ready, slot_ready, slotT_done, slotT_ready = (sem(x) for x in (
            "centred", "ex_ready", "slot_ready", "slotT_done", "slotT_ready"))
        own_v, own_p, held = sem("dve_own_e"), sem("pool_own_e"), sem("dve_held_e")
        HD = PH // 2
        open_counts(nc, (centred, ex_ready, hit_numbered, hit_ready, number_ready, number_used, slotT_done, slotT_ready,
                         slot_ready))
        block = ctx.enter_context(nc.Block())

        def ranks(t, i, z, a, n):
            return t[:, :, z, bass.ts(i, 1), a:a + n].rearrange("p h o k -> p h (o k)")

        def sums(eng, own, dst, t, i):
            for a in range(8):
                own.mark(eng.tensor_tensor(dst[:, :, RUN_AT[a]:RUN_AT[a] + RUN[a]],
                                           ranks(t, i, 0, a, 1).to_broadcast([P, PH, RUN[a]]),
                                           ranks(t, i, 1, 0, RUN[a]), ALU.add))
            own.mark(eng.tensor_tensor(dst[:, :, RUN_AT[8]:], ranks(t, i, 0, 8, 8),
                                       ranks(t, i, 1, 0, 1).to_broadcast([P, PH, 8]), ALU.add))
            own.sync()

        def number_of(eng, hs):
            return eng.tensor_tensor(
                hit[:, hs, :, :], hit[:, hs, :, :],
                number[:, hs, :].rearrange("p h (o c) -> p h o c", o=1).to_broadcast([P, hs.stop - hs.start, TOPK, NC_]),
                ALU.mult)

        @block.sync
        def _(sp):
            sp.dma_start(iota[:, :], core.i["c_iota"][:, 0:NC_]).then_inc(iota_in, 16)
            sp.wait_ge(iota_in, 16)

        @block.gpsimd
        def _(pool):
            own = Own(pool, own_p)
            pool.wait_ge(scaled, 1)
            pool.wait_ge(iota_in, 16)
            with pool.Fori(0, NT) as i:
                pool.wait_ge(number_used, ONE + i)
                sums(nc.gpsimd, own, number, idxf, i)
                pool.sem_inc(number_ready, 1)
                pool.wait_ge(hit_ready, ONE + i + 1)
                number_of(nc.gpsimd, slice(HD, PH)).then_inc(hit_numbered, 1)
                own.restart()

        @block.vector
        def _(dve):
            own = Own(dve, own_v)
            own.link(nc.vector.tensor_scalar_mul(idxf[:, :, 0, :, :], idxf[:, :, 0, :, :], float(NKEY)))
            dve.sem_inc(scaled, 1)
            dve.wait_ge(iota_in, 16)
            own.restart()
            with dve.Fori(0, NT) as i:
                sums(nc.vector, own, pair, vals, i)
                for h in range(PH):
                    own.mark(nc.vector.max(best[:, h, 0:8], pair[:, h, :]))
                own.sync()
                for h in range(PH):
                    own.mark(nc.vector.max_index(at_u[:, h, 0:8], best[:, h, 0:8], pair[:, h, :]))
                    own.mark(nc.vector.match_replace(pair2[:, h, :], best[:, h, 0:8], pair[:, h, :], LOWEST))
                own.sync()
                for h in range(PH):
                    own.mark(nc.vector.max(best[:, h, 8:16], pair2[:, h, :]))
                own.sync()
                for h in range(PH):
                    own.mark(nc.vector.max_index(at_u[:, h, 8:16], best[:, h, 8:16], pair2[:, h, :]))
                own.sync()
                own.mark(nc.vector.tensor_copy(at[:, :, :], at_u[:, :, :]))
                own.sync()
                own.mark(nc.vector.tensor_tensor(ex[:, :, :], best[:, :, :],
                                                 best[:, :, 0:1].to_broadcast([P, PH, TOPK]), ALU.subtract))
                own.sync()
                dve.sem_inc(centred, 1)
                for hs in (slice(HD, PH), slice(0, HD)):
                    own.mark(nc.vector.tensor_tensor(
                        hit[:, hs, :, :],
                        at[:, hs, :].rearrange("p h (k o) -> p h k o", o=1).to_broadcast([P, HD, TOPK, NC_]),
                        iota[:, :].rearrange("p (a b c) -> p a b c", a=1, b=1).to_broadcast([P, HD, TOPK, NC_]),
                        ALU.is_equal))
                    if hs.start:
                        own.sync()
                        dve.sem_inc(hit_ready, 1)
                own.sync()
                dve.wait_ge(number_ready, ONE + i + 1)
                own.link(number_of(nc.vector, slice(0, HD)))
                e3 = expert[:, :].rearrange("p (h k) -> p h k", h=PH)
                own.mark(nc.vector.tensor_reduce(e3[:, 0:HD, :], hit[:, 0:HD, :, :], AX, ALU.add))
                dve.wait_ge(ex_ready, ONE + i + 1)
                own.link(nc.vector.tensor_reduce(den[:, :], ex[:, :, :], AX, ALU.add))
                own.link(nc.vector.reciprocal(den[:, :], den[:, :]))
                dve.wait_ge(slotT_done, ONE + i)
                own.mark(nc.vector.tensor_tensor(
                    slot[:, 2, :].rearrange("p (h k) -> p h k", h=PH), ex[:, :, :],
                    den[:, :].rearrange("p (h o) -> p h o", o=1).to_broadcast([P, PH, TOPK]), ALU.mult))
                dve.wait_ge(hit_numbered, ONE + i + 1)
                own.mark(nc.vector.tensor_reduce(e3[:, HD:, :], hit[:, HD:, :, :], AX, ALU.add))
                own.sync()
                dve.sem_inc(number_used, 1)
                own.link(nc.vector.tensor_copy(expert_i[:, :], expert[:, :]))
                own.mark(nc.vector.tensor_single_scalar(key_i[:, 0, :], expert_i[:, :], 7, ALU.logical_shift_right))
                own.link(nc.vector.tensor_single_scalar(key_i[:, 1, :], expert_i[:, :], NKEY - 1, ALU.bitwise_and))
                own.mark(nc.vector.tensor_copy(slot[:, 0:2, :], key_i[:, :, :]))
                own.sync()
                dve.sem_inc(slot_ready, 1)
                own.restart()

        @block.scalar
        def _(act):
            with act.Fori(0, NT) as i:
                act.wait_ge(centred, ONE + i + 1)
                nc.scalar.activation(ex[:, :, :], ex[:, :, :], ACT.Exp).then_inc(ex_ready, 1)
                act.wait_ge(slotT_done, ONE + i + 1)
                nc.scalar.activation(slotT[:, :, bass.ts(i, 1), :].rearrange("p z o t -> p z (o t)"),
                                     ps[:, 0, 0:3 * P].rearrange("p (z t) -> p z t", z=3), ACT.Copy).then_inc(slotT_ready, 1)

        @block.tensor
        def _(pe):
            with pe.Fori(0, NT) as i:
                pe.wait_ge(slot_ready, ONE + i + 1)
                pe.wait_ge(slotT_ready, ONE + i)
                for z in range(3):
                    last = nc.tensor.transpose(ps[:, 0, z * P:(z + 1) * P], slot[:, z, :], core.ident[:, :])
                last.then_inc(slotT_done, 1)


def spread_gates(core, slotT):
    nc, ps = core.nc, core.ps
    TU = BANK // NKEY
    UB = 4
    PASSES = P // (TU * UB)
    with ExitStack() as ctx:
        sb, sem = core.scope(ctx)
        gates = sb("gates", [P, 2, NKEY, P])
        first = sb("first", [P, 2, TU, NKEY])
        second = sb("second", [P, 2, TU, NKEY])
        iota = sb("iota_g", [P, NKEY])
        iota_in = sem("iota_in_g")
        first_ready, spread_done, gates_out = sem("first_ready"), sem("spread_done"), sem("gates_out")
        gates_sent = [sem(f"gates_sent{k}") for k in range(2)]
        open_counts(nc, (first_ready, gates_out, *gates_sent, spread_done))
        block = ctx.enter_context(nc.Block())
        UNITS = P // TU

        @block.sync
        def _(sp):
            sp.dma_start(iota[:, :], core.i["c_iota"]).then_inc(iota_in, 16)
            dst = core.scr_g.rearrange("j i t -> i j t")
            with sp.Fori(0, NT // 2) as it:
                for k in range(2):
                    sp.wait_ge(gates_out, ONE + it * (2 * UNITS) + (k + 1) * UNITS)
                    sp.dma_start(dst[:, :, bass.ts(it * 2 + k, P)], gates[:, k, :, :]).then_inc(gates_sent[k], 16)
            sp.wait_ge(iota_in, 16)
            for k in range(2):
                sp.wait_ge(gates_sent[k], ONE + 16 * NT // 2)

        @block.vector
        def _(dve):
            dve.wait_ge(iota_in, 16)
            dve.sem_inc(spread_done, 2)
            with dve.Fori(0, NT * PASSES) as it:
                for u in range(UB):
                    b = u % 2
                    dve.wait_ge(spread_done, ONE + it * UB + u + 1)
                    for s in range(TU):
                        t = bass.ds(it * (UB * TU) + (u * TU + s), 1)
                        flat = slotT[:, :, :, :].rearrange("p z i t -> p z (i t)")
                        nc.vector.tensor_scalar(first[:, b, s, :], iota[:, :], flat[:, 0, t], flat[:, 2, t],
                                                ALU.is_equal, ALU.mult)
                        last = nc.vector.tensor_scalar(second[:, b, s, :], iota[:, :], flat[:, 1, t], None, ALU.is_equal)
                    last.then_inc(first_ready, 1)

        @block.tensor
        def _(pe):
            with pe.Fori(0, NT * PASSES) as it:
                for u in range(UB):
                    pe.wait_ge(first_ready, ONE + it * UB + u + 1)
                    pe.wait_ge(gates_out, ONE + (it * UB + u + 1 - UB if u == UB - 1 else it * UB))
                    for s in range(TU):
                        last = nc.tensor.matmul(ps[:, u, s * NKEY:(s + 1) * NKEY], first[:, u % 2, s, :],
                                                second[:, u % 2, s, :], start=True, stop=True)
                    last.then_inc(spread_done, 1)

        @block.scalar
        def _(act):
            with act.Fori(0, NT // 2) as it:
                for k in range(2):
                    act.wait_ge(gates_sent[k], ONE + it * 16)
                    with act.Fori(0, PASSES) as q:
                        for u in range(UB):
                            n = it * (2 * UNITS) + (q * UB + (k * UNITS + u))
                            act.wait_ge(spread_done, ONE + n + (2 + 1))
                            nc.scalar.activation(
                                gates[:, k, :, bass.ds(q * (UB * TU) + u * TU, TU)].rearrange("p i t -> p t i"),
                                ps[:, u, :].rearrange("p (t i) -> p t i", t=TU), ACT.Copy).then_inc(gates_out, 1)


def run_experts(core, hn_hi, hn_lo, hn_in):
    nc, ps, res = core.nc, core.ps, core.res
    CH = 2
    NG = NKEY // CH
    FILLS = NT * 2
    with ExitStack() as ctx:
        sb, sem = core.scope(ctx)
        u = sb("u", [P, CH, D])
        v = sb("v", [P, CH, D])
        gate = sb("gate", [P, CH, SEQ])
        uT_hi, uT_lo = sb("uT_hi", [P, CH, KD, P], f32r), sb("uT_lo", [P, CH, KD, P], f32r)
        v_hi, v_lo = sb("v_hi", [P, CH, D], f32r), sb("v_lo", [P, CH, D], f32r)
        w = sb("w", [P, CH, SEQ])
        w_hi, w_lo = sb("w_hi2", [P, 2, CH, SEQ], f32r), sb("w_lo2", [P, 2, CH, SEQ], f32r)
        u_in = [sem(f"u_in{c}") for c in range(CH)]
        gate_in = [sem(f"gate_in{c}") for c in range(CH)]
        v_in = sem("v_in")
        uT_done, uT_hi_ready, uT_lo_ready = sem("uT_done"), sem("uT_hi_ready"), sem("uT_lo_ready")
        act_done, gelu_ready, w_ready, w_hi_ready, w_lo_ready = (sem(x) for x in (
            "act_done", "gelu_ready", "w_ready", "w_hi_ready", "w_lo_ready"))
        v_hi_ready, v_lo_ready, out_done, added = (sem(x) for x in ("v_hi_ready", "v_lo_ready", "out_done", "added"))
        open_counts(nc, (act_done, added, *gate_in, gelu_ready, out_done, uT_done, uT_hi_ready, uT_lo_ready, *u_in,
                         v_hi_ready, v_in, v_lo_ready, w_hi_ready, w_lo_ready, w_ready))
        block = ctx.enter_context(nc.Block())

        u_v = core.i["u_emb"].rearrange("l (i j) d -> j i (l d)", j=NKEY)
        v_v = core.i["v_emb"].rearrange("l (i j) d -> j i (l d)", j=NKEY)

        def need(eng, sem_, value):
            if not isinstance(value, int) or value > 0:
                eng.wait_ge(sem_, ONE + value)

        def at(ap, n):
            return ap[n] if isinstance(n, int) else ap[bass.ds(n, 1), :, :].rearrange("o p d -> p (o d)")

        def schedule(group=lambda g, b, last: None, out=lambda g, b: None, values=lambda g: None, eng=None):
            group(0, 0, False)
            values(0)
            with eng.Fori(0, NG // 2 - 1) as it:
                group(it * 2 + 1, 1, False)
                out(it * 2, 0)
                values(it * 2 + 1)
                group(it * 2 + 2, 0, False)
                out(it * 2 + 1, 1)
                values(it * 2 + 2)
            group(NG - 1, 1, True)
            out(NG - 2, 0)
            values(NG - 1)
            out(NG - 1, 1)

        @block.sync
        def _(sp):
            def load(g, b, last):
                for c in range(CH):
                    need(sp, uT_done, g * CH + c - 1)
                    sp.dma_start(u[:, c, :], at(u_v, g * CH + c)).then_inc(u_in[c], 16)
                for c in range(CH):
                    need(sp, w_ready, g * CH + c - 1)
                    sp.dma_start(gate[:, c, :], at(core.scr_g, g * CH + c)).then_inc(gate_in[c], 16)
                need(sp, v_hi_ready, g)
                need(sp, v_lo_ready, g)
                for c in range(CH):
                    sp.dma_start(v[:, c, :], at(v_v, g * CH + c)).then_inc(v_in, 16)

            schedule(load, eng=sp)

        @block.tensor
        def _(pe):
            def turn(g, c):
                n = g * CH + c
                pe.wait_ge(u_in[c], ONE + g * 16 + 16)
                need(pe, uT_hi_ready, n)
                need(pe, uT_lo_ready, n)
                for j in range(KD):
                    last = nc.tensor.transpose(ps[:, 4 + j // 4, (j % 4) * P:(j % 4 + 1) * P],
                                               u[:, c, j * P:(j + 1) * P], core.ident[:, :])
                last.then_inc(uT_done, 1)

            def activations(g, b, last_group):
                for c in range(CH):
                    n = g * CH + c
                    if not (last_group and c == CH - 1):
                        turn(g + (c + 1) // CH, (c + 1) % CH)
                    pe.wait_ge(uT_hi_ready, ONE + n + 1)
                    pe.wait_ge(uT_lo_ready, ONE + n + 1)
                    need(pe, gelu_ready, n - 1)
                    for half in range(2):
                        ts = slice(half * BANK, (half + 1) * BANK)
                        terms = [(x, y, j) for j in range(KD) for x, y in ((uT_hi, hn_hi), (uT_hi, hn_lo), (uT_lo, hn_hi))]
                        for m, (x, y, j) in enumerate(terms):
                            last = nc.tensor.matmul(ps[:, 2 * c + half, :], x[:, c, j, :], y[:, j, ts],
                                                    start=m == 0, stop=m == len(terms) - 1)
                    last.then_inc(act_done, 1)

            def out(g, b):
                pe.wait_ge(w_hi_ready, ONE + g * CH + CH)
                pe.wait_ge(w_lo_ready, ONE + g * CH + CH)
                pe.wait_ge(v_hi_ready, ONE + g + 1)
                pe.wait_ge(v_lo_ready, ONE + g + 1)
                for i in range(NT):
                    for half in range(2):
                        f = i * 2 + half
                        need(pe, added, g * FILLS + (f - 1 if f else 0))
                        terms = [(x, y, c) for c in range(CH) for x, y in ((w_hi, v_hi), (w_hi, v_lo), (w_lo, v_hi))]
                        for m, (x, y, c) in enumerate(terms):
                            last = nc.tensor.matmul(ps[:, 6 + half, :], x[:, b, c, i * P:(i + 1) * P],
                                                    y[:, c, half * BANK:(half + 1) * BANK],
                                                    start=m == 0, stop=m == len(terms) - 1)
                        last.then_inc(out_done, 1)

            turn(0, 0)
            pe.wait_ge(hn_in, 32)
            schedule(activations, out, eng=pe)

        @block.scalar
        def _(act):
            def copy_uT(g, c):
                n = g * CH + c
                act.wait_ge(uT_done, ONE + n + 1)
                need(act, act_done, n - 1)
                nc.scalar.activation(uT_hi[:, c, :, :], ps[:, 4:6, :].rearrange("p b (j e) -> p (b j) e", e=P),
                                     ACT.Copy).then_inc(uT_hi_ready, 1)

            def group(g, b, last_group):
                for c in range(CH):
                    n = g * CH + c
                    if not (last_group and c == CH - 1):
                        copy_uT(g + (c + 1) // CH, (c + 1) % CH)
                    act.wait_ge(act_done, ONE + n + 1)
                    need(act, w_lo_ready, n - 1)
                    need(act, w_hi_ready, n - 1)
                    nc.scalar.activation(w[:, c, :], ps[:, 2 * c:2 * c + 2, :].rearrange("p b t -> p (b t)"),
                                         ACT.Gelu).then_inc(gelu_ready, 1)
                for c in range(CH):
                    n = g * CH + c
                    act.wait_ge(w_ready, ONE + n + 1)
                    need(act, out_done, (g - 1) * FILLS)
                    nc.scalar.activation(w_hi[:, b, c, :], w[:, c, :], ACT.Copy).then_inc(w_hi_ready, 1)

            def values(g):
                act.wait_ge(v_in, ONE + g * (16 * CH) + 16 * CH)
                need(act, out_done, g * FILLS)
                nc.scalar.activation(v_hi[:, :, :], v[:, :, :], ACT.Copy).then_inc(v_hi_ready, 1)

            copy_uT(0, 0)
            schedule(group, values=values, eng=act)

        @block.vector
        def _(dve):
            def split_uT(g, c):
                n = g * CH + c
                dve.wait_ge(uT_hi_ready, ONE + n + 1)
                need(dve, act_done, n - 1)
                nc.vector.tensor_tensor(uT_lo[:, c, :, :], ps[:, 4:6, :].rearrange("p b (j e) -> p (b j) e", e=P),
                                        uT_hi[:, c, :, :].bitcast(f32), ALU.subtract).then_inc(uT_lo_ready, 1)

            def group(g, b, last_group):
                for c in range(CH):
                    n = g * CH + c
                    if not (last_group and c == CH - 1):
                        split_uT(g + (c + 1) // CH, (c + 1) % CH)
                    dve.wait_ge(gate_in[c], ONE + g * 16 + 16)
                    dve.wait_ge(gelu_ready, ONE + n + 1)
                    nc.vector.tensor_tensor(w[:, c, :], w[:, c, :], gate[:, c, :], ALU.mult).then_inc(w_ready, 1)
                for c in range(CH):
                    n = g * CH + c
                    dve.wait_ge(w_hi_ready, ONE + n + 1)
                    need(dve, out_done, (g - 1) * FILLS)
                    nc.vector.tensor_tensor(w_lo[:, b, c, :], w[:, c, :], w_hi[:, b, c, :].bitcast(f32), ALU.subtract
                                            ).then_inc(w_lo_ready, 1)

            def out(g, b):
                for i in range(NT):
                    for half in range(2):
                        dve.wait_ge(out_done, ONE + g * FILLS + (i * 2 + half + 1))
                        r = res[:, i, half * BANK:(half + 1) * BANK]
                        nc.vector.tensor_tensor(r, ps[:, 6 + half, :], r, ALU.add).then_inc(added, 1)

            def values(g):
                dve.wait_ge(v_hi_ready, ONE + g + 1)
                nc.vector.tensor_tensor(v_lo[:, :, :], v[:, :, :], v_hi[:, :, :].bitcast(f32), ALU.subtract
                                        ).then_inc(v_lo_ready, 1)

            split_uT(0, 0)
            schedule(group, out, values, eng=dve)
            dve.wait_ge(added, ONE + NG * FILLS)


def finish(core):
    nc, res = core.nc, core.res
    with ExitStack() as ctx:
        sb, sem = core.scope(ctx)
        g = sb("g_final", [P, D])
        junk = sb("junk_f", [P, D])
        ss, rstd = sb("ss_f", [P, NT]), sb("rstd_f", [P, NT])
        g_in, ss_ready, ms_ready, rms_ready, y_ready, sent = (sem(x) for x in (
            "g_in", "ss_ready_f", "ms_ready_f", "rms_ready_f", "y_ready_f", "sent_f"))
        own_a, own_v = sem("act_own_f"), sem("dve_own_f")
        block = ctx.enter_context(nc.Block())

        @block.sync
        def _(sp):
            sp.dma_start(g[:, :], core.i["g_final"].rearrange("(o d) -> o d", o=1).to_broadcast([P, D])).then_inc(g_in, 16)
            o = core.out.rearrange("b (i p) d -> p (b i) d", p=P)
            for i in range(NT):
                sp.wait_ge(y_ready, i + 1)
                sp.dma_start(o[:, i, :], res[:, i, :]).then_inc(sent, 16)
            sp.wait_ge(sent, 16 * NT)

        @block.scalar
        def _(act):
            own = Own(act, own_a)
            for i in range(NT):
                if i:
                    own.sync()
                own.mark(nc.scalar.activation(junk[:, :], res[:, i, :], ACT.Square, accum_out=ss[:, i:i + 1]))
            own.sync()
            act.sem_inc(ss_ready, 1)
            act.wait_ge(ms_ready, 1)
            nc.scalar.activation(rstd[:, :], ss[:, :], ACT.Sqrt).then_inc(rms_ready, 1)

        @block.vector
        def _(dve):
            own = Own(dve, own_v)
            dve.wait_ge(ss_ready, 1)
            own.link(nc.vector.tensor_scalar(ss[:, :], ss[:, :], 1.0 / D, EPS, ALU.mult, ALU.add))
            dve.sem_inc(ms_ready, 1)
            dve.wait_ge(rms_ready, 1)
            own.link(nc.vector.reciprocal(rstd[:, :], rstd[:, :]))
            dve.wait_ge(g_in, 16)
            for i in range(NT):
                nc.vector.scalar_tensor_tensor(out=res[:, i, :], in0=res[:, i, :], scalar=rstd[:, i:i + 1],
                                               in1=g[:, :], op0=ALU.mult, op1=ALU.mult).then_inc(y_ready, 1)


@contextmanager
def load_hidden(core, name):
    with ExitStack() as ctx:
        sb, sem = core.scope(ctx)
        hn_hi, hn_lo = sb("hn_hi_" + name, [P, KD, SEQ], f32r), sb("hn_lo_" + name, [P, KD, SEQ], f32r)
        hn_in = sem("hn_in_" + name)
        with core.nc.Block() as block:
            @block.sync
            def _(sp):
                sp.dma_start(hn_hi[:, :, :].bitcast(f32), core.scr_hi).then_inc(hn_in, 16)
                sp.dma_start(hn_lo[:, :, :].bitcast(f32), core.scr_lo).then_inc(hn_in, 16)
        yield hn_hi, hn_lo, hn_in


def layer(nc, ins, out):
    with ExitStack() as ctx:
        core = Core(nc, ctx, ins, out)
        project_in(core)
        with ExitStack() as mid:
            sb, sem = core.scope(mid)
            mix = sb("mix", [P, NT, D])
            w_out = sb("w_out", [P, KD, D])
            w_out_in = sem("w_out_in")
            with ExitStack() as att:
                mask = att.enter_context(nc.sbuf_tensor("mask", [P, 2, SEQ], f32))
                with nc.semaphore("mask_in") as mask_in, nc.Block() as block:
                    @block.sync
                    def _(sp):
                        sp.dma_start(mask[:, :, :], core.i["c_mask"]).then_inc(mask_in, 16)
                        sp.dma_start(w_out[:, :, :], core.i["w_out"].rearrange("l (k p) n -> p (l k) n", p=P)
                                     ).then_inc(w_out_in, 16)
                        sp.wait_ge(mask_in, 16)
                attend(core, mix, mask[:, 0, :], "a", HA, EA, core.scr_a, 0, WA, 2 * WA, 0)
                attend(core, mix, mask[:, 1, :], "m", HM, EM, core.scr_m, MQ, MK, MV, WA)
            project_out(core, mix, w_out, w_out_in)
        with ExitStack() as peer:
            slotT = peer.enter_context(nc.sbuf_tensor("slotT", [P, 3, NT, P], f32))
            with ExitStack() as mid:
                sb, sem = core.scope(mid)
                vals = sb("vals", [P, PH, 2, NT, TOPK])
                idxf = sb("idxf", [P, PH, 2, NT, TOPK])
                with load_hidden(core, "r") as hidden:
                    rank_keys(core, *hidden, vals, idxf)
                pick_experts(core, vals, idxf, slotT)
            spread_gates(core, slotT)
        with load_hidden(core, "e") as hidden:
            run_experts(core, *hidden)
        finish(core)


NAMES = ["x", "positions", "g_mix", "w_in", "g_cq", "w_uq", "g_ckv", "w_ukv", "w_out", "g_ffn",
         "w_pq", "sub_keys", "u_emb", "v_emb", "g_final"]


def constants(np):
    half = NF
    freq = np.float32(500000.0) ** (-np.arange(half, dtype=np.float32) / np.float32(half))
    dist = (SEQ - P) + np.arange(P)[:, None] - np.arange(SEQ)[None, :]
    count = ((dist >= 0) & (dist <= 128)).astype(np.int64)
    count += (dist >= 0) & (dist <= 512) & (dist % 4 == 0)
    count += (dist >= 0) & (dist <= 2048) & (dist % 16 == 0)
    mask = np.full((P, 2, SEQ), BIG, np.float32)
    mask[:, 0] = np.where(count > 0, -np.log(np.maximum(count, 1)), BIG)
    mask[:, 1] = np.where(dist >= 0, 0.0, BIG)
    return {
        "c_freq": np.broadcast_to(freq, (P, half)).copy(),
        "c_ident": np.eye(P, dtype=np.float32),
        "c_mask": mask,
        "c_iota": np.broadcast_to(np.arange(P, dtype=np.float32), (P, P)).copy(),
    }


def kernel(**inputs):
    import numpy as np
    import concourse.bacc as bacc
    from concourse.bass_utils import run_bass_kernel_spmd

    nc = bacc.Bacc("TRN2", target_bir_lowering=False, num_devices=1)
    arrays = {"in_" + n: np.ascontiguousarray(inputs[n]) for n in NAMES}
    arrays.update(constants(np))
    ins = {n.removeprefix("in_"): nc.dram_tensor(n, a.shape, mybir.dt.from_np(a.dtype), kind="ExternalInput").ap()
           for n, a in arrays.items()}
    out = nc.dram_tensor("out", (1, SEQ, D), f32, kind="ExternalOutput").ap()
    layer(nc, ins, out)
    r = run_bass_kernel_spmd(nc, [arrays], core_ids=[0])
    return r.results[0]["out"]
```

```python
from contextlib import ExitStack

import concourse.bass as bass
from concourse import mybir

P = 128
SEQ = 1024
D = 1024
NT = SEQ // P
KD = D // P
BANK = 512

HA, EA, ROT_A = 8, 64, 16
HM, NOPE, ROPE, VM = 8, 64, 32, 64
EM = NOPE + ROPE
QR, KR = 256, 128
WA = HA * EA
IN_W = 3 * WA + QR + KR + ROPE
UQ_W = HM * EM
UKV_W = HM * (NOPE + VM)
C_AT = 3 * WA
KV_AT = C_AT + QR
KR_AT = KV_AT + KR
MQ, MK, MV = 0, HM * EM, 2 * HM * EM
SM_W = 2 * HM * EM + HM * VM
NF = ROPE // 2
EPS = 1e-6

PH, NKEY, PQ, TOPK = 8, 128, 256, 16
HALFQ = PQ // 2
RUN = [TOPK // (a + 1) for a in range(TOPK)]
RUN_AT = [sum(RUN[:a]) for a in range(TOPK)]
NC_ = sum(RUN)
NEXP = NKEY * NKEY

TWO_PI_HI = 6.28125
TWO_PI_LO = 1.9353071795864769e-3
ROUND = 12582912.0
BIG = 1e30
ONE = 1
LOWEST = -3.0e38

f32 = mybir.dt.float32
f32r = mybir.dt.float32r
bf16 = mybir.dt.bfloat16
i32 = mybir.dt.int32
u32 = mybir.dt.uint32
ALU = mybir.AluOpType
ACT = mybir.ActivationFunctionType
AX = mybir.AxisListType.X


class Own:

    def __init__(self, eng, sem):
        self.eng, self.sem, self.n = eng, sem, 0

    def mark(self, ins):
        ins.then_inc(self.sem, 1)
        self.n += 1
        return self.n

    def link(self, ins):
        self.mark(ins)
        self.eng.wait_ge(self.sem, self.n)

    def sync(self):
        self.eng.wait_ge(self.sem, self.n)

    def restart(self):
        if self.n:
            self.eng.wait_ge(self.sem, self.n)
            self.eng.sem_clear(self.sem)
        self.n = 0


def open_counts(nc, sems):
    with nc.Block() as block:
        @block.sync
        def _(sp):
            for s in sems:
                sp.sem_inc(s, ONE)


class Core:

    def __init__(self, nc, ctx, ins, out):
        self.nc, self.i, self.out = nc, ins, out
        self.sb = lambda name, shape, dt=f32, c=ctx: c.enter_context(nc.sbuf_tensor(name, shape, dt))
        self.ps = ctx.enter_context(nc.psum_tensor("psum", [P, 8, BANK], f32))
        self.res = self.sb("res", [P, NT, D])
        self.ident = self.sb("ident", [P, P])
        self.g_ffn = self.sb("g_ffn_col", [P, KD])
        dram = lambda name, shape: nc.dram_tensor(name, shape, f32, kind="Internal").ap()
        self.scr_a = dram("scr_a", [SEQ, C_AT])
        self.scr_m = dram("scr_m", [SEQ, SM_W])
        self.scr_hi = dram("scr_hi", [P, KD, SEQ])
        self.scr_lo = dram("scr_lo", [P, KD, SEQ])
        self.scr_g = dram("scr_g", [NKEY, NKEY, SEQ])

    def scope(self, ctx):
        sb = lambda name, shape, dt=f32: ctx.enter_context(self.nc.sbuf_tensor(name, shape, dt))
        sem = lambda name: ctx.enter_context(self.nc.semaphore(name))
        return sb, sem


def column(v, n):
    return v.rearrange("(k p) -> p k", p=P)


def project_in(core):
    nc, ps, res = core.nc, core.ps, core.res
    I = core.i
    with ExitStack() as ctx:
        sb, sem = core.scope(ctx)
        w_in = sb("w_in", [P, KD, IN_W])
        w_uq = sb("w_uq", [P, 2, UQ_W])
        w_ukv = sb("w_ukv", [P, UKV_W])
        g_mix = sb("g_mix", [P, KD])
        g_c = sb("g_c", [P, 3])
        pos_i = sb("pos_i", [P, NT], i32)
        pos = sb("pos", [P, NT])
        freq = sb("freq", [P, NF])
        ang = sb("ang", [P, NT, NF])
        turn = sb("turn", [P, NT, NF])
        trig = sb("trig", [P, 2, NT, NF])
        ss = sb("ss", [P, NT])
        rstd = sb("rstd", [P, NT])
        junk = sb("junk", [P, D])
        xn = sb("xn", [P, 2, D])
        hT = sb("hT", [P, 2, KD, P])
        st_a = sb("st_a", [P, 2, IN_W])
        st_m = sb("st_m", [P, 2, SM_W])
        ssc = sb("ssc", [P, 2, 2])
        rstc = sb("rstc", [P, 2, 2])
        cn = sb("cn", [P, 2, QR + KR])
        cT = sb("cT", [P, 2, 3, P])
        rt = sb("rt", [P, 4, 2 * HA, NF])

        x_in = [sem(f"x_in{n}") for n in range(NT // 2)]
        w_in_in = [sem(f"w_in_in{n}") for n in range(4)]
        small_in, wc_in = sem("small_in"), sem("wc_in")
        act_own, dve_own = sem("act_own"), sem("dve_own")
        ss_ready, ms_ready, rms_ready = sem("ss_ready"), sem("ms_ready"), sem("rms_ready")
        ang_ready, trig_ready = sem("ang_ready"), sem("trig_ready")
        xn_ready, xT_done, hT_ready = sem("xn_ready"), sem("xT_done"), sem("hT_ready")
        chunk_done, chunk_out = sem("chunk_done"), sem("chunk_out")
        css_ready, cms_ready, crms_ready = sem("css_ready"), sem("cms_ready"), sem("crms_ready")
        cn_ready, cnT_done, cT_ready = sem("cn_ready"), sem("cnT_done"), sem("cT_ready")
        a_roped, m_roped = sem("a_roped"), sem("m_roped")
        a_sent = [sem(f"a_sent{k}") for k in range(2)]
        m_sent = [sem(f"m_sent{k}") for k in range(2)]
        SLOTS = 4
        PER = 16

        def width(c):
            return min(BANK, IN_W - c * BANK)

        x_v = I["x"].rearrange("b (i p) d -> p (b i) d", p=P)
        w_v = I["w_in"].rearrange("l (k p) n -> p (l k) n", p=P)
        open_counts(nc, (a_roped, *a_sent, cT_ready, chunk_done, chunk_out, cms_ready, cnT_done, cn_ready, crms_ready,
                         css_ready, hT_ready, m_roped, *m_sent, xT_done, xn_ready))
        block = ctx.enter_context(nc.Block())

        @block.sync
        def _(sp):
            for n in range(NT // 2):
                sp.dma_start(res[:, 2 * n:2 * n + 2, :], x_v[:, 2 * n:2 * n + 2, :]).then_inc(x_in[n], 16)
                if n == 0:
                    for c in range(2):
                        sp.dma_start(w_in[:, :, c * BANK:c * BANK + width(c)],
                                     w_v[:, :, c * BANK:c * BANK + width(c)]).then_inc(w_in_in[c], 16)
            for c in range(2, 4):
                sp.dma_start(w_in[:, :, c * BANK:c * BANK + width(c)],
                             w_v[:, :, c * BANK:c * BANK + width(c)]).then_inc(w_in_in[c], 16)
            sp.dma_start(w_uq[:, :, :], I["w_uq"].rearrange("l (k p) n -> p (l k) n", p=P)).then_inc(wc_in, 16)
            sp.dma_start(w_ukv[:, :], I["w_ukv"].rearrange("l p n -> p (l n)")).then_inc(wc_in, 16)
            with sp.Fori(0, NT // 2) as it:
                for k in range(2):
                    sp.wait_ge(a_roped, ONE + it * 2 + k + 1)
                    sp.dma_start(core.scr_a.rearrange("(i p) n -> i p n", p=P)[it * 2 + k],
                                 st_a[:, k, 0:C_AT]).then_inc(a_sent[k], 16)
                for k in range(2):
                    sp.wait_ge(m_roped, ONE + it * 2 + k + 1)
                    sp.dma_start(core.scr_m.rearrange("(i p) n -> i p n", p=P)[it * 2 + k],
                                 st_m[:, k, :]).then_inc(m_sent[k], 16)
            for k in range(2):
                sp.wait_ge(a_sent[k], ONE + 16 * NT // 2)
                sp.wait_ge(m_sent[k], ONE + 16 * NT // 2)

        @block.scalar
        def _(act):
            own = Own(act, act_own)
            with nc.allow_non_contiguous_dma(reason="gains and positions as columns"):
                act.dma_start(pos_i[:, :], I["positions"].rearrange("b (i p) -> p (b i)", p=P)).then_inc(small_in, 16)
                act.dma_start(g_mix[:, :], column(I["g_mix"][0], KD)).then_inc(small_in, 16)
                act.dma_start(core.g_ffn[:, :], column(I["g_ffn"][0], KD)).then_inc(small_in, 16)
                act.dma_start(g_c[:, 0:2], column(I["g_cq"][0], 2)).then_inc(small_in, 16)
                act.dma_start(g_c[:, 2:3], column(I["g_ckv"][0], 1)).then_inc(small_in, 16)
            act.dma_start(freq[:, :], I["c_freq"]).then_inc(small_in, 16)
            act.dma_start(core.ident[:, :], I["c_ident"]).then_inc(small_in, 16)
            for i in range(NT):
                act.wait_ge(x_in[i // 2], 16)
                if i:
                    own.sync()
                own.mark(nc.scalar.activation(junk[:, :], res[:, i, :], ACT.Square, accum_out=ss[:, i:i + 1]))
            own.sync()
            act.sem_inc(ss_ready, 1)
            act.wait_ge(ms_ready, 1)
            nc.scalar.activation(rstd[:, :], ss[:, :], ACT.Sqrt).then_inc(rms_ready, 1)
            act.wait_ge(ang_ready, 1)
            nc.scalar.activation(trig[:, :, :, :], trig[:, :, :, :], ACT.Sin).then_inc(trig_ready, 1)
            own.restart()
            with act.Fori(0, NT // 2) as it:
                for k in range(2):
                    act.wait_ge(a_sent[k], ONE + it * 16)
                    for c in range(4):
                        act.wait_ge(chunk_done, ONE + it * PER + k * 4 + c + 1)
                        own.mark(nc.scalar.activation(st_a[:, k, c * BANK:c * BANK + width(c)],
                                                      ps[:, 2 + c, 0:width(c)], ACT.Copy))
                        own.sync()
                        act.sem_inc(chunk_out, 1)
                    own.mark(nc.scalar.activation(junk[:, 0:QR], st_a[:, k, C_AT:KV_AT], ACT.Square,
                                                  accum_out=ssc[:, k, 0:1]))
                    own.mark(nc.scalar.activation(junk[:, QR:QR + KR], st_a[:, k, KV_AT:KR_AT], ACT.Square,
                                                  accum_out=ssc[:, k, 1:2]))
                    own.sync()
                    act.sem_inc(css_ready, 1)
                for k in range(2):
                    act.wait_ge(cms_ready, ONE + it * 2 + k + 1)
                    nc.scalar.activation(rstc[:, k, :], ssc[:, k, :], ACT.Sqrt).then_inc(crms_ready, 1)
                for k in range(2):
                    act.wait_ge(m_sent[k], ONE + it * 16)
                    mk = st_m[:, k, MK:MV].rearrange("p (h e) -> p h e", h=HM)
                    mv = st_m[:, k, MV:SM_W].rearrange("p (h e) -> p h e", h=HM)
                    for c in range(4):
                        act.wait_ge(chunk_done, ONE + it * PER + 8 + k * 4 + c + 1)
                        if c < 2:
                            n = min(BANK, UQ_W - c * BANK)
                            own.mark(nc.scalar.activation(st_m[:, k, c * BANK:c * BANK + n], ps[:, 2 + c, 0:n],
                                                          ACT.Copy))
                        else:
                            hs = slice((c - 2) * 4, (c - 2) * 4 + 4)
                            kv = ps[:, 2 + c, :].rearrange("p (h e) -> p h e", h=4)
                            own.mark(nc.scalar.activation(mk[:, hs, 0:NOPE], kv[:, :, 0:NOPE], ACT.Copy))
                            own.mark(nc.scalar.activation(mv[:, hs, :], kv[:, :, NOPE:], ACT.Copy))
                        own.sync()
                        act.sem_inc(chunk_out, 1)
                own.restart()

        @block.vector
        def _(dve):
            own = Own(dve, dve_own)
            dve.wait_ge(small_in, 16 * 7)
            own.link(nc.vector.tensor_copy(pos[:, :], pos_i[:, :]))
            own.link(nc.vector.tensor_tensor(
                ang[:, :, :], pos[:, :].rearrange("p (i o) -> p i o", o=1).to_broadcast([P, NT, NF]),
                freq[:, :].rearrange("p (o f) -> p o f", o=1).to_broadcast([P, NT, NF]), ALU.mult))
            for s, quarter in ((0, 0.25), (1, 0.0)):
                r = trig[:, s, :, :]
                own.link(nc.vector.tensor_scalar(turn[:, :, :], ang[:, :, :], 0.15915494309189535, quarter,
                                                 ALU.mult, ALU.add))
                own.link(nc.vector.tensor_scalar_add(turn[:, :, :], turn[:, :, :], ROUND))
                own.link(nc.vector.tensor_scalar_add(turn[:, :, :], turn[:, :, :], -ROUND))
                own.link(nc.vector.scalar_tensor_tensor(out=r, in0=turn[:, :, :], scalar=-TWO_PI_HI,
                                                        in1=ang[:, :, :], op0=ALU.mult, op1=ALU.add))
                own.link(nc.vector.scalar_tensor_tensor(out=r, in0=turn[:, :, :], scalar=-TWO_PI_LO,
                                                        in1=r, op0=ALU.mult, op1=ALU.add))
                own.link(nc.vector.tensor_scalar(r, r, 2 * 3.14159265358979 * quarter, 3.1415925,
                                                 ALU.add, ALU.min))
                own.link(nc.vector.tensor_scalar(r, r, -3.1415925, None, ALU.max))
            dve.sem_inc(ang_ready, 1)
            dve.wait_ge(ss_ready, 1)
            own.link(nc.vector.tensor_scalar(ss[:, :], ss[:, :], 1.0 / D, EPS, ALU.mult, ALU.add))
            dve.sem_inc(ms_ready, 1)
            dve.wait_ge(rms_ready, 1)
            own.link(nc.vector.reciprocal(rstd[:, :], rstd[:, :]))
            dve.sem_inc(chunk_out, SLOTS)
            dve.wait_ge(trig_ready, 1)
            own.restart()

            def rotate(k, i, x1, x2, heads, step, o1=None, o2=None, copies=1):
                n = NF // step
                c, s = (trig[:, z, bass.ts(i, 1), :].rearrange("p o f -> p (o f)")[:, 0:NF:step]
                        .rearrange("p (o f) -> p o f", o=1).to_broadcast([P, heads, n]) for z in range(2))
                t = [rt[:, z, 0:heads, 0:n] for z in range(4)]
                own.mark(nc.vector.tensor_tensor(t[0], x1, c, ALU.mult))
                own.mark(nc.vector.tensor_tensor(t[1], x2, s, ALU.mult))
                own.mark(nc.vector.tensor_tensor(t[2], x2, c, ALU.mult))
                own.mark(nc.vector.tensor_tensor(t[3], x1, s, ALU.mult))
                own.sync()
                if copies > 1:
                    t = [u.to_broadcast([P, copies, n]) for u in t]
                own.mark(nc.vector.tensor_tensor(x1 if o1 is None else o1, t[0], t[1], ALU.subtract))
                own.mark(nc.vector.tensor_tensor(x2 if o2 is None else o2, t[2], t[3], ALU.add))
                own.sync()

            with dve.Fori(0, NT // 2) as it:
                for k in range(2):
                    dve.wait_ge(xT_done, ONE + it * 2)
                    nc.vector.tensor_scalar(xn[:, k, :], res[:, bass.ts(it * 2 + k, 1), :].rearrange("p o d -> p (o d)"),
                                            rstd[:, bass.ts(it * 2 + k, 1)], None, ALU.mult).then_inc(xn_ready, 1)
                for k in range(2):
                    dve.wait_ge(xT_done, ONE + it * 2 + k + 1)
                    nc.vector.tensor_tensor(
                        hT[:, k, :, :], ps[:, 0:2, :].rearrange("p b (j t) -> p (b j) t", t=P),
                        g_mix[:, :].rearrange("p (j o) -> p j o", o=1).to_broadcast([P, KD, P]),
                        ALU.mult).then_inc(hT_ready, 1)
                for k in range(2):
                    dve.wait_ge(css_ready, ONE + it * 2 + k + 1)
                    own.mark(nc.vector.tensor_scalar(ssc[:, k, 0:1], ssc[:, k, 0:1], 1.0 / QR, EPS, ALU.mult, ALU.add))
                    own.mark(nc.vector.tensor_scalar(ssc[:, k, 1:2], ssc[:, k, 1:2], 1.0 / KR, EPS, ALU.mult, ALU.add))
                    own.sync()
                    dve.sem_inc(cms_ready, 1)
                    qk = st_a[:, k, 0:2 * WA].rearrange("p (h e) -> p h e", e=EA)
                    rotate(k, it * 2 + k, qk[:, :, 0:ROT_A // 2], qk[:, :, ROT_A // 2:ROT_A], 2 * HA, 2)
                    dve.sem_inc(a_roped, 1)
                for k in range(2):
                    dve.wait_ge(crms_ready, ONE + it * 2 + k + 1)
                    own.link(nc.vector.reciprocal(rstc[:, k, :], rstc[:, k, :]))
                    own.mark(nc.vector.tensor_scalar(cn[:, k, 0:QR], st_a[:, k, C_AT:KV_AT], rstc[:, k, 0:1], None, ALU.mult))
                    own.mark(nc.vector.tensor_scalar(cn[:, k, QR:], st_a[:, k, KV_AT:KR_AT], rstc[:, k, 1:2], None, ALU.mult))
                    own.sync()
                    dve.sem_inc(cn_ready, 1)
                for k in range(2):
                    dve.wait_ge(cnT_done, ONE + it * 2 + k + 1)
                    nc.vector.tensor_tensor(
                        cT[:, k, :, :], ps[:, 6 + k, 0:3 * P].rearrange("p (j t) -> p j t", t=P),
                        g_c[:, :].rearrange("p (j o) -> p j o", o=1).to_broadcast([P, 3, P]),
                        ALU.mult).then_inc(cT_ready, 1)
                for k in range(2):
                    dve.wait_ge(chunk_out, ONE + SLOTS + it * PER + 8 + k * 4 + 4)
                    q = st_m[:, k, MQ:MK].rearrange("p (h e) -> p h e", h=HM)
                    rotate(k, it * 2 + k, q[:, :, NOPE:NOPE + NF], q[:, :, NOPE + NF:], HM, 1)
                    kk = st_m[:, k, MK:MV].rearrange("p (h e) -> p h e", h=HM)
                    kr = st_a[:, k, KR_AT:IN_W].rearrange("p (o e) -> p o e", o=1)
                    rotate(k, it * 2 + k, kr[:, :, 0:NF], kr[:, :, NF:], 1, 1,
                           kk[:, :, NOPE:NOPE + NF], kk[:, :, NOPE + NF:], HM)
                    dve.sem_inc(m_roped, 1)
                own.restart()

        @block.tensor
        def _(pe):
            pe.wait_ge(small_in, 16 * 7)
            with pe.Fori(0, NT // 2) as it:
                for k in range(2):
                    pe.wait_ge(xn_ready, ONE + it * 2 + k + 1)
                    pe.wait_ge(hT_ready, ONE + it * 2 + k)
                    for j in range(KD):
                        last = nc.tensor.transpose(ps[:, j // 4, (j % 4) * P:(j % 4 + 1) * P],
                                                   xn[:, k, j * P:(j + 1) * P], core.ident[:, :])
                    last.then_inc(xT_done, 1)
                for k in range(2):
                    pe.wait_ge(hT_ready, ONE + it * 2 + k + 1)
                    for c in range(4):
                        pe.wait_ge(w_in_in[c], 16)
                        pe.wait_ge(chunk_out, ONE + it * PER + k * 4 + c + 1)
                        for j in range(KD):
                            last = nc.tensor.matmul(ps[:, 2 + c, 0:width(c)], hT[:, k, j, :],
                                                    w_in[:, j, c * BANK:c * BANK + width(c)],
                                                    start=j == 0, stop=j == KD - 1)
                        last.then_inc(chunk_done, 1)
                for k in range(2):
                    pe.wait_ge(cn_ready, ONE + it * 2 + k + 1)
                    for j in range(3):
                        last = nc.tensor.transpose(ps[:, 6 + k, j * P:(j + 1) * P], cn[:, k, j * P:(j + 1) * P],
                                                   core.ident[:, :])
                    last.then_inc(cnT_done, 1)
                pe.wait_ge(wc_in, 32)
                for k in range(2):
                    pe.wait_ge(cT_ready, ONE + it * 2 + k + 1)
                    for c in range(4):
                        pe.wait_ge(chunk_out, ONE + it * PER + 8 + k * 4 + c + 1)
                        if c < 2:
                            n = min(BANK, UQ_W - c * BANK)
                            for j in range(2):
                                last = nc.tensor.matmul(ps[:, 2 + c, 0:n], cT[:, k, j, :],
                                                        w_uq[:, j, c * BANK:c * BANK + n], start=j == 0, stop=j == 1)
                        else:
                            last = nc.tensor.matmul(ps[:, 2 + c, :], cT[:, k, 2, :],
                                                    w_ukv[:, (c - 2) * BANK:(c - 1) * BANK], start=True, stop=True)
                        last.then_inc(chunk_done, 1)


def attend(core, mix, mask, group, heads, dim, scr, q_at, k_at, v_at, mix_at):
    nc, ps = core.nc, core.ps
    ev = EA
    N = NT * 2
    with ExitStack() as ctx:
        sb, sem = core.scope(ctx)
        g = lambda s: f"{s}_{group}"
        qn, kn = sb(g("qn"), [P, 2, NT, dim]), sb(g("kn"), [P, 2, NT, dim])
        vn = sb(g("vn"), [P, 2, NT, ev])
        qT, kT = sb(g("qT"), [dim, 2, SEQ]), sb(g("kT"), [dim, 2, SEQ])
        sm = sb(g("sm"), [P, 2, SEQ])
        pr = sb(g("pr"), [P, 2, SEQ])
        pT = sb(g("pT"), [P, 2, NT, P])
        least = sb(g("least"), [P, N])
        den = sb(g("den"), [P, N])
        rden = sb(g("rden"), [P, N])
        qkv_in = [sem(g(f"qkv_in{k}")) for k in range(2)]
        qkv_used = [sem(g(f"qkv_used{k}")) for k in range(2)]
        score_done, masked_ready, prob_ready = sem(g("score_done")), sem(g("masked_ready")), sem(g("prob_ready"))
        turned = sem(g("turned"))
        out_act, out_dve = sem(g("out_act")), sem(g("out_dve"))
        pv_done, o_out = sem(g("pv_done")), sem(g("o_out"))
        dve_own, dve_held, pe_held = sem(g("dve_own")), sem(g("dve_held")), sem(g("pe_held"))
        scale = float(dim) ** -0.5

        fills, of_unit = [], {}
        order = []
        def fill(what):
            fills.append(what)
            return len(fills) - 1
        head_fills = {}

        def head_turn(k):
            head_fills[k] = [fill(("qk", k, z, half)) for z in range(2) for half in range(2)]
            order.append(("head", k))

        def score(u):
            if u < N:
                if u % NT == 0:
                    head_turn(u // NT)
                order.append(("score", u))

        score(0)
        score(1)
        for u in range(N):
            i = u % NT
            of_unit[u] = [fill(("p", u, b0, min(4, i + 1 - b0))) for b0 in range(0, i + 1, 4)]
            order.append(("turn", u))
            if u:
                order.append(("pv", u - 1))
            score(u + 2)
        order.append(("pv", N - 1))
        NFILL = len(fills)
        assert NFILL % 2 == 0

        def outs_before(n):
            return (n + 1) // 2, n // 2

        open_counts(nc, (masked_ready, o_out, out_act, out_dve, prob_ready, pv_done, *qkv_in, *qkv_used, score_done,
                         turned))
        block = ctx.enter_context(nc.Block())

        @block.sync
        def _(sp):
            tiles = scr.rearrange("(i p) n -> p i n", p=P)
            with sp.Fori(0, heads // 2) as it:
                for k in range(2):
                    sp.wait_ge(qkv_used[k], ONE + it)
                    for dst, at, w in ((qn, q_at, dim), (kn, k_at, dim), (vn, v_at, ev)):
                        sp.dma_start(dst[:, k, :, :], tiles[:, :, bass.ds(it * (2 * w) + (at + k * w), w)]
                                     ).then_inc(qkv_in[k], 16)

        @block.tensor
        def _(pe):
            def wait_bank(it, n):
                a, d = outs_before(n)
                if n % 2 == 0:
                    pe.wait_ge(out_act, ONE + it * (NFILL // 2) + a)
                else:
                    pe.wait_ge(out_dve, ONE + it * (NFILL // 2) + d)

            def wait_copied(it, n):
                a, d = outs_before(n + 1)
                if n % 2 == 0:
                    pe.wait_ge(out_act, ONE + it * (NFILL // 2) + a)
                else:
                    pe.wait_ge(out_dve, ONE + it * (NFILL // 2) + d)

            with pe.Fori(0, heads // 2) as it:
                for kind, x in order:
                    if kind == "head":
                        pe.wait_ge(qkv_in[x], ONE + it * 48 + 48)
                        for n in head_fills[x]:
                            _, _, z, half = fills[n]
                            wait_bank(it, n)
                            pe.sem_inc(pe_held, 1)
                            src = (qn, kn)[z]
                            for j in range(4):
                                last = nc.tensor.transpose(ps[0:dim, 4 + n % 2, j * P:(j + 1) * P],
                                                           src[:, x, half * 4 + j, :], core.ident[:, :])
                            last.then_inc(turned, 1)
                        for n in head_fills[x][-2:]:
                            wait_copied(it, n)
                    elif kind == "score":
                        k, i, b = x // NT, x % NT, x % 2
                        nk = (i + 1) * P
                        pe.wait_ge(masked_ready, ONE + (it * N + x - 1 if x else it * N))
                        for c in range(0, nk, BANK):
                            w = min(BANK, nk - c)
                            last = nc.tensor.matmul(ps[:, 2 * b + c // BANK, 0:w], qT[:, k, i * P:(i + 1) * P],
                                                    kT[:, k, c:c + w], start=True, stop=True)
                        last.then_inc(score_done, 1)
                    elif kind == "turn":
                        k, b = x // NT, x % 2
                        pe.wait_ge(prob_ready, ONE + it * N + x + 1)
                        for n in of_unit[x]:
                            _, _, b0, nb = fills[n]
                            wait_bank(it, n)
                            for j in range(nb):
                                last = nc.tensor.transpose(ps[:, 4 + n % 2, j * P:(j + 1) * P],
                                                           pr[:, b, (b0 + j) * P:(b0 + j + 1) * P], core.ident[:, :])
                            last.then_inc(turned, 1)
                    else:
                        k, i, b = x // NT, x % NT, x % 2
                        for n in of_unit[x]:
                            wait_copied(it, n)
                        pe.wait_ge(o_out, ONE + (it * N + x - 1 if x else it * N))
                        for j in range(i + 1):
                            last = nc.tensor.matmul(ps[:, 6 + b, 0:ev], pT[:, b, j, :], vn[:, k, j, :],
                                                    start=j == 0, stop=j == i)
                        last.then_inc(pv_done, 1)
                        if i == NT - 1:
                            pe.wait_ge(pv_done, ONE + it * N + x + 1)
                            pe.sem_inc(qkv_used[k], 1)

        def copy_fill(eng, it, n):
            what, x, z, c = fills[n]
            eng.wait_ge(turned, ONE + it * NFILL + n + 1)
            done = (out_act, out_dve)[n % 2]
            if what == "qk":
                dst = (qT, kT)[z][:, x, c * BANK:(c + 1) * BANK]
                src = ps[0:dim, 4 + n % 2, :]
                s = -scale if z == 0 else 1.0
                if n % 2 == 0:
                    nc.scalar.activation(dst, src, ACT.Copy, scale=s).then_inc(done, 1)
                else:
                    nc.vector.tensor_scalar_mul(dst, src, s).then_inc(done, 1)
            else:
                eng.wait_ge(pv_done, ONE + (it * N + x - 1 if x else it * N))
                dst = pT[:, x % 2, z:z + c, :]
                src = ps[:, 4 + n % 2, 0:c * P].rearrange("p (j t) -> p j t", t=P)
                if n % 2 == 0:
                    nc.scalar.activation(dst, src, ACT.Copy).then_inc(done, 1)
                else:
                    nc.vector.tensor_copy(dst, src).then_inc(done, 1)

        @block.scalar
        def _(act):
            def exp(it, u):
                i, b = u % NT, u % 2
                nk = (i + 1) * P
                act.wait_ge(masked_ready, ONE + it * N + u + 1)
                if u >= 2:
                    act.wait_ge(turned, ONE + it * NFILL + of_unit[u - 2][-1] + 1)
                else:
                    act.wait_ge(turned, ONE + it * NFILL)
                nc.scalar.activation(pr[:, b, 0:nk], sm[:, b, 0:nk], ACT.Exp, scale=-1.0, bias=least[:, u:u + 1],
                                     accum_out=den[:, u:u + 1]).then_inc(prob_ready, 1)

            with act.Fori(0, heads // 2) as it:
                for kind, x in order:
                    if kind == "head":
                        for n in head_fills[x]:
                            if n % 2 == 0:
                                copy_fill(act, it, n)
                    elif kind == "score":
                        exp(it, x)
                    elif kind == "turn":
                        for n in of_unit[x]:
                            if n % 2 == 0:
                                copy_fill(act, it, n)

        @block.vector
        def _(dve):
            own = Own(dve, dve_own)
            with dve.Fori(0, heads // 2) as it:
                for kind, x in order:
                    if kind == "head":
                        for n in head_fills[x]:
                            if n % 2 == 1:
                                copy_fill(dve, it, n)
                    elif kind == "score":
                        i, b = x % NT, x % 2
                        nk = (i + 1) * P
                        dve.wait_ge(prob_ready, ONE + (it * N + x - 1 if x else it * N))
                        dve.wait_ge(score_done, ONE + it * N + x + 1)
                        dve.sem_inc(dve_held, 1)
                        nc.vector.tensor_tensor_reduce(
                            out=sm[:, b, 0:nk], in0=ps[:, 2 * b:2 * b + 2, :].rearrange("p b n -> p (b n)")[:, 0:nk],
                            in1=mask[:, (NT - 1 - i) * P:], scale=1.0, scalar=3.0e38, op0=ALU.add, op1=ALU.min,
                            accum_out=least[:, x:x + 1]).then_inc(masked_ready, 1)
                    elif kind == "turn":
                        for n in of_unit[x]:
                            if n % 2 == 1:
                                copy_fill(dve, it, n)
                    else:
                        k, i, b = x // NT, x % NT, x % 2
                        own.link(nc.vector.reciprocal(rden[:, x:x + 1], den[:, x:x + 1]))
                        dve.wait_ge(pv_done, ONE + it * N + x + 1)
                        nc.vector.tensor_scalar(mix[:, i, bass.ds(it * (2 * ev) + (mix_at + k * ev), ev)],
                                                ps[:, 6 + b, 0:ev], rden[:, x:x + 1], None, ALU.mult).then_inc(o_out, 1)
                own.restart()


def project_out(core, mix, w_out, w_out_in, hn_hi, hn_lo):
    nc, ps, res = core.nc, core.ps, core.res
    with ExitStack() as ctx:
        sb, sem = core.scope(ctx)
        st = sb("mix_st", [P, 2, D])
        mT = sb("mixT", [P, 2, KD, P])
        hn = sb("hn", [P, 2, D])
        full = sb("hnT", [P, 2, KD, P])
        junk = sb("junk_o", [P, D])
        ss = sb("ss_o", [P, 2])
        rstd = sb("rstd_o", [P, 2])
        staged, mT_done, mT_ready = sem("staged"), sem("mT_done"), sem("mT_ready")
        y_done, h_ready, hss_ready, hms_ready, hrms_ready = (sem(x) for x in (
            "y_done", "h_ready", "hss_ready", "hms_ready", "hrms_ready"))
        hn_ready, hnT_done, full_ready, hi_ready, lo_ready = (sem(x) for x in (
            "hn_ready", "hnT_done", "full_ready", "hi_ready", "lo_ready"))
        own_a, own_v, held = sem("act_own_o"), sem("dve_own_o"), sem("act_held_o")
        open_counts(nc, (full_ready, h_ready, hi_ready, hms_ready, hnT_done, hn_ready, hrms_ready, hss_ready,
                         lo_ready, mT_done, mT_ready, staged, y_done))
        block = ctx.enter_context(nc.Block())

        def split_banks(k):
            return ps[:, 2 + 2 * k:4 + 2 * k, :]

        @block.tensor
        def _(pe):
            pe.wait_ge(w_out_in, 16)
            with pe.Fori(0, NT // 2) as it:
                for k in range(2):
                    pe.wait_ge(staged, ONE + it * 2 + k + 1)
                    pe.wait_ge(mT_ready, ONE + it * 2 + k)
                    for j in range(KD):
                        last = nc.tensor.transpose(ps[:, j // 4, (j % 4) * P:(j % 4 + 1) * P],
                                                   st[:, k, j * P:(j + 1) * P], core.ident[:, :])
                    last.then_inc(mT_done, 1)
                for k in range(2):
                    pe.wait_ge(mT_ready, ONE + it * 2 + k + 1)
                    pe.wait_ge(h_ready, ONE + it * 2)
                    for c in range(2):
                        for j in range(KD):
                            last = nc.tensor.matmul(split_banks(k)[:, c, :], mT[:, k, j, :],
                                                    w_out[:, j, c * BANK:(c + 1) * BANK], start=j == 0, stop=j == KD - 1)
                    last.then_inc(y_done, 1)
                for k in range(2):
                    pe.wait_ge(hn_ready, ONE + it * 2 + k + 1)
                    pe.wait_ge(full_ready, ONE + it * 2 + k)
                    for j in range(KD):
                        last = nc.tensor.transpose(ps[:, 6 + j // 4, (j % 4) * P:(j % 4 + 1) * P],
                                                   hn[:, k, j * P:(j + 1) * P], core.ident[:, :])
                    last.then_inc(hnT_done, 1)

        @block.scalar
        def _(act):
            own = Own(act, own_a)
            with act.Fori(0, NT // 2) as it:
                for k in range(2):
                    act.wait_ge(mT_done, ONE + it * 2)
                    nc.scalar.activation(st[:, k, :], mix[:, bass.ts(it * 2 + k, 1), :].rearrange("p o d -> p (o d)"),
                                         ACT.Copy).then_inc(staged, 1)
                for k in range(2):
                    act.wait_ge(h_ready, ONE + it * 2 + k + 1)
                    own.sync()
                    own.mark(nc.scalar.activation(junk[:, :], res[:, bass.ts(it * 2 + k, 1), :].rearrange("p o d -> p (o d)"),
                                                  ACT.Square, accum_out=ss[:, k:k + 1]))
                    own.sync()
                    act.sem_inc(hss_ready, 1)
                for k in range(2):
                    act.wait_ge(hms_ready, ONE + it * 2 + k + 1)
                    nc.scalar.activation(rstd[:, k:k + 1], ss[:, k:k + 1], ACT.Sqrt).then_inc(hrms_ready, 1)
                for k in range(2):
                    act.wait_ge(full_ready, ONE + it * 2 + k + 1)
                    act.sem_inc(held, 1)
                    nc.scalar.activation(hn_hi[:, :, bass.ts(it * 2 + k, P)], full[:, k, :, :], ACT.Copy
                                         ).then_inc(hi_ready, 1)
                own.restart()

        @block.vector
        def _(dve):
            own = Own(dve, own_v)
            with dve.Fori(0, NT // 2) as it:
                for k in range(2):
                    dve.wait_ge(mT_done, ONE + it * 2 + k + 1)
                    nc.vector.tensor_copy(mT[:, k, :, :], ps[:, 0:2, :].rearrange("p b (j t) -> p (b j) t", t=P)
                                          ).then_inc(mT_ready, 1)
                for k in range(2):
                    dve.wait_ge(y_done, ONE + it * 2 + k + 1)
                    h = res[:, bass.ts(it * 2 + k, 1), :].rearrange("p o d -> p (o d)")
                    nc.vector.tensor_tensor(h, split_banks(k).rearrange("p b n -> p (b n)"), h, ALU.add
                                            ).then_inc(h_ready, 1)
                for k in range(2):
                    dve.wait_ge(hss_ready, ONE + it * 2 + k + 1)
                    own.link(nc.vector.tensor_scalar(ss[:, k:k + 1], ss[:, k:k + 1], 1.0 / D, EPS, ALU.mult, ALU.add))
                    dve.sem_inc(hms_ready, 1)
                for k in range(2):
                    dve.wait_ge(hrms_ready, ONE + it * 2 + k + 1)
                    own.link(nc.vector.reciprocal(rstd[:, k:k + 1], rstd[:, k:k + 1]))
                    dve.wait_ge(hnT_done, ONE + it * 2)
                    nc.vector.tensor_scalar(hn[:, k, :], res[:, bass.ts(it * 2 + k, 1), :].rearrange("p o d -> p (o d)"),
                                            rstd[:, k:k + 1], None, ALU.mult).then_inc(hn_ready, 1)
                for k in range(2):
                    dve.wait_ge(hnT_done, ONE + it * 2 + k + 1)
                    nc.vector.tensor_tensor(
                        full[:, k, :, :], ps[:, 6:8, :].rearrange("p b (j t) -> p (b j) t", t=P),
                        core.g_ffn[:, :].rearrange("p (j o) -> p j o", o=1).to_broadcast([P, KD, P]),
                        ALU.mult).then_inc(full_ready, 1)
                for k in range(2):
                    dve.wait_ge(hi_ready, ONE + it * 2 + k + 1)
                    at = bass.ts(it * 2 + k, P)
                    nc.vector.tensor_tensor(hn_lo[:, :, at], full[:, k, :, :], hn_hi[:, :, at].bitcast(f32), ALU.subtract
                                            ).then_inc(lo_ready, 1)
                own.restart()


def route(core, hn_hi, hn_lo, slotT):
    nc, ps = core.nc, core.ps
    NS = PH * TOPK
    QT = 2
    NQ = NT // QT
    with ExitStack() as ctx:
        sb, sem = core.scope(ctx)
        w_raw = sb("w_raw", [P, 2, KD, PQ])
        w_hi = sb("w_hi", [P, KD, PQ], f32r)
        w_lo = sb("w_lo", [P, KD, PQ], f32r)
        keys = sb("keys", [P, 2, 2, HALFQ])
        keysT = sb("keysT", [P, 2, NKEY])
        qT = sb("peer_qT", [P, 2, SEQ])
        sc = sb("sc", [P, 2, NT, NKEY])
        sc2 = sb("sc2", [P, NT, NKEY])
        top = sb("top", [P, 2, NT, TOPK])
        top_u = sb("top_u", [P, 2, NT, TOPK], u32)
        top_key = sb("top_key", [P, 2, NT, TOPK])
        pair = sb("pair", [P, NT, NC_])
        pair2 = sb("pair2", [P, NT, NC_])
        number = sb("number", [P, NT, NC_])
        best = sb("best", [P, NT, TOPK])
        at_u = sb("at_u", [P, NT, TOPK], u32)
        at = sb("at", [P, NT, TOPK], bf16)
        hit = sb("hit", [P, 2, QT, NC_, TOPK], bf16)
        found = sb("found", [P, 2, QT, NC_, TOPK])
        iota = sb("iota_p", [P, NC_, TOPK], bf16)
        iota_f = sb("iota_f", [P, NC_])
        expert = sb("expert", [P, NT, TOPK])
        expert_i = sb("expert_i", [P, NT, TOPK], i32)
        key_i = sb("key_i", [P, 2, NT, TOPK], i32)
        slot = sb("slot", [P, 3, NT, NS])
        ex = sb("ex", [P, NT, TOPK])
        den = sb("den_p", [P, NT])
        iota_in, parked = sem("iota_in"), sem("parked")
        w_pq_in = [sem(f"w_pq_in{b}") for b in range(2)]
        keys_in = [sem(f"keys_in{b}") for b in range(2)]
        hi_made, lo_made, kT_done, kT_ready = sem("wpq_hi_made"), sem("wpq_lo_made"), sem("kT_done"), sem("kT_ready")
        q_done, q_out, sc_done, sc_out, ranked = (sem(x) for x in ("q_done", "q_out", "sc_done", "sc_out", "ranked"))
        keys_ranked, number_ready, hit_ready, found_ready, summed = (sem(x) for x in (
            "keys_ranked", "number_ready", "hit_ready", "found_ready", "summed"))
        centred, ex_ready, slot_ready, slotT_done, slotT_ready = (sem(x) for x in (
            "centred", "ex_ready", "slot_ready", "slotT_done", "slotT_ready"))
        own_v, held, own_p = sem("dve_own_r"), sem("dve_held_r"), sem("pool_own_r")
        open_counts(nc, (*w_pq_in, *keys_in, hi_made, lo_made, kT_done, kT_ready, q_done, q_out, sc_done, sc_out, ranked,
                         keys_ranked, number_ready, hit_ready, found_ready, summed, centred, ex_ready))
        block = ctx.enter_context(nc.Block())
        NH2 = PH // 2

        @block.sync
        def _(sp):
            sp.dma_start(core.scr_hi, hn_hi[:, :, :].bitcast(f32)).then_inc(parked, 16)
            sp.dma_start(core.scr_lo, hn_lo[:, :, :].bitcast(f32)).then_inc(parked, 16)
            w_v = core.i["w_pq"].rearrange("l (k p) n -> p (l k) n", p=P)
            k_v = core.i["sub_keys"].rearrange("l h z n c -> n (l h) z c")
            sp.dma_start(iota_f[:, :], core.i["c_iota"][:, 0:NC_]).then_inc(iota_in, 16)
            with sp.Fori(0, NH2) as it:
                for b in range(2):
                    sp.wait_ge(lo_made, ONE + (it * 2 + b - 1 if b else it * 2))
                    sp.dma_start(w_raw[:, b, :, :], w_v[:, :, bass.ds(it * (2 * PQ) + b * PQ, PQ)]).then_inc(w_pq_in[b], 16)
                    sp.wait_ge(kT_done, ONE + (it * 2 + b - 1 if b else it * 2))
                    sp.dma_start(keys[:, b, :, :], k_v[:, bass.ts(it * 2 + b, 1), :, :].rearrange("n o z c -> n (o z) c")
                                 ).then_inc(keys_in[b], 16)
            sp.wait_ge(iota_in, 16)
            sp.wait_ge(parked, 32)

        @block.tensor
        def _(pe):
            with pe.Fori(0, NH2) as it:
                for b in range(2):
                    pe.wait_ge(keys_in[b], ONE + it * 16 + 16)
                    pe.wait_ge(kT_ready, ONE + it * 2 + b)
                    for z in range(2):
                        last = nc.tensor.transpose(ps[:, 2, z * NKEY:(z + 1) * NKEY], keys[:, b, z, :], core.ident[:, :])
                    last.then_inc(kT_done, 1)
                    pe.wait_ge(hi_made, ONE + it * 2 + b + 1)
                    pe.wait_ge(lo_made, ONE + it * 2 + b + 1)
                    for z in range(2):
                        cs = slice(z * HALFQ, (z + 1) * HALFQ)
                        for half in range(2):
                            pe.wait_ge(q_out, ONE + (it * 8 + b * 4 + z * 2 + half - 1 if b or z or half else it * 8))
                            ts = slice(half * BANK, (half + 1) * BANK)
                            terms = [(w, x, j) for w, x in ((w_hi, hn_hi), (w_hi, hn_lo), (w_lo, hn_hi)) for j in range(KD)]
                            for n, (w, x, j) in enumerate(terms):
                                last = nc.tensor.matmul(ps[:, half, :], w[:, j, cs], x[:, j, ts],
                                                        start=n == 0, stop=n == len(terms) - 1)
                            last.then_inc(q_done, 1)
                    pe.wait_ge(kT_ready, ONE + it * 2 + b + 1)
                    for z in range(2):
                        pe.wait_ge(q_out, ONE + it * 8 + b * 4 + z * 2 + 2)
                        pe.wait_ge(sc_out, ONE + (it * 4 + b * 2 + z - 1 if b or z else it * 4))
                        for i in range(NT):
                            last = nc.tensor.matmul(ps[:, 4 + 2 * z + i // 4, (i % 4) * P:(i % 4 + 1) * P],
                                                    qT[:, z, i * P:(i + 1) * P], keysT[:, z, :], start=True, stop=True)
                        last.then_inc(sc_done, 1)
            pe.wait_ge(slot_ready, 1)
            for i in range(NT):
                if i >= 2:
                    pe.wait_ge(slotT_ready, i - 1)
                for z in range(3):
                    last = nc.tensor.transpose(ps[:, i % 2, z * P:(z + 1) * P], slot[:, z, i, :], core.ident[:, :])
                last.then_inc(slotT_done, 1)

        @block.scalar
        def _(act):
            def head(h, b, first=False, split_next=True):
                act.wait_ge(kT_done, ONE + h + 1)
                act.wait_ge(sc_done, ONE + h * 2)
                nc.scalar.activation(keysT[:, :, :], ps[:, 2, 0:2 * NKEY].rearrange("p (z n) -> p z n", z=2),
                                     ACT.Copy).then_inc(kT_ready, 1)
                for z in range(2):
                    for half in range(2):
                        act.wait_ge(q_done, ONE + h * 4 + z * 2 + half + 1)
                        nc.scalar.activation(qT[:, z, half * BANK:(half + 1) * BANK], ps[:, half, :],
                                             ACT.Copy).then_inc(q_out, 1)
                if split_next:
                    act.wait_ge(w_pq_in[1 - b], ONE + (h + 1 - (1 - b)) * 8 + 16)
                    nc.scalar.activation(w_hi[:, :, :], w_raw[:, 1 - b, :, :], ACT.Copy).then_inc(hi_made, 1)
                if not first:
                    exponentials(h)
                for z in range(2):
                    act.wait_ge(sc_done, ONE + h * 2 + z + 1)
                    if not first:
                        act.wait_ge(ranked, ONE + h * 2 + z - 1)
                    nc.scalar.activation(sc[:, z, :, :], ps[:, 4 + 2 * z:6 + 2 * z, :].rearrange(
                        "p b (i n) -> p (b i) n", n=NKEY), ACT.Copy).then_inc(sc_out, 1)

            def exponentials(heads):
                act.wait_ge(centred, ONE + heads)
                nc.scalar.activation(ex[:, :, :], ex[:, :, :], ACT.Exp).then_inc(ex_ready, 1)

            act.wait_ge(w_pq_in[0], ONE + 16)
            nc.scalar.activation(w_hi[:, :, :], w_raw[:, 0, :, :], ACT.Copy).then_inc(hi_made, 1)
            head(0, 0, first=True)
            with act.Fori(0, NH2 - 1) as it:
                head(it * 2 + 1, 1)
                head(it * 2 + 2, 0)
            head(PH - 1, 1, split_next=False)
            exponentials(PH)
            for i in range(NT):
                act.wait_ge(slotT_done, i + 1)
                nc.scalar.activation(slotT[:, :, i, :], ps[:, i % 2, 0:3 * P].rearrange("p (z t) -> p z t", z=3),
                                     ACT.Copy).then_inc(slotT_ready, 1)

        def pair_sums(eng, own, dst, src):
            for a in range(8):
                own.mark(eng.tensor_tensor(dst[:, :, RUN_AT[a]:RUN_AT[a] + RUN[a]],
                                           src[:, 0, :, a:a + 1].to_broadcast([P, NT, RUN[a]]),
                                           src[:, 1, :, 0:RUN[a]], ALU.add))
            own.mark(eng.tensor_tensor(dst[:, :, RUN_AT[8]:], src[:, 0, :, 8:16],
                                       src[:, 1, :, 0:1].to_broadcast([P, NT, 8]), ALU.add))
            own.sync()

        @block.gpsimd
        def _(pool):
            own = Own(pool, own_p)
            with pool.Fori(0, NH2) as it:
                for b in range(2):
                    pool.wait_ge(keys_ranked, ONE + it * 2 + b + 1)
                    pool.wait_ge(found_ready, ONE + (it * 2 + b) * NQ)
                    pair_sums(nc.gpsimd, own, number, top_key)
                    pool.sem_inc(number_ready, 1)
                    for q in range(NQ):
                        n = (it * 2 + b) * NQ + q
                        pool.wait_ge(hit_ready, ONE + n + 1)
                        pool.wait_ge(summed, ONE + (n - 1 if q else n))
                        nc.gpsimd.tensor_tensor(
                            found[:, q % 2, :, :, :], hit[:, q % 2, :, :, :],
                            number[:, q * QT:(q + 1) * QT, :].rearrange("p i (c o) -> p i c o", o=1)
                            .to_broadcast([P, QT, NC_, TOPK]), ALU.mult).then_inc(found_ready, 1)
                own.restart()

        @block.vector
        def _(dve):
            own = Own(dve, own_v)

            def best16(values, indices, src, rest):
                for i in range(NT):
                    own.mark(nc.vector.max(values[:, i, 0:8], src[:, i, :]))
                own.sync()
                for i in range(NT):
                    own.mark(nc.vector.match_replace(rest[:, i, :], values[:, i, 0:8], src[:, i, :], LOWEST))
                for i in range(NT):
                    own.mark(nc.vector.max_index(indices[:, i, 0:8], values[:, i, 0:8], src[:, i, :]))
                for i in range(NT):
                    if i == 0:
                        own.sync()
                    own.mark(nc.vector.max(values[:, i, 8:16], rest[:, i, :]))
                own.sync()
                for i in range(NT):
                    own.mark(nc.vector.max_index(indices[:, i, 8:16], values[:, i, 8:16], rest[:, i, :]))
                own.sync()

            dve.wait_ge(iota_in, 16)
            own.link(nc.vector.tensor_copy(iota[:, :, :], iota_f[:, :].rearrange("p (c o) -> p c o", o=1)
                                           .to_broadcast([P, NC_, TOPK])))
            own.restart()
            dve.wait_ge(hi_made, ONE + 1)
            nc.vector.tensor_tensor(w_lo[:, :, :], w_raw[:, 0, :, :], w_hi[:, :, :].bitcast(f32), ALU.subtract
                                    ).then_inc(lo_made, 1)

            def look(h, q):
                if not isinstance(h, int) or h * NQ + q >= 2:
                    dve.wait_ge(found_ready, ONE + h * NQ + q - 1)
                nc.vector.tensor_tensor(
                    hit[:, q % 2, :, :, :],
                    at[:, q * QT:(q + 1) * QT, :].rearrange("p i (o k) -> p i o k", o=1)
                    .to_broadcast([P, QT, NC_, TOPK]),
                    iota[:, :, :].rearrange("p (o c) k -> p o c k", o=1).to_broadcast([P, QT, NC_, TOPK]),
                    ALU.is_equal).then_inc(hit_ready, 1)

            def total(h, q):
                dve.wait_ge(found_ready, ONE + h * NQ + q + 1)
                nc.vector.tensor_reduce(expert[:, q * QT:(q + 1) * QT, :],
                                        found[:, q % 2, :, :, :].rearrange("p i c k -> p i k c"), AX, ALU.add
                                        ).then_inc(summed, 1)

            def finish_gates(h):
                dve.wait_ge(ex_ready, ONE + h + 1)
                own.link(nc.vector.tensor_reduce(den[:, :], ex[:, :, :], AX, ALU.add))
                own.link(nc.vector.reciprocal(den[:, :], den[:, :]))
                own.mark(nc.vector.tensor_tensor(
                    slot[:, 2, :, bass.ds(h * TOPK, TOPK)], ex[:, :, :],
                    den[:, :].rearrange("p (i o) -> p i o", o=1).to_broadcast([P, NT, TOPK]), ALU.mult))
                total(h, 0)
                look(h, 2)
                total(h, 1)
                look(h, 3)

            def finish_keys(h):
                total(h, 2)
                total(h, 3)
                dve.wait_ge(summed, ONE + (h + 1) * NQ)
                own.link(nc.vector.tensor_copy(expert_i[:, :, :], expert[:, :, :]))
                own.mark(nc.vector.tensor_single_scalar(key_i[:, 0, :, :], expert_i[:, :, :], 7, ALU.logical_shift_right))
                own.mark(nc.vector.tensor_single_scalar(key_i[:, 1, :, :], expert_i[:, :, :], NKEY - 1, ALU.bitwise_and))
                own.sync()
                for z in range(2):
                    own.mark(nc.vector.tensor_copy(slot[:, z, :, bass.ds(h * TOPK, TOPK)], key_i[:, z, :, :]))

            def head(h, b, first=False, split_next=True):
                for z in range(2):
                    dve.wait_ge(sc_out, ONE + h * 2 + z + 1)
                    dve.sem_inc(held, 1)
                    best16(top[:, z, :, :], top_u[:, z, :, :], sc[:, z, :, :], sc2)
                    dve.sem_inc(ranked, 1)
                    if z == 0 and split_next:
                        dve.wait_ge(hi_made, ONE + h + 2)
                        nc.vector.tensor_tensor(w_lo[:, :, :], w_raw[:, 1 - b, :, :], w_hi[:, :, :].bitcast(f32),
                                                ALU.subtract).then_inc(lo_made, 1)
                    if not first:
                        (finish_gates, finish_keys)[z](h - 1)
                if not first:
                    dve.wait_ge(number_ready, ONE + h)
                own.mark(nc.vector.tensor_scalar(top_key[:, 0, :, :], top_u[:, 0, :, :], float(NKEY), None, ALU.mult))
                own.mark(nc.vector.tensor_copy(top_key[:, 1, :, :], top_u[:, 1, :, :]))
                own.sync()
                dve.sem_inc(keys_ranked, 1)
                pair_sums(nc.vector, own, pair, top)
                best16(best, at_u, pair, pair2)
                own.mark(nc.vector.tensor_copy(at[:, :, :], at_u[:, :, :]))
                own.mark(nc.vector.tensor_tensor(ex[:, :, :], best[:, :, :],
                                                 best[:, :, 0:1].to_broadcast([P, NT, TOPK]), ALU.subtract))
                own.sync()
                dve.sem_inc(centred, 1)
                look(h, 0)
                look(h, 1)
                own.restart()

            head(0, 0, first=True)
            with dve.Fori(0, NH2 - 1) as it:
                head(it * 2 + 1, 1)
                head(it * 2 + 2, 0)
            head(PH - 1, 1, split_next=False)
            finish_gates(PH - 1)
            finish_keys(PH - 1)
            own.restart()
            dve.sem_inc(slot_ready, 1)


def spread_gates(core, slotT):
    nc, ps = core.nc, core.ps
    OCT = 8
    TU = BANK // NKEY
    NB = OCT // TU
    BODY = 2
    PER_TILE = P // OCT
    NOCT = SEQ // OCT
    ON_POOL = 5
    with ExitStack() as ctx:
        sb, sem = core.scope(ctx)
        gates = sb("gates", [P, 2, NKEY, P])
        one1 = sb("one1", [P, BODY, NKEY, OCT], bf16)
        one2 = sb("one2", [P, BODY, NKEY, OCT], bf16)
        first = sb("first", [P, BODY, OCT, NKEY])
        second = sb("second", [P, BODY, OCT, NKEY])
        iota_f = sb("iota_g", [P, NKEY])
        iota = sb("iota_gb", [P, NKEY, OCT], bf16)
        keysT = sb("slot_keys", [P, 2, SEQ], bf16)
        iota_in = sem("iota_in_g")
        ones_ready, first_dve, first_pool, second_ready = (sem(x) for x in (
            "ones_ready", "first_dve", "first_pool", "second_ready"))
        spread_done, gates_out, own_v = sem("spread_done"), sem("gates_out"), sem("dve_own_g")
        gates_sent = [sem(f"gates_sent{k}") for k in range(2)]
        open_counts(nc, (ones_ready, first_dve, first_pool, second_ready, spread_done, gates_out, *gates_sent))
        block = ctx.enter_context(nc.Block())
        flat = slotT[:, :, :, :].rearrange("p z i t -> p z (i t)")

        @block.sync
        def _(sp):
            sp.dma_start(iota_f[:, :], core.i["c_iota"]).then_inc(iota_in, 16)
            dst = core.scr_g.rearrange("j i t -> i j t")
            with sp.Fori(0, NT // 2) as it:
                for k in range(2):
                    sp.wait_ge(gates_out, ONE + BODY * NB + it * (2 * PER_TILE * NB) + (k + 1) * PER_TILE * NB)
                    sp.dma_start(dst[:, :, bass.ts(it * 2 + k, P)], gates[:, k, :, :]).then_inc(gates_sent[k], 16)
            sp.wait_ge(iota_in, 16)
            for k in range(2):
                sp.wait_ge(gates_sent[k], ONE + 16 * NT // 2)

        def weigh(eng, n, b, lo, hi):
            gate = flat[:, 2, bass.ds(n * OCT + lo, hi - lo)]
            return eng.tensor_tensor(
                first[:, b, lo:hi, :].rearrange("p t i -> p i t"), one1[:, b, :, lo:hi],
                gate.rearrange("p (o t) -> p o t", o=1).to_broadcast([P, NKEY, hi - lo]), ALU.mult)

        @block.vector
        def _(dve):
            own = Own(dve, own_v)
            dve.wait_ge(iota_in, 16)
            own.mark(nc.vector.tensor_copy(iota[:, :, :], iota_f[:, :].rearrange("p (i o) -> p i o", o=1)
                                           .to_broadcast([P, NKEY, OCT])))
            own.mark(nc.vector.tensor_copy(keysT[:, :, :], flat[:, 0:2, :]))
            own.sync()
            dve.sem_inc(spread_done, BODY * NB)
            dve.sem_inc(gates_out, BODY * NB)
            with dve.Fori(0, NOCT // BODY) as it:
                for b in range(BODY):
                    n = it * BODY + b
                    dve.wait_ge(spread_done, ONE + n * NB + NB)
                    for z, dst in ((0, one1), (1, one2)):
                        nc.vector.tensor_tensor(
                            dst[:, b, :, :], iota[:, :, :],
                            keysT[:, z, bass.ds(n * OCT, OCT)].rearrange("p (o t) -> p o t", o=1)
                            .to_broadcast([P, NKEY, OCT]), ALU.is_equal).then_inc(ones_ready, 1)
                    dve.wait_ge(ones_ready, ONE + n * 2 + 1)
                    weigh(nc.vector, n, b, ON_POOL, OCT).then_inc(first_dve, 1)

        @block.gpsimd
        def _(pool):
            with pool.Fori(0, NOCT // BODY) as it:
                for b in range(BODY):
                    n = it * BODY + b
                    pool.wait_ge(ones_ready, ONE + n * 2 + 1)
                    weigh(nc.gpsimd, n, b, 0, ON_POOL).then_inc(first_pool, 1)

        @block.tensor
        def _(pe):
            with pe.Fori(0, NOCT // BODY) as it:
                for b in range(BODY):
                    n = it * BODY + b
                    pe.wait_ge(first_dve, ONE + n + 1)
                    pe.wait_ge(first_pool, ONE + n + 1)
                    pe.wait_ge(second_ready, ONE + n + 1)
                    for u in range(NB):
                        bank = b * NB + u
                        pe.wait_ge(gates_out, ONE + n * NB + u + 1)
                        for s in range(TU):
                            last = nc.tensor.matmul(ps[:, bank, s * NKEY:(s + 1) * NKEY], first[:, b, u * TU + s, :],
                                                    second[:, b, u * TU + s, :], start=True, stop=True)
                        last.then_inc(spread_done, 1)

        @block.scalar
        def _(act):
            def widen(n, b):
                act.wait_ge(ones_ready, ONE + n * 2 + 2)
                act.wait_ge(spread_done, ONE + n * NB + NB)
                nc.scalar.activation(second[:, b, :, :], one2[:, b, :, :].rearrange("p i t -> p t i"),
                                     ACT.Copy).then_inc(second_ready, 1)

            def copy_out(n, q, k, b):
                for u in range(NB):
                    act.wait_ge(spread_done, ONE + BODY * NB + n * NB + u + 1)
                    nc.scalar.activation(
                        gates[:, k, :, bass.ds(q * (BODY * OCT) + (b * OCT + u * TU), TU)].rearrange("p i t -> p t i"),
                        ps[:, b * NB + u, :].rearrange("p (t i) -> p t i", t=TU), ACT.Copy).then_inc(gates_out, 1)

            def octs(tile, q, k, last=False):
                n = tile * PER_TILE + q * BODY
                widen(n + 1, 1)
                copy_out(n, q, k, 0)
                if not last:
                    widen(n + 2, 0)
                copy_out(n + 1, q, k, 1)

            def tile_pair(it, last):
                for k in range(2):
                    act.wait_ge(gates_sent[k], ONE + it * 16)
                    peel = last and k == 1
                    with act.Fori(0, PER_TILE // BODY - peel) as q:
                        octs(it * 2 + k, q, k)
                    if peel:
                        octs(it * 2 + k, PER_TILE // BODY - 1, k, True)

            widen(0, 0)
            with act.Fori(0, NT // 2 - 1) as it:
                tile_pair(it, False)
            tile_pair(NT // 2 - 1, True)


def run_experts(core):
    nc, ps, res = core.nc, core.ps, core.res
    CH = 2
    NG = NKEY // CH
    FILLS = NT * 2
    with ExitStack() as ctx:
        sb, sem = core.scope(ctx)
        hn_hi, hn_lo = sb("hn_hi_e", [P, KD, SEQ], f32r), sb("hn_lo_e", [P, KD, SEQ], f32r)
        hn_in = [sem(f"hn_in{half}") for half in range(2)]
        u = sb("u", [P, CH, D])
        v = sb("v", [P, CH, D])
        gate = sb("gate", [P, CH, SEQ])
        uT_hi, uT_lo = sb("uT_hi", [P, CH, KD, P], f32r), sb("uT_lo", [P, CH, KD, P], f32r)
        v_hi, v_lo = sb("v_hi", [P, CH, D], f32r), sb("v_lo", [P, CH, D], f32r)
        w = sb("w", [P, CH, SEQ])
        w_hi, w_lo = sb("w_hi2", [P, 2, CH, SEQ], f32r), sb("w_lo2", [P, 2, CH, SEQ], f32r)
        u_in = [sem(f"u_in{c}") for c in range(CH)]
        gate_in = [sem(f"gate_in{c}") for c in range(CH)]
        v_in = sem("v_in")
        uT_done, uT_hi_ready, uT_lo_ready = sem("uT_done"), sem("uT_hi_ready"), sem("uT_lo_ready")
        act_done, gelu_ready, w_ready, w_hi_ready, w_lo_ready = (sem(x) for x in (
            "act_done", "gelu_ready", "w_ready", "w_hi_ready", "w_lo_ready"))
        v_hi_ready, v_lo_ready, out_done, added = (sem(x) for x in ("v_hi_ready", "v_lo_ready", "out_done", "added"))
        open_counts(nc, (act_done, added, *gate_in, gelu_ready, out_done, uT_done, uT_hi_ready, uT_lo_ready, *u_in,
                         v_hi_ready, v_in, v_lo_ready, w_hi_ready, w_lo_ready, w_ready))
        block = ctx.enter_context(nc.Block())

        u_v = core.i["u_emb"].rearrange("l (i j) d -> j i (l d)", j=NKEY)
        v_v = core.i["v_emb"].rearrange("l (i j) d -> j i (l d)", j=NKEY)

        def need(eng, sem_, value):
            if not isinstance(value, int) or value > 0:
                eng.wait_ge(sem_, ONE + value)

        def at(ap, n):
            return ap[n] if isinstance(n, int) else ap[bass.ds(n, 1), :, :].rearrange("o p d -> p (o d)")

        def schedule(group=lambda g, b, last: None, out=lambda g, b: None, values=lambda g: None, eng=None):
            group(0, 0, False)
            values(0)
            with eng.Fori(0, NG // 2 - 1) as it:
                group(it * 2 + 1, 1, False)
                out(it * 2, 0)
                values(it * 2 + 1)
                group(it * 2 + 2, 0, False)
                out(it * 2 + 1, 1)
                values(it * 2 + 2)
            group(NG - 1, 1, True)
            out(NG - 2, 0)
            values(NG - 1)
            out(NG - 1, 1)

        @block.sync
        def _(sp):
            sp.dma_start(u[:, 0, :], at(u_v, 0)).then_inc(u_in[0], 16)
            for half in range(2):
                ts = slice(half * BANK, (half + 1) * BANK)
                sp.dma_start(hn_hi[:, :, ts].bitcast(f32), core.scr_hi[:, :, ts]).then_inc(hn_in[half], 16)
                sp.dma_start(hn_lo[:, :, ts].bitcast(f32), core.scr_lo[:, :, ts]).then_inc(hn_in[half], 16)

            def load(g, b, last):
                for c in range(CH):
                    need(sp, uT_done, g * CH + c - 1)
                    if isinstance(g, int) and g * CH + c == 0:
                        continue
                    sp.dma_start(u[:, c, :], at(u_v, g * CH + c)).then_inc(u_in[c], 16)
                for c in range(CH):
                    need(sp, w_ready, g * CH + c - 1)
                    sp.dma_start(gate[:, c, :], at(core.scr_g, g * CH + c)).then_inc(gate_in[c], 16)
                need(sp, v_hi_ready, g)
                need(sp, v_lo_ready, g)
                for c in range(CH):
                    sp.dma_start(v[:, c, :], at(v_v, g * CH + c)).then_inc(v_in, 16)

            schedule(load, eng=sp)

        @block.tensor
        def _(pe):
            def turn(g, c):
                n = g * CH + c
                pe.wait_ge(u_in[c], ONE + g * 16 + 16)
                need(pe, uT_hi_ready, n)
                need(pe, uT_lo_ready, n)
                for j in range(KD):
                    last = nc.tensor.transpose(ps[:, 4 + j // 4, (j % 4) * P:(j % 4 + 1) * P],
                                               u[:, c, j * P:(j + 1) * P], core.ident[:, :])
                last.then_inc(uT_done, 1)

            def activations(g, b, last_group):
                for c in range(CH):
                    n = g * CH + c
                    if not (last_group and c == CH - 1):
                        turn(g + (c + 1) // CH, (c + 1) % CH)
                    pe.wait_ge(uT_hi_ready, ONE + n + 1)
                    pe.wait_ge(uT_lo_ready, ONE + n + 1)
                    need(pe, gelu_ready, n - 1)
                    for half in range(2):
                        if isinstance(g, int) and g == 0:
                            pe.wait_ge(hn_in[half], 32)
                        ts = slice(half * BANK, (half + 1) * BANK)
                        terms = [(x, y, j) for j in range(KD) for x, y in ((uT_hi, hn_hi), (uT_hi, hn_lo), (uT_lo, hn_hi))]
                        for m, (x, y, j) in enumerate(terms):
                            last = nc.tensor.matmul(ps[:, 2 * c + half, :], x[:, c, j, :], y[:, j, ts],
                                                    start=m == 0, stop=m == len(terms) - 1)
                    last.then_inc(act_done, 1)

            def out(g, b):
                pe.wait_ge(w_hi_ready, ONE + g * CH + CH)
                pe.wait_ge(w_lo_ready, ONE + g * CH + CH)
                pe.wait_ge(v_hi_ready, ONE + g + 1)
                pe.wait_ge(v_lo_ready, ONE + g + 1)
                for i in range(NT):
                    for half in range(2):
                        f = i * 2 + half
                        need(pe, added, g * FILLS + (f - 1 if f else 0))
                        terms = [(x, y, c) for c in range(CH) for x, y in ((w_hi, v_hi), (w_hi, v_lo), (w_lo, v_hi))]
                        for m, (x, y, c) in enumerate(terms):
                            last = nc.tensor.matmul(ps[:, 6 + half, :], x[:, b, c, i * P:(i + 1) * P],
                                                    y[:, c, half * BANK:(half + 1) * BANK],
                                                    start=m == 0, stop=m == len(terms) - 1)
                        last.then_inc(out_done, 1)

            turn(0, 0)
            schedule(activations, out, eng=pe)

        @block.scalar
        def _(act):
            def copy_uT(g, c):
                n = g * CH + c
                act.wait_ge(uT_done, ONE + n + 1)
                need(act, act_done, n - 1)
                nc.scalar.activation(uT_hi[:, c, :, :], ps[:, 4:6, :].rearrange("p b (j e) -> p (b j) e", e=P),
                                     ACT.Copy).then_inc(uT_hi_ready, 1)

            def group(g, b, last_group):
                for c in range(CH):
                    n = g * CH + c
                    if not (last_group and c == CH - 1):
                        copy_uT(g + (c + 1) // CH, (c + 1) % CH)
                    act.wait_ge(act_done, ONE + n + 1)
                    need(act, w_lo_ready, n - 1)
                    nc.scalar.activation(w[:, c, :], ps[:, 2 * c:2 * c + 2, :].rearrange("p b t -> p (b t)"),
                                         ACT.Gelu).then_inc(gelu_ready, 1)
                    act.wait_ge(w_ready, ONE + n + 1)
                    need(act, out_done, (g - 1) * FILLS)
                    nc.scalar.activation(w_hi[:, b, c, :], w[:, c, :], ACT.Copy).then_inc(w_hi_ready, 1)

            def values(g):
                act.wait_ge(v_in, ONE + g * (16 * CH) + 16 * CH)
                need(act, out_done, g * FILLS)
                nc.scalar.activation(v_hi[:, :, :], v[:, :, :], ACT.Copy).then_inc(v_hi_ready, 1)

            copy_uT(0, 0)
            schedule(group, values=values, eng=act)

        @block.vector
        def _(dve):
            def split_uT(g, c):
                n = g * CH + c
                dve.wait_ge(uT_hi_ready, ONE + n + 1)
                need(dve, act_done, n - 1)
                nc.vector.tensor_tensor(uT_lo[:, c, :, :], ps[:, 4:6, :].rearrange("p b (j e) -> p (b j) e", e=P),
                                        uT_hi[:, c, :, :].bitcast(f32), ALU.subtract).then_inc(uT_lo_ready, 1)

            def gated(g, c):
                dve.wait_ge(gate_in[c], ONE + g * 16 + 16)
                dve.wait_ge(gelu_ready, ONE + g * CH + c + 1)
                nc.vector.tensor_tensor(w[:, c, :], w[:, c, :], gate[:, c, :], ALU.mult).then_inc(w_ready, 1)

            def low(g, b, c):
                dve.wait_ge(w_hi_ready, ONE + g * CH + c + 1)
                need(dve, out_done, (g - 1) * FILLS)
                nc.vector.tensor_tensor(w_lo[:, b, c, :], w[:, c, :], w_hi[:, b, c, :].bitcast(f32), ALU.subtract
                                        ).then_inc(w_lo_ready, 1)

            def group(g, b, last_group):
                split_uT(g, 1)
                gated(g, 0)
                low(g, b, 0)
                if not last_group:
                    split_uT(g + 1, 0)
                if isinstance(g, int) and g == 0:
                    gated(g, 1)
                    low(g, b, 1)

            def out(g, b):
                for f in range(FILLS):
                    i, half = f // 2, f % 2
                    dve.wait_ge(out_done, ONE + g * FILLS + (f + 1))
                    r = res[:, i, half * BANK:(half + 1) * BANK]
                    nc.vector.tensor_tensor(r, ps[:, 6 + half, :], r, ALU.add).then_inc(added, 1)
                    if not (isinstance(g, int) and g == NG - 1):
                        if f == 1:
                            gated(g + 1, 1)
                        if f == 4:
                            low(g + 1, 1 - b, 1)

            def values(g):
                dve.wait_ge(v_hi_ready, ONE + g + 1)
                nc.vector.tensor_tensor(v_lo[:, :, :], v[:, :, :], v_hi[:, :, :].bitcast(f32), ALU.subtract
                                        ).then_inc(v_lo_ready, 1)

            split_uT(0, 0)
            schedule(group, out, values, eng=dve)
            dve.wait_ge(added, ONE + NG * FILLS)


def finish(core):
    nc, res = core.nc, core.res
    with ExitStack() as ctx:
        sb, sem = core.scope(ctx)
        g = sb("g_final", [P, D])
        junk = sb("junk_f", [P, D])
        ss, rstd = sb("ss_f", [P, NT]), sb("rstd_f", [P, NT])
        g_in, ss_ready, ms_ready, rms_ready, y_ready, sent = (sem(x) for x in (
            "g_in", "ss_ready_f", "ms_ready_f", "rms_ready_f", "y_ready_f", "sent_f"))
        own_a, own_v = sem("act_own_f"), sem("dve_own_f")
        block = ctx.enter_context(nc.Block())

        @block.sync
        def _(sp):
            sp.dma_start(g[:, :], core.i["g_final"].rearrange("(o d) -> o d", o=1).to_broadcast([P, D])).then_inc(g_in, 16)
            o = core.out.rearrange("b (i p) d -> p (b i) d", p=P)
            for i in range(NT):
                sp.wait_ge(y_ready, i + 1)
                sp.dma_start(o[:, i, :], res[:, i, :]).then_inc(sent, 16)
            sp.wait_ge(sent, 16 * NT)

        @block.scalar
        def _(act):
            own = Own(act, own_a)
            for i in range(NT):
                if i:
                    own.sync()
                own.mark(nc.scalar.activation(junk[:, :], res[:, i, :], ACT.Square, accum_out=ss[:, i:i + 1]))
            own.sync()
            act.sem_inc(ss_ready, 1)
            act.wait_ge(ms_ready, 1)
            nc.scalar.activation(rstd[:, :], ss[:, :], ACT.Sqrt).then_inc(rms_ready, 1)

        @block.vector
        def _(dve):
            own = Own(dve, own_v)
            dve.wait_ge(ss_ready, 1)
            own.link(nc.vector.tensor_scalar(ss[:, :], ss[:, :], 1.0 / D, EPS, ALU.mult, ALU.add))
            dve.sem_inc(ms_ready, 1)
            dve.wait_ge(rms_ready, 1)
            own.link(nc.vector.reciprocal(rstd[:, :], rstd[:, :]))
            dve.wait_ge(g_in, 16)
            for i in range(NT):
                nc.vector.scalar_tensor_tensor(out=res[:, i, :], in0=res[:, i, :], scalar=rstd[:, i:i + 1],
                                               in1=g[:, :], op0=ALU.mult, op1=ALU.mult).then_inc(y_ready, 1)


def layer(nc, ins, out):
    with ExitStack() as ctx, ExitStack() as outer:
        core = Core(nc, ctx, ins, out)
        project_in(core)
        with ExitStack() as mid:
            sb, sem = core.scope(mid)
            mix = sb("mix", [P, NT, D])
            w_out = sb("w_out", [P, KD, D])
            w_out_in = sem("w_out_in")
            with ExitStack() as att:
                mask = att.enter_context(nc.sbuf_tensor("mask", [P, 2, SEQ], f32))
                with nc.semaphore("mask_in") as mask_in, nc.Block() as block:
                    @block.sync
                    def _(sp):
                        sp.dma_start(mask[:, :, :], core.i["c_mask"]).then_inc(mask_in, 16)
                        sp.dma_start(w_out[:, :, :], core.i["w_out"].rearrange("l (k p) n -> p (l k) n", p=P)
                                     ).then_inc(w_out_in, 16)
                        sp.wait_ge(mask_in, 16)
                attend(core, mix, mask[:, 0, :], "a", HA, EA, core.scr_a, 0, WA, 2 * WA, 0)
                attend(core, mix, mask[:, 1, :], "m", HM, EM, core.scr_m, MQ, MK, MV, WA)
            hidden = outer.enter_context(ExitStack())
            hn_hi, hn_lo = (hidden.enter_context(nc.sbuf_tensor(n, [P, KD, SEQ], f32r, side="right"))
                            for n in ("hn_hi", "hn_lo"))
            project_out(core, mix, w_out, w_out_in, hn_hi, hn_lo)
        with ExitStack() as peer:
            slotT = peer.enter_context(nc.sbuf_tensor("slotT", [P, 3, NT, P], f32))
            route(core, hn_hi, hn_lo, slotT)
            hidden.close()
            spread_gates(core, slotT)
        run_experts(core)
        finish(core)


NAMES = ["x", "positions", "g_mix", "w_in", "g_cq", "w_uq", "g_ckv", "w_ukv", "w_out", "g_ffn",
         "w_pq", "sub_keys", "u_emb", "v_emb", "g_final"]


def constants(np):
    half = NF
    freq = np.float32(500000.0) ** (-np.arange(half, dtype=np.float32) / np.float32(half))
    dist = (SEQ - P) + np.arange(P)[:, None] - np.arange(SEQ)[None, :]
    count = ((dist >= 0) & (dist <= 128)).astype(np.int64)
    count += (dist >= 0) & (dist <= 512) & (dist % 4 == 0)
    count += (dist >= 0) & (dist <= 2048) & (dist % 16 == 0)
    mask = np.full((P, 2, SEQ), BIG, np.float32)
    mask[:, 0] = np.where(count > 0, -np.log(np.maximum(count, 1)), BIG)
    mask[:, 1] = np.where(dist >= 0, 0.0, BIG)
    return {
        "c_freq": np.broadcast_to(freq, (P, half)).copy(),
        "c_ident": np.eye(P, dtype=np.float32),
        "c_mask": mask,
        "c_iota": np.broadcast_to(np.arange(P, dtype=np.float32), (P, P)).copy(),
    }


def kernel(**inputs):
    import numpy as np
    import concourse.bacc as bacc
    from concourse.bass_utils import run_bass_kernel_spmd

    nc = bacc.Bacc("TRN2", target_bir_lowering=False, num_devices=1)
    arrays = {"in_" + n: np.ascontiguousarray(inputs[n]) for n in NAMES}
    arrays.update(constants(np))
    ins = {n.removeprefix("in_"): nc.dram_tensor(n, a.shape, mybir.dt.from_np(a.dtype), kind="ExternalInput").ap()
           for n, a in arrays.items()}
    out = nc.dram_tensor("out", (1, SEQ, D), f32, kind="ExternalOutput").ap()
    layer(nc, ins, out)
    r = run_bass_kernel_spmd(nc, [arrays], core_ids=[0])
    return r.results[0]["out"]
```

```python
from contextlib import ExitStack

import concourse.bass as bass
from concourse import mybir

P = 128
SEQ = 1024
D = 1024
NT = SEQ // P
KD = D // P
BANK = 512

HA, EA, ROT_A = 8, 64, 16
HM, NOPE, ROPE, VM = 8, 64, 32, 64
EM = NOPE + ROPE
QR, KR = 256, 128
WA = HA * EA
IN_W = 3 * WA + QR + KR + ROPE
UQ_W = HM * EM
UKV_W = HM * (NOPE + VM)
C_AT = 3 * WA
KV_AT = C_AT + QR
KR_AT = KV_AT + KR
MQ, MK, MV = 0, HM * EM, 2 * HM * EM
SM_W = 2 * HM * EM + HM * VM
NF = ROPE // 2
EPS = 1e-6

PH, NKEY, PQ, TOPK = 8, 128, 256, 16
HALFQ = PQ // 2
RUN = [TOPK // (a + 1) for a in range(TOPK)]
RUN_AT = [sum(RUN[:a]) for a in range(TOPK)]
NC_ = sum(RUN)
NEXP = NKEY * NKEY
FIRST = 6
PRE = 10

TWO_PI_HI = 6.28125
TWO_PI_LO = 1.9353071795864769e-3
ROUND = 12582912.0
BIG = 1e30
ONE = 1
LOWEST = -3.0e38

f32 = mybir.dt.float32
f32r = mybir.dt.float32r
bf16 = mybir.dt.bfloat16
i32 = mybir.dt.int32
u32 = mybir.dt.uint32
ALU = mybir.AluOpType
ACT = mybir.ActivationFunctionType
AX = mybir.AxisListType.X


class Own:

    def __init__(self, eng, sem):
        self.eng, self.sem, self.n = eng, sem, 0

    def mark(self, ins):
        ins.then_inc(self.sem, 1)
        self.n += 1
        return self.n

    def link(self, ins):
        self.mark(ins)
        self.eng.wait_ge(self.sem, self.n)

    def sync(self):
        self.eng.wait_ge(self.sem, self.n)

    def restart(self):
        if self.n:
            self.eng.wait_ge(self.sem, self.n)
            self.eng.sem_clear(self.sem)
        self.n = 0


def open_counts(nc, sems):
    with nc.Block() as block:
        @block.sync
        def _(sp):
            for s in sems:
                sp.sem_inc(s, ONE)


class Core:

    def __init__(self, nc, ctx, ins, out):
        self.nc, self.i, self.out = nc, ins, out
        self.sb = lambda name, shape, dt=f32, c=ctx: c.enter_context(nc.sbuf_tensor(name, shape, dt))
        self.ps = ctx.enter_context(nc.psum_tensor("psum", [P, 8, BANK], f32))
        self.res = self.sb("res", [P, NT, D])
        self.ident = self.sb("ident", [P, P])
        self.g_ffn = self.sb("g_ffn_col", [P, KD])
        self.act_own, self.dve_own = (ctx.enter_context(nc.semaphore(n)) for n in ("act_own", "dve_own"))
        dram = lambda name, shape: nc.dram_tensor(name, shape, f32, kind="Internal").ap()
        self.scr_a = dram("scr_a", [SEQ, C_AT])
        self.scr_m = dram("scr_m", [SEQ, SM_W])
        self.scr_hi = dram("scr_hi", [P, KD, SEQ])
        self.scr_lo = dram("scr_lo", [P, KD, SEQ])
        self.scr_w = dram("scr_w", [PRE, P, SEQ])
        self.scr_g = dram("scr_g", [NKEY, NKEY, SEQ])

    def scope(self, ctx):
        sb = lambda name, shape, dt=f32: ctx.enter_context(self.nc.sbuf_tensor(name, shape, dt))
        sem = lambda name: ctx.enter_context(self.nc.semaphore(name))
        return sb, sem


def column(v, n):
    return v.rearrange("(k p) -> p k", p=P)


def project_in(core):
    nc, ps, res = core.nc, core.ps, core.res
    I = core.i
    with ExitStack() as ctx:
        sb, sem = core.scope(ctx)
        w_in = sb("w_in", [P, KD, IN_W])
        w_uq = sb("w_uq", [P, 2, UQ_W])
        w_ukv = sb("w_ukv", [P, UKV_W])
        g_mix = sb("g_mix", [P, KD])
        g_c = sb("g_c", [P, 3])
        pos_i = sb("pos_i", [P, NT], i32)
        pos = sb("pos", [P, NT])
        freq = sb("freq", [P, NF])
        ang = sb("ang", [P, NT, NF])
        turn = sb("turn", [P, NT, NF])
        trig = sb("trig", [P, 2, NT, NF])
        ss = sb("ss", [P, 2])
        rstd = sb("rstd", [P, 2])
        junk = sb("junk", [P, D])
        xn = sb("xn", [P, 2, D])
        hT = sb("hT", [P, 2, KD, P])
        st_a = sb("st_a", [P, 2, IN_W])
        st_m = sb("st_m", [P, 2, SM_W])
        ssc = sb("ssc", [P, 2, 2])
        rstc = sb("rstc", [P, 2, 2])
        cn = sb("cn", [P, 2, QR + KR])
        cT = sb("cT", [P, 2, 3, P])
        rt = sb("rt", [P, 4, 2 * HA, NF])

        x_in = [sem(f"x_in{n}") for n in range(NT // 2)]
        w_in_in = [sem(f"w_in_in{n}") for n in range(4)]
        mix_in, small_in, wc_in = sem("mix_in"), sem("small_in"), sem("wc_in")
        ss_ready, ms_ready, rms_ready = sem("ss_ready"), sem("ms_ready"), sem("rms_ready")
        ang_ready, trig_ready = sem("ang_ready"), sem("trig_ready")
        xn_ready, xT_done, hT_ready = sem("xn_ready"), sem("xT_done"), sem("hT_ready")
        chunk_done, chunk_out = sem("chunk_done"), sem("chunk_out")
        css_ready, cms_ready, crms_ready = sem("css_ready"), sem("cms_ready"), sem("crms_ready")
        cn_ready, cnT_done, cT_ready = sem("cn_ready"), sem("cnT_done"), sem("cT_ready")
        a_roped, m_roped = sem("a_roped"), sem("m_roped")
        a_sent = [sem(f"a_sent{k}") for k in range(2)]
        m_sent = [sem(f"m_sent{k}") for k in range(2)]
        SLOTS = 4
        PER = 16

        def width(c):
            return min(BANK, IN_W - c * BANK)

        x_v = I["x"].rearrange("b (i p) d -> p (b i) d", p=P)
        w_v = I["w_in"].rearrange("l (k p) n -> p (l k) n", p=P)
        LAST = NT // 2 - 1
        open_counts(nc, (ss_ready, ms_ready, rms_ready, a_roped, *a_sent, cT_ready, chunk_done, chunk_out, cms_ready,
                         cnT_done, cn_ready, crms_ready,
                         css_ready, hT_ready, m_roped, *m_sent, xT_done, xn_ready))
        block = ctx.enter_context(nc.Block())

        @block.sync
        def _(sp):
            def load_x(n):
                sp.dma_start(res[:, 2 * n:2 * n + 2, :], x_v[:, 2 * n:2 * n + 2, :]).then_inc(x_in[n], 16)

            sp.dma_start(core.ident[:, :], I["c_ident"]).then_inc(mix_in, 16)
            load_x(0)
            for c in range(4):
                sp.dma_start(w_in[:, :, c * BANK:c * BANK + width(c)],
                             w_v[:, :, c * BANK:c * BANK + width(c)]).then_inc(w_in_in[c], 16)
            for n in range(1, NT // 2):
                load_x(n)
            sp.dma_start(w_uq[:, :, :], I["w_uq"].rearrange("l (k p) n -> p (l k) n", p=P)).then_inc(wc_in, 16)
            sp.dma_start(w_ukv[:, :], I["w_ukv"].rearrange("l p n -> p (l n)")).then_inc(wc_in, 16)
            with sp.Fori(0, NT // 2) as it:
                for k in range(2):
                    sp.wait_ge(a_roped, ONE + it * 2 + k + 1)
                    sp.dma_start(core.scr_a.rearrange("(i p) n -> i p n", p=P)[it * 2 + k],
                                 st_a[:, k, 0:C_AT]).then_inc(a_sent[k], 16)
                for k in range(2):
                    sp.wait_ge(m_roped, ONE + it * 2 + k + 1)
                    sp.dma_start(core.scr_m.rearrange("(i p) n -> i p n", p=P)[it * 2 + k],
                                 st_m[:, k, :]).then_inc(m_sent[k], 16)
            for k in range(2):
                sp.wait_ge(a_sent[k], ONE + 16 * NT // 2)
                sp.wait_ge(m_sent[k], ONE + 16 * NT // 2)

        @block.scalar
        def _(act):
            own = Own(act, core.act_own)
            with nc.allow_non_contiguous_dma(reason="gains and positions as columns"):
                act.dma_start(g_mix[:, :], column(I["g_mix"][0], KD)).then_inc(mix_in, 16)
                act.dma_start(pos_i[:, :], I["positions"].rearrange("b (i p) -> p (b i)", p=P)).then_inc(small_in, 16)
                act.dma_start(core.g_ffn[:, :], column(I["g_ffn"][0], KD)).then_inc(small_in, 16)
                act.dma_start(g_c[:, 0:2], column(I["g_cq"][0], 2)).then_inc(small_in, 16)
                act.dma_start(g_c[:, 2:3], column(I["g_ckv"][0], 1)).then_inc(small_in, 16)
            act.dma_start(freq[:, :], I["c_freq"]).then_inc(small_in, 16)

            def row_norms(n):
                if isinstance(n, int):
                    act.wait_ge(x_in[n], 16)
                else:
                    for x in x_in[1:]:
                        act.wait_ge(x, 16)
                    act.wait_ge(xn_ready, ONE + n * 2)
                for k in range(2):
                    own.sync()
                    own.mark(nc.scalar.activation(junk[:, :], res[:, bass.ts(n * 2 + k, 1), :].rearrange("p o d -> p (o d)"),
                                                  ACT.Square, accum_out=ss[:, k:k + 1]))
                own.sync()
                act.sem_inc(ss_ready, 1)
                act.wait_ge(ms_ready, ONE + n + 1)
                nc.scalar.activation(rstd[:, :], ss[:, :], ACT.Sqrt).then_inc(rms_ready, 1)

            def pair(n, ahead):
                for k in range(2):
                    act.wait_ge(a_sent[k], ONE + n * 16)
                    act.wait_ge(m_roped, ONE + n * 2)
                    for c in range(4):
                        act.wait_ge(chunk_done, ONE + n * PER + k * 4 + c + 1)
                        own.mark(nc.scalar.activation(st_a[:, k, c * BANK:c * BANK + width(c)],
                                                      ps[:, 2 + c, 0:width(c)], ACT.Copy))
                        own.sync()
                        act.sem_inc(chunk_out, 1)
                    own.mark(nc.scalar.activation(junk[:, 0:QR], st_a[:, k, C_AT:KV_AT], ACT.Square,
                                                  accum_out=ssc[:, k, 0:1]))
                    own.mark(nc.scalar.activation(junk[:, QR:QR + KR], st_a[:, k, KV_AT:KR_AT], ACT.Square,
                                                  accum_out=ssc[:, k, 1:2]))
                    own.sync()
                    act.sem_inc(css_ready, 1)
                    act.wait_ge(cms_ready, ONE + n * 2 + k + 1)
                    nc.scalar.activation(rstc[:, k, :], ssc[:, k, :], ACT.Sqrt).then_inc(crms_ready, 1)
                    if ahead and k == 0:
                        row_norms(n + 1)
                for k in range(2):
                    act.wait_ge(m_sent[k], ONE + n * 16)
                    mk = st_m[:, k, MK:MV].rearrange("p (h e) -> p h e", h=HM)
                    mv = st_m[:, k, MV:SM_W].rearrange("p (h e) -> p h e", h=HM)
                    for c in range(4):
                        act.wait_ge(chunk_done, ONE + n * PER + 8 + k * 4 + c + 1)
                        if c < 2:
                            w = min(BANK, UQ_W - c * BANK)
                            own.mark(nc.scalar.activation(st_m[:, k, c * BANK:c * BANK + w], ps[:, 2 + c, 0:w],
                                                          ACT.Copy))
                        else:
                            hs = slice((c - 2) * 4, (c - 2) * 4 + 4)
                            kv = ps[:, 2 + c, :].rearrange("p (h e) -> p h e", h=4)
                            own.mark(nc.scalar.activation(mk[:, hs, 0:NOPE], kv[:, :, 0:NOPE], ACT.Copy))
                            own.mark(nc.scalar.activation(mv[:, hs, :], kv[:, :, NOPE:], ACT.Copy))
                        own.sync()
                        act.sem_inc(chunk_out, 1)
                own.restart()

            row_norms(0)
            act.wait_ge(ang_ready, 1)
            nc.scalar.activation(trig[:, :, :, :], trig[:, :, :, :], ACT.Sin).then_inc(trig_ready, 1)
            own.restart()
            with act.Fori(0, LAST) as it:
                pair(it, True)
            pair(LAST, False)

        @block.vector
        def _(dve):
            own = Own(dve, core.dve_own)
            dve.sem_inc(chunk_out, SLOTS)

            def row_norms(n):
                dve.wait_ge(ss_ready, ONE + n + 1)
                own.link(nc.vector.tensor_scalar(ss[:, :], ss[:, :], 1.0 / D, EPS, ALU.mult, ALU.add))
                dve.sem_inc(ms_ready, 1)
                dve.wait_ge(rms_ready, ONE + n + 1)
                own.link(nc.vector.reciprocal(rstd[:, :], rstd[:, :]))

            def normalise(n, k):
                if not isinstance(n, int):
                    dve.wait_ge(xT_done, ONE + n * 2 - 1 + k)
                nc.vector.tensor_scalar(xn[:, k, :], res[:, bass.ts(n * 2 + k, 1), :].rearrange("p o d -> p (o d)"),
                                        rstd[:, k:k + 1], None, ALU.mult).then_inc(xn_ready, 1)

            def gain(n, k):
                dve.wait_ge(xT_done, ONE + n * 2 + k + 1)
                nc.vector.tensor_tensor(
                    hT[:, k, :, :], ps[:, 0:2, :].rearrange("p b (j t) -> p (b j) t", t=P),
                    g_mix[:, :].rearrange("p (j o) -> p j o", o=1).to_broadcast([P, KD, P]),
                    ALU.mult).then_inc(hT_ready, 1)

            row_norms(0)
            normalise(0, 0)
            normalise(0, 1)
            dve.wait_ge(mix_in, 32)
            gain(0, 0)
            gain(0, 1)
            dve.wait_ge(small_in, 16 * 5)
            own.link(nc.vector.tensor_copy(pos[:, :], pos_i[:, :]))
            own.link(nc.vector.tensor_tensor(
                ang[:, :, :], pos[:, :].rearrange("p (i o) -> p i o", o=1).to_broadcast([P, NT, NF]),
                freq[:, :].rearrange("p (o f) -> p o f", o=1).to_broadcast([P, NT, NF]), ALU.mult))
            for s, quarter in ((0, 0.25), (1, 0.0)):
                r = trig[:, s, :, :]
                own.link(nc.vector.tensor_scalar(turn[:, :, :], ang[:, :, :], 0.15915494309189535, quarter,
                                                 ALU.mult, ALU.add))
                own.link(nc.vector.tensor_scalar_add(turn[:, :, :], turn[:, :, :], ROUND))
                own.link(nc.vector.tensor_scalar_add(turn[:, :, :], turn[:, :, :], -ROUND))
                own.link(nc.vector.scalar_tensor_tensor(out=r, in0=turn[:, :, :], scalar=-TWO_PI_HI,
                                                        in1=ang[:, :, :], op0=ALU.mult, op1=ALU.add))
                own.link(nc.vector.scalar_tensor_tensor(out=r, in0=turn[:, :, :], scalar=-TWO_PI_LO,
                                                        in1=r, op0=ALU.mult, op1=ALU.add))
                own.link(nc.vector.tensor_scalar(r, r, 2 * 3.14159265358979 * quarter, 3.1415925,
                                                 ALU.add, ALU.min))
                own.link(nc.vector.tensor_scalar(r, r, -3.1415925, None, ALU.max))
            dve.sem_inc(ang_ready, 1)
            dve.wait_ge(trig_ready, 1)
            own.restart()

            def rotate(k, i, x1, x2, heads, step, o1=None, o2=None, copies=1):
                n = NF // step
                c, s = (trig[:, z, bass.ts(i, 1), :].rearrange("p o f -> p (o f)")[:, 0:NF:step]
                        .rearrange("p (o f) -> p o f", o=1).to_broadcast([P, heads, n]) for z in range(2))
                t = [rt[:, z, 0:heads, 0:n] for z in range(4)]
                own.mark(nc.vector.tensor_tensor(t[0], x1, c, ALU.mult))
                own.mark(nc.vector.tensor_tensor(t[1], x2, s, ALU.mult))
                own.mark(nc.vector.tensor_tensor(t[2], x2, c, ALU.mult))
                own.mark(nc.vector.tensor_tensor(t[3], x1, s, ALU.mult))
                own.sync()
                if copies > 1:
                    t = [u.to_broadcast([P, copies, n]) for u in t]
                own.mark(nc.vector.tensor_tensor(x1 if o1 is None else o1, t[0], t[1], ALU.subtract))
                own.mark(nc.vector.tensor_tensor(x2 if o2 is None else o2, t[2], t[3], ALU.add))
                own.sync()

            def mean_squares(n, k):
                dve.wait_ge(css_ready, ONE + n * 2 + k + 1)
                own.mark(nc.vector.tensor_scalar(ssc[:, k, 0:1], ssc[:, k, 0:1], 1.0 / QR, EPS, ALU.mult, ALU.add))
                own.mark(nc.vector.tensor_scalar(ssc[:, k, 1:2], ssc[:, k, 1:2], 1.0 / KR, EPS, ALU.mult, ALU.add))
                own.sync()
                dve.sem_inc(cms_ready, 1)

            def normalise_c(n, k):
                dve.wait_ge(crms_ready, ONE + n * 2 + k + 1)
                own.link(nc.vector.reciprocal(rstc[:, k, :], rstc[:, k, :]))
                own.mark(nc.vector.tensor_scalar(cn[:, k, 0:QR], st_a[:, k, C_AT:KV_AT], rstc[:, k, 0:1], None, ALU.mult))
                own.mark(nc.vector.tensor_scalar(cn[:, k, QR:], st_a[:, k, KV_AT:KR_AT], rstc[:, k, 1:2], None, ALU.mult))
                own.sync()
                dve.sem_inc(cn_ready, 1)

            def gain_c(n, k):
                dve.wait_ge(cnT_done, ONE + n * 2 + k + 1)
                nc.vector.tensor_tensor(
                    cT[:, k, :, :], ps[:, 6 + k, 0:3 * P].rearrange("p (j t) -> p j t", t=P),
                    g_c[:, :].rearrange("p (j o) -> p j o", o=1).to_broadcast([P, 3, P]),
                    ALU.mult).then_inc(cT_ready, 1)

            def rotate_a(n, k):
                qk = st_a[:, k, 0:2 * WA].rearrange("p (h e) -> p h e", e=EA)
                rotate(k, n * 2 + k, qk[:, :, 0:ROT_A // 2], qk[:, :, ROT_A // 2:ROT_A], 2 * HA, 2)
                dve.sem_inc(a_roped, 1)

            def rotate_m(n, k):
                dve.wait_ge(chunk_out, ONE + SLOTS + n * PER + 8 + k * 4 + 4)
                q = st_m[:, k, MQ:MK].rearrange("p (h e) -> p h e", h=HM)
                rotate(k, n * 2 + k, q[:, :, NOPE:NOPE + NF], q[:, :, NOPE + NF:], HM, 1)
                kk = st_m[:, k, MK:MV].rearrange("p (h e) -> p h e", h=HM)
                kr = st_a[:, k, KR_AT:IN_W].rearrange("p (o e) -> p o e", o=1)
                rotate(k, n * 2 + k, kr[:, :, 0:NF], kr[:, :, NF:], 1, 1,
                       kk[:, :, NOPE:NOPE + NF], kk[:, :, NOPE + NF:], HM)
                dve.sem_inc(m_roped, 1)

            def pair(n, ahead):
                mean_squares(n, 0)
                rotate_a(n, 0)
                normalise_c(n, 0)
                if ahead:
                    row_norms(n + 1)
                    normalise(n + 1, 0)
                    normalise(n + 1, 1)
                mean_squares(n, 1)
                gain_c(n, 0)
                normalise_c(n, 1)
                if ahead:
                    gain(n + 1, 0)
                gain_c(n, 1)
                rotate_a(n, 1)
                if ahead:
                    gain(n + 1, 1)
                rotate_m(n, 0)
                rotate_m(n, 1)
                own.restart()

            with dve.Fori(0, LAST) as it:
                pair(it, True)
            pair(LAST, False)

        @block.tensor
        def _(pe):
            def turn_x(n, k):
                pe.wait_ge(xn_ready, ONE + n * 2 + k + 1)
                pe.wait_ge(hT_ready, ONE + n * 2 + k)
                for j in range(KD):
                    last = nc.tensor.transpose(ps[:, j // 4, (j % 4) * P:(j % 4 + 1) * P],
                                               xn[:, k, j * P:(j + 1) * P], core.ident[:, :])
                last.then_inc(xT_done, 1)

            def project(n, k):
                pe.wait_ge(hT_ready, ONE + n * 2 + k + 1)
                for c in range(4):
                    pe.wait_ge(w_in_in[c], 16)
                    pe.wait_ge(chunk_out, ONE + n * PER + k * 4 + c + 1)
                    for j in range(KD):
                        last = nc.tensor.matmul(ps[:, 2 + c, 0:width(c)], hT[:, k, j, :],
                                                w_in[:, j, c * BANK:c * BANK + width(c)],
                                                start=j == 0, stop=j == KD - 1)
                    last.then_inc(chunk_done, 1)

            def turn_c(n, k):
                pe.wait_ge(cn_ready, ONE + n * 2 + k + 1)
                for j in range(3):
                    last = nc.tensor.transpose(ps[:, 6 + k, j * P:(j + 1) * P], cn[:, k, j * P:(j + 1) * P],
                                               core.ident[:, :])
                last.then_inc(cnT_done, 1)

            def expand(n, k):
                pe.wait_ge(cT_ready, ONE + n * 2 + k + 1)
                for c in range(4):
                    pe.wait_ge(chunk_out, ONE + n * PER + 8 + k * 4 + c + 1)
                    if c < 2:
                        w = min(BANK, UQ_W - c * BANK)
                        for j in range(2):
                            last = nc.tensor.matmul(ps[:, 2 + c, 0:w], cT[:, k, j, :],
                                                    w_uq[:, j, c * BANK:c * BANK + w], start=j == 0, stop=j == 1)
                    else:
                        last = nc.tensor.matmul(ps[:, 2 + c, :], cT[:, k, 2, :],
                                                w_ukv[:, (c - 2) * BANK:(c - 1) * BANK], start=True, stop=True)
                    last.then_inc(chunk_done, 1)

            def pair(n, ahead):
                project(n, 0)
                project(n, 1)
                turn_c(n, 0)
                if ahead:
                    turn_x(n + 1, 0)
                pe.wait_ge(wc_in, 32)
                expand(n, 0)
                turn_c(n, 1)
                if ahead:
                    turn_x(n + 1, 1)
                expand(n, 1)

            pe.wait_ge(mix_in, 32)
            turn_x(0, 0)
            turn_x(0, 1)
            with pe.Fori(0, LAST) as it:
                pair(it, True)
            pair(LAST, False)


def attend(core, mix, mask, group, heads, dim, scr, q_at, k_at, v_at, mix_at):
    nc, ps = core.nc, core.ps
    ev = EA
    N = NT * 2
    with ExitStack() as ctx:
        sb, sem = core.scope(ctx)
        g = lambda s: f"{s}_{group}"
        qn, kn = sb(g("qn"), [P, 2, NT, dim]), sb(g("kn"), [P, 2, NT, dim])
        vn = sb(g("vn"), [P, 2, NT, ev])
        qT, kT = sb(g("qT"), [dim, 2, SEQ]), sb(g("kT"), [dim, 2, SEQ])
        sm = sb(g("sm"), [P, 2, SEQ])
        pr = sb(g("pr"), [P, 2, SEQ])
        pT = sb(g("pT"), [P, 2, NT, P])
        least = sb(g("least"), [P, N])
        den = sb(g("den"), [P, N])
        rden = sb(g("rden"), [P, N])
        qkv_in = [sem(g(f"qkv_in{k}")) for k in range(2)]
        qkv_used = [sem(g(f"qkv_used{k}")) for k in range(2)]
        score_done, masked_ready, prob_ready = sem(g("score_done")), sem(g("masked_ready")), sem(g("prob_ready"))
        turned = sem(g("turned"))
        out_act, out_dve = sem(g("out_act")), sem(g("out_dve"))
        pv_done, o_out = sem(g("pv_done")), sem(g("o_out"))
        dve_held, pe_held = sem(g("dve_held")), sem(g("pe_held"))
        scale = float(dim) ** -0.5

        fills, of_unit = [], {}
        order = []
        def fill(what):
            fills.append(what)
            return len(fills) - 1
        head_fills = {}

        def head_turn(k):
            head_fills[k] = [fill(("qk", k, z, half)) for z in range(2) for half in range(2)]
            order.append(("head", k))

        def score(u):
            if u < N:
                if u % NT == 0:
                    head_turn(u // NT)
                order.append(("score", u))

        score(0)
        score(1)
        for u in range(N):
            i = u % NT
            of_unit[u] = [fill(("p", u, b0, min(4, i + 1 - b0))) for b0 in range(0, i + 1, 4)]
            order.append(("turn", u))
            if u:
                order.append(("pv", u - 1))
            score(u + 2)
        order.append(("pv", N - 1))
        NFILL = len(fills)
        assert NFILL % 2 == 0

        def outs_before(n):
            return (n + 1) // 2, n // 2

        open_counts(nc, (masked_ready, o_out, out_act, out_dve, prob_ready, pv_done, *qkv_in, *qkv_used, score_done,
                         turned))
        block = ctx.enter_context(nc.Block())

        @block.sync
        def _(sp):
            tiles = scr.rearrange("(i p) n -> p i n", p=P)
            with sp.Fori(0, heads // 2) as it:
                for k in range(2):
                    sp.wait_ge(qkv_used[k], ONE + it)
                    for dst, at, w in ((qn, q_at, dim), (kn, k_at, dim), (vn, v_at, ev)):
                        sp.dma_start(dst[:, k, :, :], tiles[:, :, bass.ds(it * (2 * w) + (at + k * w), w)]
                                     ).then_inc(qkv_in[k], 16)

        @block.tensor
        def _(pe):
            def wait_bank(it, n):
                a, d = outs_before(n)
                if n % 2 == 0:
                    pe.wait_ge(out_act, ONE + it * (NFILL // 2) + a)
                else:
                    pe.wait_ge(out_dve, ONE + it * (NFILL // 2) + d)

            def wait_copied(it, n):
                a, d = outs_before(n + 1)
                if n % 2 == 0:
                    pe.wait_ge(out_act, ONE + it * (NFILL // 2) + a)
                else:
                    pe.wait_ge(out_dve, ONE + it * (NFILL // 2) + d)

            with pe.Fori(0, heads // 2) as it:
                for kind, x in order:
                    if kind == "head":
                        pe.wait_ge(qkv_in[x], ONE + it * 48 + 48)
                        for n in head_fills[x]:
                            _, _, z, half = fills[n]
                            wait_bank(it, n)
                            pe.sem_inc(pe_held, 1)
                            src = (qn, kn)[z]
                            for j in range(4):
                                last = nc.tensor.transpose(ps[0:dim, 4 + n % 2, j * P:(j + 1) * P],
                                                           src[:, x, half * 4 + j, :], core.ident[:, :])
                            last.then_inc(turned, 1)
                        for n in head_fills[x][-2:]:
                            wait_copied(it, n)
                    elif kind == "score":
                        k, i, b = x // NT, x % NT, x % 2
                        nk = (i + 1) * P
                        pe.wait_ge(masked_ready, ONE + (it * N + x - 1 if x else it * N))
                        for c in range(0, nk, BANK):
                            w = min(BANK, nk - c)
                            last = nc.tensor.matmul(ps[:, 2 * b + c // BANK, 0:w], qT[:, k, i * P:(i + 1) * P],
                                                    kT[:, k, c:c + w], start=True, stop=True)
                        last.then_inc(score_done, 1)
                    elif kind == "turn":
                        k, b = x // NT, x % 2
                        pe.wait_ge(prob_ready, ONE + it * N + x + 1)
                        for n in of_unit[x]:
                            _, _, b0, nb = fills[n]
                            wait_bank(it, n)
                            for j in range(nb):
                                last = nc.tensor.transpose(ps[:, 4 + n % 2, j * P:(j + 1) * P],
                                                           pr[:, b, (b0 + j) * P:(b0 + j + 1) * P], core.ident[:, :])
                            last.then_inc(turned, 1)
                    else:
                        k, i, b = x // NT, x % NT, x % 2
                        for n in of_unit[x]:
                            wait_copied(it, n)
                        pe.wait_ge(o_out, ONE + (it * N + x - 1 if x else it * N))
                        for j in range(i + 1):
                            last = nc.tensor.matmul(ps[:, 6 + b, 0:ev], pT[:, b, j, :], vn[:, k, j, :],
                                                    start=j == 0, stop=j == i)
                        last.then_inc(pv_done, 1)
                        if i == NT - 1:
                            pe.wait_ge(pv_done, ONE + it * N + x + 1)
                            pe.sem_inc(qkv_used[k], 1)

        def copy_fill(eng, it, n):
            what, x, z, c = fills[n]
            eng.wait_ge(turned, ONE + it * NFILL + n + 1)
            done = (out_act, out_dve)[n % 2]
            if what == "qk":
                dst = (qT, kT)[z][:, x, c * BANK:(c + 1) * BANK]
                src = ps[0:dim, 4 + n % 2, :]
                s = -scale if z == 0 else 1.0
                if n % 2 == 0:
                    nc.scalar.activation(dst, src, ACT.Copy, scale=s).then_inc(done, 1)
                else:
                    nc.vector.tensor_scalar_mul(dst, src, s).then_inc(done, 1)
            else:
                eng.wait_ge(pv_done, ONE + (it * N + x - 1 if x else it * N))
                dst = pT[:, x % 2, z:z + c, :]
                src = ps[:, 4 + n % 2, 0:c * P].rearrange("p (j t) -> p j t", t=P)
                if n % 2 == 0:
                    nc.scalar.activation(dst, src, ACT.Copy).then_inc(done, 1)
                else:
                    nc.vector.tensor_copy(dst, src).then_inc(done, 1)

        @block.scalar
        def _(act):
            def exp(it, u):
                i, b = u % NT, u % 2
                nk = (i + 1) * P
                act.wait_ge(masked_ready, ONE + it * N + u + 1)
                if u >= 2:
                    act.wait_ge(turned, ONE + it * NFILL + of_unit[u - 2][-1] + 1)
                else:
                    act.wait_ge(turned, ONE + it * NFILL)
                nc.scalar.activation(pr[:, b, 0:nk], sm[:, b, 0:nk], ACT.Exp, scale=-1.0, bias=least[:, u:u + 1],
                                     accum_out=den[:, u:u + 1]).then_inc(prob_ready, 1)

            with act.Fori(0, heads // 2) as it:
                for kind, x in order:
                    if kind == "head":
                        for n in head_fills[x]:
                            if n % 2 == 0:
                                copy_fill(act, it, n)
                    elif kind == "turn":
                        if x == 0:
                            exp(it, 0)
                        for n in of_unit[x]:
                            if n % 2 == 0:
                                copy_fill(act, it, n)
                        if x + 1 < N:
                            exp(it, x + 1)

        @block.vector
        def _(dve):
            own = Own(dve, core.dve_own)
            with dve.Fori(0, heads // 2) as it:
                for kind, x in order:
                    if kind == "head":
                        for n in head_fills[x]:
                            if n % 2 == 1:
                                copy_fill(dve, it, n)
                    elif kind == "score":
                        i, b = x % NT, x % 2
                        nk = (i + 1) * P
                        dve.wait_ge(prob_ready, ONE + (it * N + x - 1 if x else it * N))
                        dve.wait_ge(score_done, ONE + it * N + x + 1)
                        dve.sem_inc(dve_held, 1)
                        nc.vector.tensor_tensor_reduce(
                            out=sm[:, b, 0:nk], in0=ps[:, 2 * b:2 * b + 2, :].rearrange("p b n -> p (b n)")[:, 0:nk],
                            in1=mask[:, (NT - 1 - i) * P:], scale=1.0, scalar=3.0e38, op0=ALU.add, op1=ALU.min,
                            accum_out=least[:, x:x + 1]).then_inc(masked_ready, 1)
                    elif kind == "turn":
                        for n in of_unit[x]:
                            if n % 2 == 1:
                                copy_fill(dve, it, n)
                    else:
                        k, i, b = x // NT, x % NT, x % 2
                        own.link(nc.vector.reciprocal(rden[:, x:x + 1], den[:, x:x + 1]))
                        dve.wait_ge(pv_done, ONE + it * N + x + 1)
                        nc.vector.tensor_scalar(mix[:, i, bass.ds(it * (2 * ev) + (mix_at + k * ev), ev)],
                                                ps[:, 6 + b, 0:ev], rden[:, x:x + 1], None, ALU.mult).then_inc(o_out, 1)
                own.restart()


def project_out(core, mix, w_out, w_out_in, hn_hi, hn_lo):
    nc, ps, res = core.nc, core.ps, core.res
    with ExitStack() as ctx:
        sb, sem = core.scope(ctx)
        st = sb("mix_st", [P, 2, D])
        mT = sb("mixT", [P, 2, KD, P])
        hn = sb("hn", [P, 2, D])
        full = sb("hnT", [P, 2, KD, P])
        junk = sb("junk_o", [P, D])
        ss = sb("ss_o", [P, 2])
        rstd = sb("rstd_o", [P, 2])
        staged, mT_done, mT_ready = sem("staged"), sem("mT_done"), sem("mT_ready")
        y_done, h_ready, hss_ready, hms_ready, hrms_ready = (sem(x) for x in (
            "y_done", "h_ready", "hss_ready", "hms_ready", "hrms_ready"))
        hn_ready, hnT_done, full_ready, hi_ready, lo_ready = (sem(x) for x in (
            "hn_ready", "hnT_done", "full_ready", "hi_ready", "lo_ready"))
        held = sem("act_held_o")
        open_counts(nc, (full_ready, h_ready, hi_ready, hms_ready, hnT_done, hn_ready, hrms_ready, hss_ready,
                         lo_ready, mT_done, mT_ready, staged, y_done))
        block = ctx.enter_context(nc.Block())

        def split_banks(k):
            return ps[:, 2 + 2 * k:4 + 2 * k, :]

        LAST = NT // 2 - 1

        def again(eng, sem_, n, k):
            if not (isinstance(n, int) and n == 0):
                eng.wait_ge(sem_, ONE + n * 2 - 1 + k)

        def row(t, n, k):
            return t[:, bass.ts(n * 2 + k, 1), :].rearrange("p o d -> p (o d)")

        def pairs(eng, pair):
            pair(0, True, False)
            with eng.Fori(0, LAST - 1) as it:
                pair(it + 1, False, False)
            pair(LAST, False, True)

        @block.tensor
        def _(pe):
            def turn_mix(n, k):
                pe.wait_ge(staged, ONE + n * 2 + k + 1)
                pe.wait_ge(mT_ready, ONE + n * 2 + k)
                for j in range(KD):
                    last = nc.tensor.transpose(ps[:, j // 4, (j % 4) * P:(j % 4 + 1) * P],
                                               st[:, k, j * P:(j + 1) * P], core.ident[:, :])
                last.then_inc(mT_done, 1)

            def multiply(n, k):
                pe.wait_ge(mT_ready, ONE + n * 2 + k + 1)
                again(pe, h_ready, n, k)
                for c in range(2):
                    for j in range(KD):
                        last = nc.tensor.matmul(split_banks(k)[:, c, :], mT[:, k, j, :],
                                                w_out[:, j, c * BANK:(c + 1) * BANK], start=j == 0, stop=j == KD - 1)
                last.then_inc(y_done, 1)

            def turn_hidden(n, k):
                pe.wait_ge(hn_ready, ONE + n * 2 + k + 1)
                pe.wait_ge(full_ready, ONE + n * 2 + k)
                for j in range(KD):
                    last = nc.tensor.transpose(ps[:, 6 + j // 4, (j % 4) * P:(j % 4 + 1) * P],
                                               hn[:, k, j * P:(j + 1) * P], core.ident[:, :])
                last.then_inc(hnT_done, 1)

            def pair(n, first, last):
                multiply(n, 0)
                if not first:
                    turn_hidden(n - 1, 1)
                if not last:
                    turn_mix(n + 1, 0)
                multiply(n, 1)
                turn_hidden(n, 0)
                if not last:
                    turn_mix(n + 1, 1)

            turn_mix(0, 0)
            turn_mix(0, 1)
            pe.wait_ge(w_out_in, 16)
            pairs(pe, pair)
            turn_hidden(LAST, 1)

        @block.scalar
        def _(act):
            own = Own(act, core.act_own)

            def stage(n, k):
                again(act, mT_done, n, k)
                nc.scalar.activation(st[:, k, :], row(mix, n, k), ACT.Copy).then_inc(staged, 1)

            def norms(n, k):
                act.wait_ge(h_ready, ONE + n * 2 + k + 1)
                own.sync()
                own.mark(nc.scalar.activation(junk[:, :], row(res, n, k), ACT.Square, accum_out=ss[:, k:k + 1]))
                own.sync()
                act.sem_inc(hss_ready, 1)
                act.wait_ge(hms_ready, ONE + n * 2 + k + 1)
                nc.scalar.activation(rstd[:, k:k + 1], ss[:, k:k + 1], ACT.Sqrt).then_inc(hrms_ready, 1)

            def copy_hi(n, k):
                act.wait_ge(full_ready, ONE + n * 2 + k + 1)
                act.sem_inc(held, 1)
                nc.scalar.activation(hn_hi[:, :, bass.ts(n * 2 + k, P)], full[:, k, :, :], ACT.Copy
                                     ).then_inc(hi_ready, 1)

            def pair(n, first, last):
                if not last:
                    stage(n + 1, 0)
                    stage(n + 1, 1)
                norms(n, 0)
                if not first:
                    copy_hi(n - 1, 1)
                norms(n, 1)
                copy_hi(n, 0)
                own.restart()

            stage(0, 0)
            stage(0, 1)
            pairs(act, pair)
            copy_hi(LAST, 1)

        @block.vector
        def _(dve):
            own = Own(dve, core.dve_own)

            def copy_mix(n, k):
                dve.wait_ge(mT_done, ONE + n * 2 + k + 1)
                again(dve, y_done, n, k)
                nc.vector.tensor_copy(mT[:, k, :, :], ps[:, 0:2, :].rearrange("p b (j t) -> p (b j) t", t=P)
                                      ).then_inc(mT_ready, 1)

            def add(n, k):
                dve.wait_ge(y_done, ONE + n * 2 + k + 1)
                h = row(res, n, k)
                nc.vector.tensor_tensor(h, split_banks(k).rearrange("p b n -> p (b n)"), h, ALU.add
                                        ).then_inc(h_ready, 1)

            def normalise(n, k):
                dve.wait_ge(hss_ready, ONE + n * 2 + k + 1)
                own.link(nc.vector.tensor_scalar(ss[:, k:k + 1], ss[:, k:k + 1], 1.0 / D, EPS, ALU.mult, ALU.add))
                dve.sem_inc(hms_ready, 1)
                dve.wait_ge(hrms_ready, ONE + n * 2 + k + 1)
                own.link(nc.vector.reciprocal(rstd[:, k:k + 1], rstd[:, k:k + 1]))
                again(dve, hnT_done, n, k)
                nc.vector.tensor_scalar(hn[:, k, :], row(res, n, k), rstd[:, k:k + 1], None, ALU.mult
                                        ).then_inc(hn_ready, 1)

            def gain(n, k):
                dve.wait_ge(hnT_done, ONE + n * 2 + k + 1)
                nc.vector.tensor_tensor(
                    full[:, k, :, :], ps[:, 6:8, :].rearrange("p b (j t) -> p (b j) t", t=P),
                    core.g_ffn[:, :].rearrange("p (j o) -> p j o", o=1).to_broadcast([P, KD, P]),
                    ALU.mult).then_inc(full_ready, 1)

            def low(n, k):
                dve.wait_ge(hi_ready, ONE + n * 2 + k + 1)
                at = bass.ts(n * 2 + k, P)
                nc.vector.tensor_tensor(hn_lo[:, :, at], full[:, k, :, :], hn_hi[:, :, at].bitcast(f32), ALU.subtract
                                        ).then_inc(lo_ready, 1)

            def pair(n, first, last):
                add(n, 0)
                if not first:
                    gain(n - 1, 1)
                normalise(n, 0)
                if not last:
                    copy_mix(n + 1, 0)
                if not first:
                    low(n - 1, 1)
                add(n, 1)
                gain(n, 0)
                normalise(n, 1)
                if not last:
                    copy_mix(n + 1, 1)
                low(n, 0)
                own.restart()

            copy_mix(0, 0)
            copy_mix(0, 1)
            pairs(dve, pair)
            gain(LAST, 1)
            low(LAST, 1)


def route(core, hn_hi, hn_lo, slotT):
    nc, ps = core.nc, core.ps
    NS = PH * TOPK
    QT = 2
    NQ = NT // QT
    with ExitStack() as ctx:
        sb, sem = core.scope(ctx)
        w_raw = sb("w_raw", [P, KD, PQ])
        w_hi = sb("w_hi", [P, KD, PQ], f32r)
        w_lo = sb("w_lo", [P, KD, PQ], f32r)
        keys = sb("keys", [P, 2, 2, HALFQ])
        keysT = sb("keysT", [P, 2, NKEY])
        qT = sb("peer_qT", [P, 2, SEQ])
        sc = sb("sc", [P, 2, NT, NKEY])
        rest = sb("rest", [P, NT, NKEY])
        top = sb("top", [P, 2, NT, TOPK])
        top_u = sb("top_u", [P, 2, NT, TOPK], u32)
        top_key = sb("top_key", [P, 2, NT, TOPK])
        pair = sb("pair", [P, NT, NC_])
        number = sb("number", [P, NT, NC_])
        best = sb("best", [P, NT, TOPK])
        at_u = sb("at_u", [P, NT, TOPK], u32)
        at = sb("at", [P, NT, TOPK], bf16)
        hit = sb("hit", [P, 2, QT, NC_, TOPK], bf16)
        found = sb("found", [P, 2, QT, NC_, TOPK])
        iota = sb("iota_p", [P, NC_, TOPK], bf16)
        iota_f = sb("iota_f", [P, NC_])
        expert = sb("expert", [P, NT, TOPK])
        expert_i = sb("expert_i", [P, NT, TOPK], i32)
        key_i = sb("key_i", [P, 2, NT, TOPK], i32)
        slot = sb("slot", [P, 3, NT, NS])
        u = slotT[:, 0, :, :].rearrange("p i t -> p (i t)")
        gelu = [slotT[:, 1 + k, :, :].rearrange("p i t -> p (i t)") for k in range(2)]
        uT_hi, uT_lo = sb("uT_hi_r", [P, KD, P], f32r), sb("uT_lo_r", [P, KD, P], f32r)
        minus = sb("minus_ident", [P, P], f32r)
        ex = sb("ex", [P, NT, TOPK])
        den = sb("den_p", [P, NT])
        iota_in, parked = sem("iota_in"), sem("parked")
        w_pq_in = sem("w_pq_in")
        u_in, uT_done, uT_hi_ready, uT_left, uT_lo_ready = (sem(x + "_r") for x in (
            "u_in", "uT_done", "uT_hi_ready", "uT_left", "uT_lo_ready"))
        act_done, gelu_ready, minus_ready = sem("act_done_r"), sem("gelu_ready_r"), sem("minus_ready")
        gelu_sent = [sem(f"gelu_sent{k}") for k in range(2)]
        keys_in = [sem(f"keys_in{b}") for b in range(2)]
        hi_made, lo_made, kT_done, kT_ready = sem("wpq_hi_made"), sem("wpq_lo_made"), sem("kT_done"), sem("kT_ready")
        q_done, q_out, sc_done, sc_out, ranked = (sem(x) for x in ("q_done", "q_out", "sc_done", "sc_out", "ranked"))
        keys_ranked, number_ready, hit_ready, found_ready, summed = (sem(x) for x in (
            "keys_ranked", "number_ready", "hit_ready", "found_ready", "summed"))
        centred, ex_ready, slot_ready, slotT_done, slotT_ready = (sem(x) for x in (
            "centred", "ex_ready", "slot_ready", "slotT_done", "slotT_ready"))
        held, own_p = sem("dve_held_r"), sem("pool_own_r")
        open_counts(nc, (w_pq_in, u_in, uT_done, uT_hi_ready, uT_left, uT_lo_ready, act_done, gelu_ready, *gelu_sent,
                         *keys_in, hi_made, lo_made, kT_done, kT_ready, q_done, q_out, sc_done, sc_out, ranked,
                         keys_ranked, number_ready, hit_ready, found_ready, summed, centred, ex_ready))
        block = ctx.enter_context(nc.Block())
        NH2 = PH // 2

        @block.sync
        def _(sp):
            w_v = core.i["w_pq"].rearrange("l (k p) n -> p (l k) n", p=P)
            k_v = core.i["sub_keys"].rearrange("l h z n c -> n (l h) z c")
            u_v = core.i["u_emb"].rearrange("l (i j) d -> j i (l d)", j=NKEY)
            sp.dma_start(iota_f[:, :], core.i["c_iota"][:, 0:NC_]).then_inc(iota_in, 16)
            with sp.Fori(0, NH2) as it:
                for b in range(2):
                    sp.wait_ge(lo_made, ONE + it * 2 + b)
                    sp.dma_start(w_raw[:, :, :], w_v[:, :, bass.ds(it * (2 * PQ) + b * PQ, PQ)]).then_inc(w_pq_in, 16)
                    sp.wait_ge(kT_done, ONE + (it * 2 + b - 1 if b else it * 2))
                    sp.dma_start(keys[:, b, :, :], k_v[:, bass.ts(it * 2 + b, 1), :, :].rearrange("n o z c -> n (o z) c")
                                 ).then_inc(keys_in[b], 16)
                    sp.wait_ge(uT_left, ONE + it * 4 + b * 2)
                    sp.dma_start(u, u_v[bass.ds(it * 2 + b, 1), :, :].rearrange("o p d -> p (o d)")).then_inc(u_in, 16)
            for n in range(PH, PRE):
                sp.wait_ge(uT_left, ONE + 2 * n)
                sp.dma_start(u, u_v[n]).then_inc(u_in, 16)
            sp.wait_ge(iota_in, 16)
            sp.wait_ge(parked, 32)

        @block.tensor
        def _(pe):
            def turn(n, part):
                if part == 0:
                    pe.wait_ge(u_in, ONE + n * 16 + 16)
                pe.wait_ge(uT_lo_ready, ONE + n * 2 + part)
                for j in range(4):
                    at = (part * 4 + j) * P
                    last = nc.tensor.matmul(ps[:, 3, j * P:(j + 1) * P], u[:, at:at + P], core.ident[:, :],
                                            start=True, stop=True)
                last.then_inc(uT_done, 1)

            def leave_low(n, part):
                pe.wait_ge(uT_hi_ready, ONE + n * 2 + part + 1)
                nc.tensor.matmul(ps[:, 3, :], minus[:, :], uT_hi[:, part * 4:part * 4 + 4, :].rearrange("p j e -> p (j e)"),
                                 start=True, stop=False)
                for j in range(4):
                    at = (part * 4 + j) * P
                    last = nc.tensor.matmul(ps[:, 3, j * P:(j + 1) * P], u[:, at:at + P], core.ident[:, :],
                                            start=False, stop=j == 3)
                last.then_inc(uT_left, 1)

            def activations(n):
                pe.wait_ge(uT_lo_ready, ONE + n * 2 + 2)
                pe.wait_ge(gelu_ready, ONE + n * 2)
                for half in range(2):
                    ts = slice(half * BANK, (half + 1) * BANK)
                    terms = [(x, y, j) for j in range(KD) for x, y in ((uT_hi, hn_hi), (uT_hi, hn_lo), (uT_lo, hn_hi))]
                    for m, (x, y, j) in enumerate(terms):
                        last = nc.tensor.matmul(ps[:, 6 + half, :], x[:, j, :], y[:, j, ts],
                                                start=m == 0, stop=m == len(terms) - 1)
                    last.then_inc(act_done, 1)

            pe.wait_ge(minus_ready, 1)
            with pe.Fori(0, NH2) as it:
                for b in range(2):
                    pe.wait_ge(keys_in[b], ONE + it * 16 + 16)
                    pe.wait_ge(kT_ready, ONE + it * 2 + b)
                    for z in range(2):
                        last = nc.tensor.transpose(ps[:, 2, z * NKEY:(z + 1) * NKEY], keys[:, b, z, :], core.ident[:, :])
                    last.then_inc(kT_done, 1)
                    pe.wait_ge(hi_made, ONE + it * 2 + b + 1)
                    pe.wait_ge(lo_made, ONE + it * 2 + b + 1)
                    for z in range(2):
                        cs = slice(z * HALFQ, (z + 1) * HALFQ)
                        for half in range(2):
                            pe.wait_ge(q_out, ONE + (it * 8 + b * 4 + z * 2 + half - 1 if b or z or half else it * 8))
                            ts = slice(half * BANK, (half + 1) * BANK)
                            terms = [(w, x, j) for w, x in ((w_hi, hn_hi), (w_hi, hn_lo), (w_lo, hn_hi)) for j in range(KD)]
                            for n, (w, x, j) in enumerate(terms):
                                last = nc.tensor.matmul(ps[:, half, :], w[:, j, cs], x[:, j, ts],
                                                        start=n == 0, stop=n == len(terms) - 1)
                            last.then_inc(q_done, 1)
                            if half == 0:
                                turn(it * 2 + b, z)
                            else:
                                leave_low(it * 2 + b, z)
                    pe.wait_ge(kT_ready, ONE + it * 2 + b + 1)
                    for z in range(2):
                        pe.wait_ge(q_out, ONE + it * 8 + b * 4 + z * 2 + 2)
                        pe.wait_ge(sc_out, ONE + it * 4 + b * 2 + z)
                        for i in range(NT):
                            last = nc.tensor.matmul(ps[:, 4 + i // 4, (i % 4) * P:(i % 4 + 1) * P],
                                                    qT[:, z, i * P:(i + 1) * P], keysT[:, z, :], start=True, stop=True)
                        last.then_inc(sc_done, 1)
                    activations(it * 2 + b)
            for n in range(PH, PRE):
                for part in range(2):
                    turn(n, part)
                    leave_low(n, part)
                activations(n)
            pe.wait_ge(slot_ready, 1)
            for i in range(NT):
                if i >= 2:
                    pe.wait_ge(slotT_ready, i - 1)
                for z in range(3):
                    last = nc.tensor.transpose(ps[:, i % 2, z * P:(z + 1) * P], slot[:, z, i, :], core.ident[:, :])
                last.then_inc(slotT_done, 1)

        @block.scalar
        def _(act):
            def copy_hi(n, part):
                act.wait_ge(uT_done, ONE + n * 2 + part + 1)
                act.wait_ge(act_done, ONE + n * 2)
                nc.scalar.activation(uT_hi[:, part * 4:part * 4 + 4, :], ps[:, 3, :].rearrange("p (j e) -> p j e", e=P),
                                     ACT.Copy).then_inc(uT_hi_ready, 1)

            def copy_lo(n, part):
                act.wait_ge(uT_left, ONE + n * 2 + part + 1)
                nc.scalar.activation(uT_lo[:, part * 4:part * 4 + 4, :], ps[:, 3, :].rearrange("p (j e) -> p j e", e=P),
                                     ACT.Copy).then_inc(uT_lo_ready, 1)

            def gelus(n, k):
                if not isinstance(n, int) or n >= 2:
                    act.wait_ge(gelu_sent[k], ONE + (n - k) * 8)
                for half in range(2):
                    act.wait_ge(act_done, ONE + n * 2 + half + 1)
                    nc.scalar.activation(gelu[k][:, half * BANK:(half + 1) * BANK], ps[:, 6 + half, :],
                                         ACT.Gelu).then_inc(gelu_ready, 1)
                act.wait_ge(gelu_ready, ONE + n * 2 + 2)
                dst = core.scr_w[n] if isinstance(n, int) else core.scr_w[bass.ds(n, 1), :, :].rearrange("o p t -> p (o t)")
                act.dma_start(dst, gelu[k]).then_inc(gelu_sent[k], 16)

            def head(h, b, first=False, split_next=True):
                act.wait_ge(kT_done, ONE + h + 1)
                act.wait_ge(sc_done, ONE + h * 2)
                nc.scalar.activation(keysT[:, :, :], ps[:, 2, 0:2 * NKEY].rearrange("p (z n) -> p z n", z=2),
                                     ACT.Copy).then_inc(kT_ready, 1)
                for z in range(2):
                    for half in range(2):
                        act.wait_ge(q_done, ONE + h * 4 + z * 2 + half + 1)
                        nc.scalar.activation(qT[:, z, half * BANK:(half + 1) * BANK], ps[:, half, :],
                                             ACT.Copy).then_inc(q_out, 1)
                        (copy_hi, copy_lo)[half](h, z)
                if split_next:
                    act.wait_ge(w_pq_in, ONE + h * 16 + 32)
                    nc.scalar.activation(w_hi[:, :, :], w_raw[:, :, :], ACT.Copy).then_inc(hi_made, 1)
                for z in range(2):
                    act.wait_ge(sc_done, ONE + h * 2 + z + 1)
                    if not first:
                        act.wait_ge(ranked, ONE + h * 2 + z - 1)
                    nc.scalar.activation(sc[:, z, :, :], ps[:, 4:6, :].rearrange(
                        "p b (i n) -> p (b i) n", n=NKEY), ACT.Copy).then_inc(sc_out, 1)
                if not first:
                    exponentials(h)
                gelus(h, b)

            def exponentials(heads):
                act.wait_ge(centred, ONE + heads)
                nc.scalar.activation(ex[:, :, :], ex[:, :, :], ACT.Exp).then_inc(ex_ready, 1)

            nc.scalar.activation(minus[:, :], core.ident[:, :], ACT.Copy, scale=-1.0).then_inc(minus_ready, 1)
            act.wait_ge(w_pq_in, ONE + 16)
            nc.scalar.activation(w_hi[:, :, :], w_raw[:, :, :], ACT.Copy).then_inc(hi_made, 1)
            act.dma_start(core.scr_hi, hn_hi[:, :, :].bitcast(f32)).then_inc(parked, 16)
            act.dma_start(core.scr_lo, hn_lo[:, :, :].bitcast(f32)).then_inc(parked, 16)
            head(0, 0, first=True)
            with act.Fori(0, NH2 - 1) as it:
                head(it * 2 + 1, 1)
                head(it * 2 + 2, 0)
            head(PH - 1, 1, split_next=False)
            for n in range(PH, PRE):
                for part in range(2):
                    copy_hi(n, part)
                    copy_lo(n, part)
                gelus(n, n % 2)
            exponentials(PH)
            for k in range(2):
                act.wait_ge(gelu_sent[k], ONE + 16 * PRE // 2)
            for i in range(NT):
                act.wait_ge(slotT_done, i + 1)
                nc.scalar.activation(slotT[:, :, i, :], ps[:, i % 2, 0:3 * P].rearrange("p (z t) -> p z t", z=3),
                                     ACT.Copy).then_inc(slotT_ready, 1)

        def pair_sums(eng, own, dst, src):
            for a in range(8):
                own.mark(eng.tensor_tensor(dst[:, :, RUN_AT[a]:RUN_AT[a] + RUN[a]],
                                           src[:, 0, :, a:a + 1].to_broadcast([P, NT, RUN[a]]),
                                           src[:, 1, :, 0:RUN[a]], ALU.add))
            own.mark(eng.tensor_tensor(dst[:, :, RUN_AT[8]:], src[:, 0, :, 8:16],
                                       src[:, 1, :, 0:1].to_broadcast([P, NT, 8]), ALU.add))
            own.sync()

        @block.gpsimd
        def _(pool):
            own = Own(pool, own_p)
            with pool.Fori(0, NH2) as it:
                for b in range(2):
                    pool.wait_ge(keys_ranked, ONE + it * 2 + b + 1)
                    pool.wait_ge(found_ready, ONE + (it * 2 + b) * NQ)
                    pair_sums(nc.gpsimd, own, number, top_key)
                    pool.sem_inc(number_ready, 1)
                    for q in range(NQ):
                        n = (it * 2 + b) * NQ + q
                        pool.wait_ge(hit_ready, ONE + n + 1)
                        pool.wait_ge(summed, ONE + (n - 1 if q else n))
                        nc.gpsimd.tensor_tensor(
                            found[:, q % 2, :, :, :], hit[:, q % 2, :, :, :],
                            number[:, q * QT:(q + 1) * QT, :].rearrange("p i (c o) -> p i c o", o=1)
                            .to_broadcast([P, QT, NC_, TOPK]), ALU.mult).then_inc(found_ready, 1)
                own.restart()

        @block.vector
        def _(dve):
            own = Own(dve, core.dve_own)

            def best16(values, indices, src, rest):
                for i in range(NT):
                    own.mark(nc.vector.max(values[:, i, 0:8], src[:, i, :]))
                own.sync()
                for i in range(NT):
                    own.mark(nc.vector.match_replace(rest[:, i, :], values[:, i, 0:8], src[:, i, :], LOWEST))
                for i in range(NT):
                    own.mark(nc.vector.max_index(indices[:, i, 0:8], values[:, i, 0:8], src[:, i, :]))
                for i in range(NT):
                    if i == 0:
                        own.sync()
                    own.mark(nc.vector.max(values[:, i, 8:16], rest[:, i, :]))
                own.sync()
                for i in range(NT):
                    own.mark(nc.vector.max_index(indices[:, i, 8:16], values[:, i, 8:16], rest[:, i, :]))
                own.sync()

            dve.wait_ge(iota_in, 16)
            own.link(nc.vector.tensor_copy(iota[:, :, :], iota_f[:, :].rearrange("p (c o) -> p c o", o=1)
                                           .to_broadcast([P, NC_, TOPK])))
            own.restart()
            dve.wait_ge(hi_made, ONE + 1)
            nc.vector.tensor_tensor(w_lo[:, :, :], w_raw[:, :, :], w_hi[:, :, :].bitcast(f32), ALU.subtract
                                    ).then_inc(lo_made, 1)

            def look(h, q):
                if not isinstance(h, int) or h * NQ + q >= 2:
                    dve.wait_ge(found_ready, ONE + h * NQ + q - 1)
                nc.vector.tensor_tensor(
                    hit[:, q % 2, :, :, :],
                    at[:, q * QT:(q + 1) * QT, :].rearrange("p i (o k) -> p i o k", o=1)
                    .to_broadcast([P, QT, NC_, TOPK]),
                    iota[:, :, :].rearrange("p (o c) k -> p o c k", o=1).to_broadcast([P, QT, NC_, TOPK]),
                    ALU.is_equal).then_inc(hit_ready, 1)

            def total(h, q):
                dve.wait_ge(found_ready, ONE + h * NQ + q + 1)
                nc.vector.tensor_reduce(expert[:, q * QT:(q + 1) * QT, :],
                                        found[:, q % 2, :, :, :].rearrange("p i c k -> p i k c"), AX, ALU.add
                                        ).then_inc(summed, 1)

            def finish_gates(h):
                dve.wait_ge(ex_ready, ONE + h + 1)
                own.link(nc.vector.tensor_reduce(den[:, :], ex[:, :, :], AX, ALU.add))
                own.link(nc.vector.reciprocal(den[:, :], den[:, :]))
                own.mark(nc.vector.tensor_tensor(
                    slot[:, 2, :, bass.ds(h * TOPK, TOPK)], ex[:, :, :],
                    den[:, :].rearrange("p (i o) -> p i o", o=1).to_broadcast([P, NT, TOPK]), ALU.mult))
                total(h, 0)
                look(h, 2)
                total(h, 1)
                look(h, 3)

            def finish_keys(h):
                total(h, 2)
                total(h, 3)
                dve.wait_ge(summed, ONE + (h + 1) * NQ)
                own.link(nc.vector.tensor_copy(expert_i[:, :, :], expert[:, :, :]))
                own.mark(nc.vector.tensor_single_scalar(key_i[:, 0, :, :], expert_i[:, :, :], 7, ALU.logical_shift_right))
                own.mark(nc.vector.tensor_single_scalar(key_i[:, 1, :, :], expert_i[:, :, :], NKEY - 1, ALU.bitwise_and))
                own.sync()
                for z in range(2):
                    own.mark(nc.vector.tensor_copy(slot[:, z, :, bass.ds(h * TOPK, TOPK)], key_i[:, z, :, :]))

            def head(h, b, first=False, split_next=True):
                for z in range(2):
                    dve.wait_ge(sc_out, ONE + h * 2 + z + 1)
                    dve.sem_inc(held, 1)
                    best16(top[:, z, :, :], top_u[:, z, :, :], sc[:, z, :, :], rest)
                    dve.sem_inc(ranked, 1)
                    if z == 0 and split_next:
                        dve.wait_ge(hi_made, ONE + h + 2)
                        nc.vector.tensor_tensor(w_lo[:, :, :], w_raw[:, :, :], w_hi[:, :, :].bitcast(f32),
                                                ALU.subtract).then_inc(lo_made, 1)
                    if not first:
                        (finish_gates, finish_keys)[z](h - 1)
                if not first:
                    dve.wait_ge(number_ready, ONE + h)
                own.mark(nc.vector.tensor_scalar(top_key[:, 0, :, :], top_u[:, 0, :, :], float(NKEY), None, ALU.mult))
                own.mark(nc.vector.tensor_copy(top_key[:, 1, :, :], top_u[:, 1, :, :]))
                own.sync()
                dve.sem_inc(keys_ranked, 1)
                pair_sums(nc.vector, own, pair, top)
                best16(best, at_u, pair, rest[:, :, 0:NC_])
                own.mark(nc.vector.tensor_copy(at[:, :, :], at_u[:, :, :]))
                own.mark(nc.vector.tensor_tensor(ex[:, :, :], best[:, :, :],
                                                 best[:, :, 0:1].to_broadcast([P, NT, TOPK]), ALU.subtract))
                own.sync()
                dve.sem_inc(centred, 1)
                look(h, 0)
                look(h, 1)
                own.restart()

            head(0, 0, first=True)
            with dve.Fori(0, NH2 - 1) as it:
                head(it * 2 + 1, 1)
                head(it * 2 + 2, 0)
            head(PH - 1, 1, split_next=False)
            finish_gates(PH - 1)
            finish_keys(PH - 1)
            own.restart()
            dve.sem_inc(slot_ready, 1)


def spread_gates(core, slotT, first_sent, gates_sent):
    nc, ps = core.nc, core.ps
    OCT = 8
    TU = BANK // NKEY
    NB = OCT // TU
    BODY = 2
    PER_TILE = P // OCT
    NOCT = SEQ // OCT
    ON_ACT = 6
    ON_POOL = 6
    with ExitStack() as ctx:
        sb, sem = core.scope(ctx)
        gates = [sb(f"gates{k}", [P, NKEY, P]) for k in (1, 0)][::-1]
        one1 = sb("one1", [P, BODY, NKEY, OCT], bf16)
        one2 = sb("one2", [P, BODY, NKEY, OCT], bf16)
        first = sb("first", [P, BODY, OCT, NKEY])
        second = sb("second", [P, BODY, OCT, NKEY])
        iota_f = sb("iota_g", [P, NKEY])
        iota = sb("iota_gb", [P, NKEY, OCT], bf16)
        keysT = sb("slot_keys", [P, 2, SEQ], bf16)
        iota_in = sem("iota_in_g")
        ones_ready, by_dve, first_pool, second_ready = (sem(x) for x in (
            "ones_ready", "by_dve", "first_pool", "second_ready"))
        spread_done, gates_out = sem("spread_done"), sem("gates_out")
        open_counts(nc, (ones_ready, by_dve, first_pool, first_pool, second_ready, second_ready, spread_done, gates_out,
                         *first_sent, *gates_sent))
        block = ctx.enter_context(nc.Block())
        flat = slotT[:, :, :, :].rearrange("p z i t -> p z (i t)")

        @block.sync
        def _(sp):
            sp.dma_start(iota_f[:, :], core.i["c_iota"]).then_inc(iota_in, 16)
            dst = core.scr_g.rearrange("j i t -> i j t")

            def send(pair, k, parts):
                sp.wait_ge(gates_out, ONE + BODY * NB + pair * (2 * PER_TILE * NB) + (k + 1) * PER_TILE * NB)
                for js, sent in parts:
                    sp.dma_start(dst[:, js, bass.ts(pair * 2 + k, P)], gates[k][:, js, :]).then_inc(sent[k], 16)

            parts = ((slice(0, FIRST), first_sent), (slice(FIRST, NKEY), gates_sent))
            with sp.Fori(0, NT // 2 - 1) as it:
                for k in range(2):
                    send(it, k, parts)
            send(NT // 2 - 1, 0, parts)
            send(NT // 2 - 1, 1, parts[:1])
            sp.wait_ge(iota_in, 16)

        def weigh(eng, n, b, lo, hi):
            gate = flat[:, 2, bass.ds(n * OCT + lo, hi - lo)]
            return eng.tensor_tensor(
                first[:, b, lo:hi, :].rearrange("p t i -> p i t"), one1[:, b, :, lo:hi],
                gate.rearrange("p (o t) -> p o t", o=1).to_broadcast([P, NKEY, hi - lo]), ALU.mult)

        @block.vector
        def _(dve):
            own = Own(dve, core.dve_own)
            dve.wait_ge(iota_in, 16)
            own.mark(nc.vector.tensor_copy(iota[:, :, :], iota_f[:, :].rearrange("p (i o) -> p i o", o=1)
                                           .to_broadcast([P, NKEY, OCT])))
            own.mark(nc.vector.tensor_copy(keysT[:, :, :], flat[:, 0:2, :]))
            own.restart()
            dve.sem_inc(spread_done, BODY * NB)
            dve.sem_inc(gates_out, BODY * NB)
            with dve.Fori(0, NOCT // BODY) as it:
                for b in range(BODY):
                    n = it * BODY + b
                    dve.wait_ge(first_pool, ONE + n)
                    dve.wait_ge(second_ready, ONE + n)
                    for z, dst in ((0, one1), (1, one2)):
                        nc.vector.tensor_tensor(
                            dst[:, b, :, :], iota[:, :, :],
                            keysT[:, z, bass.ds(n * OCT, OCT)].rearrange("p (o t) -> p o t", o=1)
                            .to_broadcast([P, NKEY, OCT]), ALU.is_equal).then_inc(ones_ready, 1)
                    dve.wait_ge(ones_ready, ONE + n * 2 + 1)
                    dve.wait_ge(spread_done, ONE + n * NB + NB)
                    weigh(nc.vector, n, b, ON_POOL, OCT).then_inc(by_dve, 1)
                    dve.wait_ge(ones_ready, ONE + n * 2 + 2)
                    nc.vector.tensor_copy(second[:, b, ON_ACT:, :], one2[:, b, :, ON_ACT:].rearrange("p i t -> p t i")
                                          ).then_inc(by_dve, 1)

        @block.gpsimd
        def _(pool):
            with pool.Fori(0, NOCT // BODY) as it:
                for b in range(BODY):
                    n = it * BODY + b
                    pool.wait_ge(ones_ready, ONE + n * 2 + 1)
                    pool.wait_ge(spread_done, ONE + n * NB + NB)
                    weigh(nc.gpsimd, n, b, 0, ON_POOL).then_inc(first_pool, 1)

        @block.tensor
        def _(pe):
            with pe.Fori(0, NOCT // BODY) as it:
                for b in range(BODY):
                    n = it * BODY + b
                    pe.wait_ge(by_dve, ONE + n * 2 + 2)
                    pe.wait_ge(first_pool, ONE + n + 2)
                    pe.wait_ge(second_ready, ONE + n + 2)
                    for u in range(NB):
                        bank = b * NB + u
                        pe.wait_ge(gates_out, ONE + n * NB + u + 1)
                        for s in range(TU):
                            last = nc.tensor.matmul(ps[:, bank, s * NKEY:(s + 1) * NKEY], first[:, b, u * TU + s, :],
                                                    second[:, b, u * TU + s, :], start=True, stop=True)
                        last.then_inc(spread_done, 1)

        @block.scalar
        def _(act):
            def widen(n, b):
                act.wait_ge(ones_ready, ONE + n * 2 + 2)
                act.wait_ge(spread_done, ONE + n * NB + NB)
                nc.scalar.activation(second[:, b, 0:ON_ACT, :], one2[:, b, :, 0:ON_ACT].rearrange("p i t -> p t i"),
                                     ACT.Copy).then_inc(second_ready, 1)

            def copy_out(n, q, k, b):
                for u in range(NB):
                    act.wait_ge(spread_done, ONE + BODY * NB + n * NB + u + 1)
                    nc.scalar.activation(
                        gates[k][:, :, bass.ds(q * (BODY * OCT) + (b * OCT + u * TU), TU)].rearrange("p i t -> p t i"),
                        ps[:, b * NB + u, :].rearrange("p (t i) -> p t i", t=TU), ACT.Copy).then_inc(gates_out, 1)

            def octs(tile, q, k, last=False):
                n = tile * PER_TILE + q * BODY
                widen(n + 1, 1)
                copy_out(n, q, k, 0)
                if not last:
                    widen(n + 2, 0)
                copy_out(n + 1, q, k, 1)

            def tile_pair(it, last):
                for k in range(2):
                    act.wait_ge(first_sent[k], ONE + it * 16)
                    act.wait_ge(gates_sent[k], ONE + it * 16)
                    peel = last and k == 1
                    with act.Fori(0, PER_TILE // BODY - peel) as q:
                        octs(it * 2 + k, q, k)
                    if peel:
                        octs(it * 2 + k, PER_TILE // BODY - 1, k, True)

            widen(0, 0)
            with act.Fori(0, NT // 2 - 1) as it:
                tile_pair(it, False)
            tile_pair(NT // 2 - 1, True)

        return core.scr_g.rearrange("j i t -> i j t")[:, FIRST:, (NT - 1) * P:], gates[1][:, FIRST:, :]


def run_experts(core, first_sent, gates_sent, last_gates):
    nc, ps, res = core.nc, core.ps, core.res
    CH = 2
    NG = NKEY // CH
    PG = PRE // CH
    assert FIRST >= 3 * CH
    assert PG % 2 == 1 and NG % 2 == 0 and PG >= 4
    HN_LOADS = 2
    HN_W = KD // HN_LOADS
    FILLS = NT * 2
    with ExitStack() as ctx:
        sb, sem = core.scope(ctx)
        hn_hi, hn_lo = sb("hn_hi_e", [P, KD, SEQ], f32r), sb("hn_lo_e", [P, KD, SEQ], f32r)
        hn_in = sem("hn_in")
        w_in = [sem(f"made_in{c}") for c in range(CH)]
        u = sb("u", [P, CH, D])
        v = sb("v", [P, CH, D])
        gate = sb("gate", [P, CH, SEQ])
        uT_hi, uT_lo = sb("uT_hi", [P, CH, KD, P], f32r), sb("uT_lo", [P, CH, KD, P], f32r)
        v_hi, v_lo = sb("v_hi", [P, CH, D], f32r), sb("v_lo", [P, CH, D], f32r)
        w = sb("w", [P, CH, SEQ])
        w_hi, w_lo = sb("w_hi2", [P, 2, CH, SEQ], f32r), sb("w_lo2", [P, 2, CH, SEQ], f32r)
        u_in = [sem(f"u_in{c}") for c in range(CH)]
        gate_in = [sem(f"gate_in{c}") for c in range(CH)]
        v_in = sem("v_in")
        uT_done, uT_hi_ready, uT_lo_ready = sem("uT_done"), sem("uT_hi_ready"), sem("uT_lo_ready")
        act_done, gelu_ready, w_ready, w_hi_ready, w_lo_ready = (sem(x) for x in (
            "act_done", "gelu_ready", "w_ready", "w_hi_ready", "w_lo_ready"))
        v_hi_ready, v_lo_ready, out_done, added = (sem(x) for x in ("v_hi_ready", "v_lo_ready", "out_done", "added"))
        open_counts(nc, (hn_in, *w_in, act_done, added, *gate_in, gelu_ready, out_done, uT_done, uT_hi_ready,
                         uT_lo_ready, *u_in,
                         v_hi_ready, v_in, v_lo_ready, w_hi_ready, w_lo_ready, w_ready))
        block = ctx.enter_context(nc.Block())

        u_v = core.i["u_emb"].rearrange("l (i j) d -> j i (l d)", j=NKEY)
        v_v = core.i["v_emb"].rearrange("l (i j) d -> j i (l d)", j=NKEY)

        def need(eng, sem_, value):
            if not isinstance(value, int) or value > 0:
                eng.wait_ge(sem_, ONE + value)

        def at(ap, n):
            return ap[n] if isinstance(n, int) else ap[bass.ds(n, 1), :, :].rearrange("o p d -> p (o d)")

        def schedule(made=lambda g, b: None, group=lambda g, b, last: None, out=lambda g, b, next_made: None,
                     values=lambda g: None, start=lambda: None, eng=None, made_too=True):
            if made_too:
                made(0, 0)
                values(0)
                with eng.Fori(0, PG // 2) as it:
                    made(it * 2 + 1, 1)
                    out(it * 2, 0, True)
                    values(it * 2 + 1)
                    made(it * 2 + 2, 0)
                    out(it * 2 + 1, 1, True)
                    values(it * 2 + 2)
            start()
            group(PG, 1, False)
            out(PG - 1, 0, False)
            values(PG)
            with eng.Fori(0, (NG - PG) // 2 - 1) as it:
                group(it * 2 + PG + 1, 0, False)
                out(it * 2 + PG, 1, False)
                values(it * 2 + PG + 1)
                group(it * 2 + PG + 2, 1, False)
                out(it * 2 + PG + 1, 0, False)
                values(it * 2 + PG + 2)
            for g in (NG - 2, NG - 1):
                group(g, g % 2, g == NG - 1)
                out(g - 1, (g - 1) % 2, False)
                values(g)
            out(NG - 1, (NG - 1) % 2, False)

        def own_count(g, c):
            return g * CH + c - PRE

        @block.sync
        def _(sp):
            def load_rest(g):
                for c in range(CH):
                    need(sp, w_ready, g * CH + c - 1)
                    sp.dma_start(gate[:, c, :], at(core.scr_g, g * CH + c)).then_inc(gate_in[c], 16)
                need(sp, v_hi_ready, g)
                need(sp, v_lo_ready, g)
                for c in range(CH):
                    sp.dma_start(v[:, c, :], at(v_v, g * CH + c)).then_inc(v_in, 16)

            def load_made(g, b):
                for c in range(CH):
                    need(sp, w_lo_ready, g * CH + c - 1)
                    sp.dma_start(w[:, c, :], at(core.scr_w, g * CH + c)).then_inc(w_in[c], 16)
                load_rest(g)

            def load_hidden(part):
                for k in range(2):
                    sp.wait_ge(gates_sent[k], ONE + 16 * NT // 2)
                js = slice(part * HN_W, (part + 1) * HN_W)
                sp.dma_start(hn_hi[:, js, :].bitcast(f32), core.scr_hi[:, js, :]).then_inc(hn_in, 16)
                sp.dma_start(hn_lo[:, js, :].bitcast(f32), core.scr_lo[:, js, :]).then_inc(hn_in, 16)

            def load(g, b, last):
                for c in range(CH):
                    need(sp, uT_done, own_count(g, c) - 1)
                    sp.dma_start(u[:, c, :], at(u_v, g * CH + c)).then_inc(u_in[c], 16)
                load_rest(g)

            for k in range(2):
                sp.wait_ge(first_sent[k], ONE + 16 * NT // 2)
            sp.wait_ge(gates_sent[0], ONE + 16 * NT // 2)
            for g in range(PG):
                load_made(g, g % 2)
                if g == 1:
                    sp.dma_start(*last_gates).then_inc(gates_sent[1], 16)
                if g >= 2 and g - 2 < HN_LOADS:
                    load_hidden(g - 2)
            schedule(group=load, eng=sp, made_too=False)

        @block.tensor
        def _(pe):
            def turn(g, c):
                n = own_count(g, c)
                pe.wait_ge(u_in[c], ONE + (g - PG) * 16 + 16)
                need(pe, uT_hi_ready, n)
                need(pe, uT_lo_ready, n)
                for j in range(KD):
                    last = nc.tensor.transpose(ps[:, 4 + j // 4, (j % 4) * P:(j % 4 + 1) * P],
                                               u[:, c, j * P:(j + 1) * P], core.ident[:, :])
                last.then_inc(uT_done, 1)

            def activations(g, b, last_group):
                if isinstance(g, int) and g == PG:
                    pe.wait_ge(hn_in, ONE + 16 * 2 * HN_LOADS)
                for c in range(CH):
                    n = own_count(g, c)
                    if not (last_group and c == CH - 1):
                        turn(g + (c + 1) // CH, (c + 1) % CH)
                    pe.wait_ge(uT_hi_ready, ONE + n + 1)
                    pe.wait_ge(uT_lo_ready, ONE + n + 1)
                    need(pe, gelu_ready, n - 1)
                    for half in range(2):
                        ts = slice(half * BANK, (half + 1) * BANK)
                        terms = [(x, y, j) for j in range(KD) for x, y in ((uT_hi, hn_hi), (uT_hi, hn_lo), (uT_lo, hn_hi))]
                        for m, (x, y, j) in enumerate(terms):
                            last = nc.tensor.matmul(ps[:, 2 * c + half, :], x[:, c, j, :], y[:, j, ts],
                                                    start=m == 0, stop=m == len(terms) - 1)
                    last.then_inc(act_done, 1)

            def out(g, b, _):
                pe.wait_ge(w_hi_ready, ONE + g * CH + CH)
                pe.wait_ge(w_lo_ready, ONE + g * CH + CH)
                pe.wait_ge(v_hi_ready, ONE + g + 1)
                pe.wait_ge(v_lo_ready, ONE + g + 1)
                for i in range(NT):
                    for half in range(2):
                        f = i * 2 + half
                        need(pe, added, g * FILLS + (f - 1 if f else 0))
                        terms = [(x, y, c) for c in range(CH) for x, y in ((w_hi, v_hi), (w_hi, v_lo), (w_lo, v_hi))]
                        for m, (x, y, c) in enumerate(terms):
                            last = nc.tensor.matmul(ps[:, 6 + half, :], x[:, b, c, i * P:(i + 1) * P],
                                                    y[:, c, half * BANK:(half + 1) * BANK],
                                                    start=m == 0, stop=m == len(terms) - 1)
                        last.then_inc(out_done, 1)

            schedule(group=activations, out=out, start=lambda: turn(PG, 0), eng=pe)

        @block.scalar
        def _(act):
            def copy_uT(g, c):
                n = own_count(g, c)
                act.wait_ge(uT_done, ONE + n + 1)
                need(act, act_done, n - 1)
                nc.scalar.activation(uT_hi[:, c, :, :], ps[:, 4:6, :].rearrange("p b (j e) -> p (b j) e", e=P),
                                     ACT.Copy).then_inc(uT_hi_ready, 1)

            def group(g, b, last_group):
                for c in range(CH):
                    if not (last_group and c == CH - 1):
                        copy_uT(g + (c + 1) // CH, (c + 1) % CH)
                    act.wait_ge(act_done, ONE + own_count(g, c) + 1)
                    need(act, w_lo_ready, g * CH + c - 1)
                    nc.scalar.activation(w[:, c, :], ps[:, 2 * c:2 * c + 2, :].rearrange("p b t -> p (b t)"),
                                         ACT.Gelu).then_inc(gelu_ready, 1)
                    copy_w(g, b, c)

            def copy_w(g, b, c):
                act.wait_ge(w_ready, ONE + g * CH + c + 1)
                need(act, out_done, (g - 1) * FILLS)
                nc.scalar.activation(w_hi[:, b, c, :], w[:, c, :], ACT.Copy).then_inc(w_hi_ready, 1)

            def made(g, b):
                for c in range(CH):
                    copy_w(g, b, c)

            def values(g):
                act.wait_ge(v_in, ONE + g * (16 * CH) + 16 * CH)
                need(act, out_done, g * FILLS)
                nc.scalar.activation(v_hi[:, :, :], v[:, :, :], ACT.Copy).then_inc(v_hi_ready, 1)

            schedule(made, group, values=values, start=lambda: copy_uT(PG, 0), eng=act)

        @block.vector
        def _(dve):
            def split_uT(g, c):
                n = own_count(g, c)
                dve.wait_ge(uT_hi_ready, ONE + n + 1)
                need(dve, act_done, n - 1)
                nc.vector.tensor_tensor(uT_lo[:, c, :, :], ps[:, 4:6, :].rearrange("p b (j e) -> p (b j) e", e=P),
                                        uT_hi[:, c, :, :].bitcast(f32), ALU.subtract).then_inc(uT_lo_ready, 1)

            def gated(g, c, made=False):
                dve.wait_ge(gate_in[c], ONE + g * 16 + 16)
                if made:
                    dve.wait_ge(w_in[c], ONE + g * 16 + 16)
                else:
                    dve.wait_ge(gelu_ready, ONE + own_count(g, c) + 1)
                nc.vector.tensor_tensor(w[:, c, :], w[:, c, :], gate[:, c, :], ALU.mult).then_inc(w_ready, 1)

            def low(g, b, c):
                dve.wait_ge(w_hi_ready, ONE + g * CH + c + 1)
                need(dve, out_done, (g - 1) * FILLS)
                nc.vector.tensor_tensor(w_lo[:, b, c, :], w[:, c, :], w_hi[:, b, c, :].bitcast(f32), ALU.subtract
                                        ).then_inc(w_lo_ready, 1)

            def group(g, b, last_group):
                split_uT(g, 1)
                gated(g, 0)
                low(g, b, 0)
                if not last_group:
                    split_uT(g + 1, 0)

            def made(g, b):
                gated(g, 0, True)
                low(g, b, 0)
                if isinstance(g, int) and g == 0:
                    gated(g, 1, True)
                    low(g, b, 1)

            def out(g, b, next_made):
                for f in range(FILLS):
                    i, half = f // 2, f % 2
                    dve.wait_ge(out_done, ONE + g * FILLS + (f + 1))
                    r = res[:, i, half * BANK:(half + 1) * BANK]
                    nc.vector.tensor_tensor(r, ps[:, 6 + half, :], r, ALU.add).then_inc(added, 1)
                    if not (isinstance(g, int) and g == NG - 1):
                        if f == 1:
                            gated(g + 1, 1, next_made)
                        if f == 4:
                            low(g + 1, 1 - b, 1)

            def values(g):
                dve.wait_ge(v_hi_ready, ONE + g + 1)
                nc.vector.tensor_tensor(v_lo[:, :, :], v[:, :, :], v_hi[:, :, :].bitcast(f32), ALU.subtract
                                        ).then_inc(v_lo_ready, 1)

            schedule(made, group, out, values, start=lambda: split_uT(PG, 0), eng=dve)
            dve.wait_ge(added, ONE + NG * FILLS)


def finish(core):
    nc, res = core.nc, core.res
    with ExitStack() as ctx:
        sb, sem = core.scope(ctx)
        g = sb("g_final", [P, D])
        junk = sb("junk_f", [P, D])
        ss, rstd = sb("ss_f", [P, NT]), sb("rstd_f", [P, NT])
        g_in, ss_ready, ms_ready, rms_ready, y_ready, sent = (sem(x) for x in (
            "g_in", "ss_ready_f", "ms_ready_f", "rms_ready_f", "y_ready_f", "sent_f"))
        block = ctx.enter_context(nc.Block())

        @block.sync
        def _(sp):
            sp.dma_start(g[:, :], core.i["g_final"].rearrange("(o d) -> o d", o=1).to_broadcast([P, D])).then_inc(g_in, 16)
            o = core.out.rearrange("b (i p) d -> p (b i) d", p=P)
            for i in range(NT):
                sp.wait_ge(y_ready, i + 1)
                sp.dma_start(o[:, i, :], res[:, i, :]).then_inc(sent, 16)
            sp.wait_ge(sent, 16 * NT)

        @block.scalar
        def _(act):
            own = Own(act, core.act_own)
            for i in range(NT):
                if i:
                    own.sync()
                own.mark(nc.scalar.activation(junk[:, :], res[:, i, :], ACT.Square, accum_out=ss[:, i:i + 1]))
            own.sync()
            act.sem_inc(ss_ready, 1)
            act.wait_ge(ms_ready, 1)
            nc.scalar.activation(rstd[:, :], ss[:, :], ACT.Sqrt).then_inc(rms_ready, 1)

        @block.vector
        def _(dve):
            own = Own(dve, core.dve_own)
            dve.wait_ge(ss_ready, 1)
            own.link(nc.vector.tensor_scalar(ss[:, :], ss[:, :], 1.0 / D, EPS, ALU.mult, ALU.add))
            dve.sem_inc(ms_ready, 1)
            dve.wait_ge(rms_ready, 1)
            own.link(nc.vector.reciprocal(rstd[:, :], rstd[:, :]))
            dve.wait_ge(g_in, 16)
            for i in range(NT):
                nc.vector.scalar_tensor_tensor(out=res[:, i, :], in0=res[:, i, :], scalar=rstd[:, i:i + 1],
                                               in1=g[:, :], op0=ALU.mult, op1=ALU.mult).then_inc(y_ready, 1)


def layer(nc, ins, out):
    with ExitStack() as ctx, ExitStack() as outer:
        core = Core(nc, ctx, ins, out)
        project_in(core)
        with ExitStack() as mid:
            sb, sem = core.scope(mid)
            mix = sb("mix", [P, NT, D])
            w_out = sb("w_out", [P, KD, D])
            w_out_in = sem("w_out_in")
            with ExitStack() as att:
                mask = att.enter_context(nc.sbuf_tensor("mask", [P, 2, SEQ], f32))
                with nc.semaphore("mask_in") as mask_in, nc.Block() as block:
                    @block.sync
                    def _(sp):
                        sp.dma_start(mask[:, :, :], core.i["c_mask"]).then_inc(mask_in, 16)
                        sp.dma_start(w_out[:, :, :], core.i["w_out"].rearrange("l (k p) n -> p (l k) n", p=P)
                                     ).then_inc(w_out_in, 16)
                        sp.wait_ge(mask_in, 16)
                attend(core, mix, mask[:, 0, :], "a", HA, EA, core.scr_a, 0, WA, 2 * WA, 0)
                attend(core, mix, mask[:, 1, :], "m", HM, EM, core.scr_m, MQ, MK, MV, WA)
            hidden = outer.enter_context(ExitStack())
            hn_hi, hn_lo = (hidden.enter_context(nc.sbuf_tensor(n, [P, KD, SEQ], f32r, side="right"))
                            for n in ("hn_hi", "hn_lo"))
            project_out(core, mix, w_out, w_out_in, hn_hi, hn_lo)
        with ExitStack() as peer:
            slotT = peer.enter_context(nc.sbuf_tensor("slotT", [P, 3, NT, P], f32))
            first_sent, gates_sent = ([peer.enter_context(nc.semaphore(f"{n}{k}")) for k in range(2)]
                                      for n in ("first_sent", "gates_sent"))
            route(core, hn_hi, hn_lo, slotT)
            hidden.close()
            last_gates = spread_gates(core, slotT, first_sent, gates_sent)
            run_experts(core, first_sent, gates_sent, last_gates)
        finish(core)


NAMES = ["x", "positions", "g_mix", "w_in", "g_cq", "w_uq", "g_ckv", "w_ukv", "w_out", "g_ffn",
         "w_pq", "sub_keys", "u_emb", "v_emb", "g_final"]


def constants(np):
    half = NF
    freq = np.float32(500000.0) ** (-np.arange(half, dtype=np.float32) / np.float32(half))
    dist = (SEQ - P) + np.arange(P)[:, None] - np.arange(SEQ)[None, :]
    count = ((dist >= 0) & (dist <= 128)).astype(np.int64)
    count += (dist >= 0) & (dist <= 512) & (dist % 4 == 0)
    count += (dist >= 0) & (dist <= 2048) & (dist % 16 == 0)
    mask = np.full((P, 2, SEQ), BIG, np.float32)
    mask[:, 0] = np.where(count > 0, -np.log(np.maximum(count, 1)), BIG)
    mask[:, 1] = np.where(dist >= 0, 0.0, BIG)
    return {
        "c_freq": np.broadcast_to(freq, (P, half)).copy(),
        "c_ident": np.eye(P, dtype=np.float32),
        "c_mask": mask,
        "c_iota": np.broadcast_to(np.arange(P, dtype=np.float32), (P, P)).copy(),
    }


def kernel(**inputs):
    import numpy as np
    import concourse.bacc as bacc
    from concourse.bass_utils import run_bass_kernel_spmd

    nc = bacc.Bacc("TRN2", target_bir_lowering=False, num_devices=1)
    arrays = {"in_" + n: np.ascontiguousarray(inputs[n]) for n in NAMES}
    arrays.update(constants(np))
    ins = {n.removeprefix("in_"): nc.dram_tensor(n, a.shape, mybir.dt.from_np(a.dtype), kind="ExternalInput").ap()
           for n, a in arrays.items()}
    out = nc.dram_tensor("out", (1, SEQ, D), f32, kind="ExternalOutput").ap()
    layer(nc, ins, out)
    r = run_bass_kernel_spmd(nc, [arrays], core_ids=[0])
    return r.results[0]["out"]
```
